# Optimizing a Trainium2 kernel written in Bass

```python
import math
import jax, jax.numpy as jnp
from jax import lax
import numpy as np

D_MODEL = 2048
BATCH = 1
SEQ = 256
DEPTH = 1

HEAD_DIM = 128
DIL_GROUPS = ((128, 1), (512, 4), (2048, 16))
HEADS_PER_DIL_GROUP = 4
N_HEADS_A = HEADS_PER_DIL_GROUP * len(DIL_GROUPS)
N_HEADS_B = 4
WIDTH_A = N_HEADS_A * HEAD_DIM
WIDTH_B = N_HEADS_B * HEAD_DIM
A_OUT = HEADS_PER_DIL_GROUP * HEAD_DIM
D_IN = 3 * WIDTH_A + 3 * WIDTH_B + 2 * D_MODEL
D_FF = 5632
CONV_WIDTH = 3
PLE_DIM = 256
BLOCK = 128
RMS_EPS = 1e-6
ALIBI_MAX = 8.0


def rmsnorm(x, g):
    xf = x.astype(jnp.float32)
    y = xf * lax.rsqrt(jnp.mean(xf * xf, axis=-1, keepdims=True) + RMS_EPS)
    return (y * g.astype(jnp.float32)).astype(x.dtype)

def alibi_slopes(n):
    return jnp.exp2(-ALIBI_MAX * jnp.arange(1, n + 1, dtype=jnp.float32) / n)

def dilated_window_group(q, k, v, window, dilation, slopes):
    b, s, hg, dh = q.shape
    n_back = window // dilation
    span = dilation * BLOCK
    s_pad = -(-s // span) * span
    L = s_pad // dilation
    nb = L // BLOCK

    def to_blocks(t):
        t = jnp.pad(t, ((0, 0), (0, s_pad - s), (0, 0), (0, 0)))
        t = t.reshape(b, L, dilation, hg, dh).transpose(0, 2, 3, 1, 4)
        return t.reshape(b, dilation, hg, nb, BLOCK, dh)

    def with_prev(t):
        prev = jnp.pad(t, ((0, 0), (0, 0), (0, 0), (1, 0), (0, 0), (0, 0)))[:, :, :, :-1]
        return jnp.concatenate([prev, t], axis=4)

    qb = to_blocks(q)
    kk = with_prev(to_blocks(k))
    vv = with_prev(to_blocks(v))
    scores = jnp.einsum('brhnqe,brhnke->brhnqk', qb, kk).astype(jnp.float32) * (1.0 / math.sqrt(dh))
    qi = jnp.arange(BLOCK)[:, None]
    ki = jnp.arange(2 * BLOCK)[None, :]
    steps = BLOCK + qi - ki
    valid = (steps >= 0) & (steps <= n_back)
    first = (jnp.arange(nb) == 0)[:, None, None]
    valid = valid[None] & ~(first & (ki < BLOCK)[None])
    bias = -slopes[:, None, None] * (steps * dilation).astype(jnp.float32)[None]
    scores = scores + bias[None, None, :, None]
    scores = jnp.where(valid[None, None, None], scores, -jnp.inf)
    lse = jax.nn.logsumexp(scores, axis=-1)
    probs = jnp.exp(scores - lse[..., None])
    out = jnp.einsum('brhnqk,brhnke->brhnqe', probs.astype(v.dtype), vv)

    def from_blocks(t):
        t = t.reshape(b, dilation, hg, L, *t.shape[5:])
        t = jnp.moveaxis(t, 3, 1)
        return t.reshape(b, s_pad, hg, *t.shape[4:])[:, :s]

    return from_blocks(out), from_blocks(lse)

def dilated_mixture_attention(q, k, v):
    b, s = q.shape[:2]
    slopes = alibi_slopes(N_HEADS_A)
    outs, lses = [], []
    for g, (window, dilation) in enumerate(DIL_GROUPS):
        sl = slice(g * HEADS_PER_DIL_GROUP, (g + 1) * HEADS_PER_DIL_GROUP)
        o, l = dilated_window_group(q[:, :, sl], k[:, :, sl], v[:, :, sl], window, dilation, slopes[sl])
        outs.append(o)
        lses.append(l)
    alpha = jax.nn.softmax(jnp.stack(lses), axis=0)
    y = jnp.sum(alpha[..., None] * jnp.stack(outs).astype(jnp.float32), axis=0)
    return y.reshape(b, s, A_OUT).astype(q.dtype)

def stick_breaking_attention(q, k, v):
    b, s, h, dh = q.shape
    nb = s // BLOCK
    qt = q.transpose(0, 2, 1, 3)
    kt = k.transpose(0, 2, 1, 3)
    vt = v.transpose(0, 2, 1, 3)
    scale = 1.0 / math.sqrt(dh)
    idx = jnp.arange(BLOCK)
    tri_within = (idx[:, None] > idx[None, :]).astype(jnp.float32)
    diag_before = idx[None, :] < idx[:, None]
    outs = []
    for n in range(nb):
        c = n + 1
        kl = c * BLOCK
        qblk = qt[:, :, n * BLOCK:(n + 1) * BLOCK]
        z = jnp.einsum('bhqe,bhke->bhqk', qblk, kt[:, :, :kl]).astype(jnp.float32) * scale
        before = jnp.concatenate([jnp.ones((BLOCK, n * BLOCK), dtype=bool), diag_before], axis=1)
        ln = jnp.where(before, jax.nn.log_sigmoid(-z), 0.0)
        lnc = ln.reshape(b, h, BLOCK, c, BLOCK)
        within = jnp.einsum('bhqcj,ji->bhqci', lnc, tri_within)
        tot = jnp.sum(lnc, axis=-1)
        cidx = jnp.arange(c)
        after = jnp.einsum('bhqc,cd->bhqd', tot, (cidx[:, None] > cidx[None, :]).astype(jnp.float32))
        logw = z.reshape(b, h, BLOCK, c, BLOCK) + lnc + within + after[..., None]
        w = jnp.where(before, jnp.exp(logw.reshape(b, h, BLOCK, kl)), 0.0)
        outs.append(jnp.einsum('bhqk,bhke->bhqe', w.astype(v.dtype), vt[:, :, :kl]))
    out = jnp.concatenate(outs, axis=2)
    return out.transpose(0, 2, 1, 3).reshape(b, s, h * dh)

def causal_depthwise_conv(x, w, bias):
    s = x.shape[1]
    xp = jnp.pad(x, ((0, 0), (CONV_WIDTH - 1, 0), (0, 0)))
    y = bias + w[0] * xp[:, 0:s]
    for j in range(1, CONV_WIDTH):
        y = y + w[j] * xp[:, j:j + s]
    return y

def first_inputs(seed: int = 0) -> dict:
    key = jax.random.key(seed)
    ks = jax.random.split(key, 20)
    f32 = jnp.float32

    def nrm(k, shape, scale):
        return jax.random.normal(k, shape, f32) * scale

    def gain(k):
        return 1.0 + 0.05 * jax.random.normal(k, (DEPTH, D_MODEL), f32)

    return {
        'x': nrm(ks[0], (BATCH, SEQ, D_MODEL), 1.0),
        'p': nrm(ks[1], (DEPTH, BATCH, SEQ, PLE_DIM), 1.0),
        'g_mix_pre': gain(ks[2]),
        'w_in': nrm(ks[3], (DEPTH, D_MODEL, D_IN), D_MODEL ** -0.5),
        'w_branch_a': nrm(ks[4], (DEPTH, A_OUT, D_MODEL), A_OUT ** -0.5),
        'w_branch_b': nrm(ks[5], (DEPTH, WIDTH_B, D_MODEL), WIDTH_B ** -0.5),
        'w_out': nrm(ks[6], (DEPTH, D_MODEL, D_MODEL), D_MODEL ** -0.5),
        'g_mix_post': gain(ks[7]),
        'g_ffn_pre': gain(ks[8]),
        'w_up': nrm(ks[9], (DEPTH, D_MODEL, 2 * D_FF), D_MODEL ** -0.5),
        'conv_w': nrm(ks[10], (DEPTH, CONV_WIDTH, 2 * D_FF), CONV_WIDTH ** -0.5),
        'conv_b': nrm(ks[11], (DEPTH, 2 * D_FF), 0.01),
        'w_down': nrm(ks[12], (DEPTH, D_FF, D_MODEL), D_FF ** -0.5),
        'g_ffn_post': gain(ks[13]),
        'w_ple_in': nrm(ks[14], (DEPTH, PLE_DIM, D_MODEL), PLE_DIM ** -0.5),
        'w_ple_gate': nrm(ks[15], (DEPTH, D_MODEL, D_MODEL), D_MODEL ** -0.5),
    }

def first_block(x, p, g_mix_pre, w_in, w_branch_a, w_branch_b, w_out, g_mix_post, g_ffn_pre, w_up, conv_w, conv_b, w_down, g_ffn_post, w_ple_in, w_ple_gate):
    b, s, _ = x.shape
    splits = [WIDTH_A, 2 * WIDTH_A, 3 * WIDTH_A,
              3 * WIDTH_A + WIDTH_B, 3 * WIDTH_A + 2 * WIDTH_B, 3 * WIDTH_A + 3 * WIDTH_B,
              3 * WIDTH_A + 3 * WIDTH_B + D_MODEL]
    h = x
    for i in range(DEPTH):
        u = rmsnorm(h, g_mix_pre[i])
        proj = u @ w_in[i]
        qa, ka, va, qb, kb, vb, gla, glb = jnp.split(proj, splits, axis=-1)
        heads_a = lambda t: t.reshape(b, s, N_HEADS_A, HEAD_DIM)
        heads_b = lambda t: t.reshape(b, s, N_HEADS_B, HEAD_DIM)
        ya = dilated_mixture_attention(heads_a(qa), heads_a(ka), heads_a(va)) @ w_branch_a[i]
        yb = stick_breaking_attention(heads_b(qb), heads_b(kb), heads_b(vb)) @ w_branch_b[i]
        gate_a = jax.nn.sigmoid(gla.astype(jnp.float32)).astype(h.dtype)
        gate_b = jax.nn.sigmoid(glb.astype(jnp.float32)).astype(h.dtype)
        mix = (gate_a * ya + gate_b * yb) @ w_out[i]
        h = h + rmsnorm(mix, g_mix_post[i])
        u = rmsnorm(h, g_ffn_pre[i])
        up = causal_depthwise_conv(u @ w_up[i], conv_w[i], conv_b[i])
        gate_ff, value = jnp.split(up, [D_FF], axis=-1)
        f = (jax.nn.gelu(gate_ff, approximate=True) * value) @ w_down[i]
        h = h + rmsnorm(f, g_ffn_post[i])
        e = p[i] @ w_ple_in[i]
        h = h + jax.nn.sigmoid((h @ w_ple_gate[i]).astype(jnp.float32)).astype(h.dtype) * e
    return h


N_Q_HEADS = 16
N_KV_HEADS = 2
HEAD_DIM_2 = 64
Q_PER_KV = N_Q_HEADS // N_KV_HEADS
WINDOW = 128
ATTN_WIDTH = N_Q_HEADS * HEAD_DIM_2
KV_WIDTH = N_KV_HEADS * HEAD_DIM_2
SSM_GROUP = 16
SSM_GROUPS = 32
SSM_WIDTH = SSM_GROUP * SSM_GROUPS
SSM_STATE = 64
DT_MIN = 0.001
DT_MAX = 0.1
IN_COLS = ATTN_WIDTH + 2 * KV_WIDTH + SSM_WIDTH + 2 * D_MODEL
SPLIT_POINTS = (ATTN_WIDTH, ATTN_WIDTH + KV_WIDTH, ATTN_WIDTH + 2 * KV_WIDTH,
                ATTN_WIDTH + 2 * KV_WIDTH + SSM_WIDTH,
                ATTN_WIDTH + 2 * KV_WIDTH + SSM_WIDTH + D_MODEL)
NEG_BIG = -1e30


def rms_norm(x, g):
    xf = x.astype(jnp.float32)
    y = xf * lax.rsqrt(jnp.mean(xf * xf, axis=-1, keepdims=True) + RMS_EPS)
    return (y * g.astype(jnp.float32)).astype(x.dtype)

def sliding_window_attention(q, k, v, sinks):
    b, l = q.shape[0], q.shape[1]
    nb = l // BLOCK
    qb = q.reshape(b, nb, BLOCK, N_KV_HEADS, Q_PER_KV, HEAD_DIM_2)
    kb = k.reshape(b, nb, BLOCK, N_KV_HEADS, HEAD_DIM_2)
    vb = v.reshape(b, nb, BLOCK, N_KV_HEADS, HEAD_DIM_2)

    def with_prev(t):
        prev = jnp.pad(t, ((0, 0), (1, 0), (0, 0), (0, 0), (0, 0)))[:, :-1]
        return jnp.concatenate([prev, t], axis=2)

    kx = with_prev(kb)
    vx = with_prev(vb)
    scores = jnp.einsum('bnqgrd,bnsgd->bngrqs', qb, kx).astype(jnp.float32) * (HEAD_DIM_2 ** -0.5)
    q_idx = jnp.arange(BLOCK)[:, None]
    s_idx = jnp.arange(2 * BLOCK)[None, :]
    dist = q_idx + BLOCK - s_idx
    band = (dist >= 0) & (dist < WINDOW)
    valid = band[None] & ((jnp.arange(nb)[:, None, None] > 0) | (s_idx[None] >= BLOCK))
    slopes = 2.0 ** (-8.0 * jnp.arange(1, N_Q_HEADS + 1, dtype=jnp.float32) / N_Q_HEADS)
    slopes = slopes.reshape(N_KV_HEADS, Q_PER_KV)
    alibi = -slopes[:, :, None, None] * dist.astype(jnp.float32)[None, None]
    scores = scores + alibi[None, None]
    scores = jnp.where(valid[None, :, None, None], scores, NEG_BIG)
    sink = sinks.astype(jnp.float32).reshape(N_KV_HEADS, Q_PER_KV)[None, None, :, :, None, None]
    m = jnp.maximum(jnp.max(scores, axis=-1, keepdims=True), sink)
    p = jnp.exp(scores - m)
    p = p / (jnp.sum(p, axis=-1, keepdims=True) + jnp.exp(sink - m))
    out = jnp.einsum('bngrqs,bnsgd->bnqgrd', p.astype(v.dtype), vx)
    return out.reshape(b, l, ATTN_WIDTH)

def s5_ssm(u, a_re, a_im, log_dt, b_re, b_im, c_re, c_im, d_skip):
    bsz, l = u.shape[0], u.shape[1]
    ug = u.reshape(bsz, l, SSM_GROUPS, SSM_GROUP)
    dt = jnp.exp(log_dt)[:, None]
    mag = jnp.exp(a_re * dt)
    ab_re = mag * jnp.cos(a_im * dt)
    ab_im = mag * jnp.sin(a_im * dt)
    nr = ab_re - 1.0
    ni = ab_im
    den = a_re * a_re + a_im * a_im
    z_re = (nr * a_re + ni * a_im) / den
    z_im = (ni * a_re - nr * a_im) / den
    bb_re = z_re[..., None] * b_re - z_im[..., None] * b_im
    bb_im = z_re[..., None] * b_im + z_im[..., None] * b_re
    bu_re = jnp.einsum('gph,blgh->blgp', bb_re, ug)
    bu_im = jnp.einsum('gph,blgh->blgp', bb_im, ug)
    a_re_t = jnp.broadcast_to(ab_re, bu_re.shape)
    a_im_t = jnp.broadcast_to(ab_im, bu_im.shape)

    def combine(left, right):
        a1r, a1i, b1r, b1i = left
        a2r, a2i, b2r, b2i = right
        return (a1r * a2r - a1i * a2i,
                a1r * a2i + a1i * a2r,
                a2r * b1r - a2i * b1i + b2r,
                a2r * b1i + a2i * b1r + b2i)

    _, _, xs_re, xs_im = lax.associative_scan(combine, (a_re_t, a_im_t, bu_re, bu_im), axis=1)
    y = (jnp.einsum('ghp,blgp->blgh', c_re, xs_re)
         - jnp.einsum('ghp,blgp->blgh', c_im, xs_im)
         + d_skip.reshape(SSM_GROUPS, SSM_GROUP) * ug)
    return y.reshape(bsz, l, SSM_WIDTH)

def causal_depthwise_conv_2(x, w, b):
    l = x.shape[1]
    xp = jnp.pad(x, ((0, 0), (CONV_WIDTH - 1, 0), (0, 0)))
    y = b
    for k in range(CONV_WIDTH):
        y = y + w[k] * xp[:, k:k + l]
    return y

def second_inputs(seed: int = 0) -> dict:
    key = jax.random.key(seed)
    ks = jax.random.split(key, 24)
    f32 = jnp.float32
    nrm = lambda k, shape, s: jax.random.normal(k, shape, f32) * s
    x = jax.random.normal(ks[0], (BATCH, SEQ, D_MODEL), f32)
    attn_norm_g = 1.0 + nrm(ks[1], (DEPTH, D_MODEL), 0.02)
    w_in = nrm(ks[2], (DEPTH, D_MODEL, IN_COLS), D_MODEL ** -0.5)
    b_in = nrm(ks[3], (DEPTH, IN_COLS), 0.02)
    attn_sinks = nrm(ks[4], (DEPTH, N_Q_HEADS), 0.5)
    ssm_a_re = -0.5 + nrm(ks[5], (DEPTH, SSM_GROUPS, SSM_STATE), 0.01)
    ssm_a_im = (jnp.pi * jnp.arange(SSM_STATE, dtype=f32))[None, None, :] + nrm(ks[6], (DEPTH, SSM_GROUPS, SSM_STATE), 0.01)
    ssm_log_dt = jax.random.uniform(ks[7], (DEPTH, SSM_GROUPS), f32, minval=math.log(DT_MIN), maxval=math.log(DT_MAX))
    ssm_b_re = nrm(ks[8], (DEPTH, SSM_GROUPS, SSM_STATE, SSM_GROUP), (2 * SSM_GROUP) ** -0.5)
    ssm_b_im = nrm(ks[9], (DEPTH, SSM_GROUPS, SSM_STATE, SSM_GROUP), (2 * SSM_GROUP) ** -0.5)
    ssm_c_re = nrm(ks[10], (DEPTH, SSM_GROUPS, SSM_GROUP, SSM_STATE), (2 * SSM_STATE) ** -0.5)
    ssm_c_im = nrm(ks[11], (DEPTH, SSM_GROUPS, SSM_GROUP, SSM_STATE), (2 * SSM_STATE) ** -0.5)
    ssm_d = nrm(ks[12], (DEPTH, SSM_WIDTH), 1.0)
    w_glu = nrm(ks[13], (DEPTH, SSM_WIDTH, 2 * SSM_WIDTH), SSM_WIDTH ** -0.5)
    b_glu = nrm(ks[14], (DEPTH, 2 * SSM_WIDTH), 0.02)
    w_branch_attn = nrm(ks[15], (DEPTH, ATTN_WIDTH, D_MODEL), ATTN_WIDTH ** -0.5)
    w_branch_ssm = nrm(ks[16], (DEPTH, SSM_WIDTH, D_MODEL), SSM_WIDTH ** -0.5)
    w_out = nrm(ks[17], (DEPTH, D_MODEL, D_MODEL), D_MODEL ** -0.5)
    ffn_norm_g = 1.0 + nrm(ks[18], (DEPTH, D_MODEL), 0.02)
    w_up = nrm(ks[19], (DEPTH, D_MODEL, 2 * D_FF), D_MODEL ** -0.5)
    conv_w = nrm(ks[20], (DEPTH, CONV_WIDTH, D_FF), CONV_WIDTH ** -0.5)
    conv_b = nrm(ks[21], (DEPTH, D_FF), 0.02)
    w_down = nrm(ks[22], (DEPTH, D_FF, D_MODEL), D_FF ** -0.5)
    final_norm_g = 1.0 + nrm(ks[23], (D_MODEL,), 0.02)
    return {"x": x, "attn_norm_g": attn_norm_g, "w_in": w_in, "b_in": b_in, "attn_sinks": attn_sinks,
            "ssm_a_re": ssm_a_re, "ssm_a_im": ssm_a_im, "ssm_log_dt": ssm_log_dt,
            "ssm_b_re": ssm_b_re, "ssm_b_im": ssm_b_im, "ssm_c_re": ssm_c_re, "ssm_c_im": ssm_c_im,
            "ssm_d": ssm_d, "w_glu": w_glu, "b_glu": b_glu, "w_branch_attn": w_branch_attn,
            "w_branch_ssm": w_branch_ssm, "w_out": w_out, "ffn_norm_g": ffn_norm_g, "w_up": w_up,
            "conv_w": conv_w, "conv_b": conv_b, "w_down": w_down, "final_norm_g": final_norm_g}

def second_block(x, attn_norm_g, w_in, b_in, attn_sinks, ssm_a_re, ssm_a_im, ssm_log_dt, ssm_b_re, ssm_b_im,
              ssm_c_re, ssm_c_im, ssm_d, w_glu, b_glu, w_branch_attn, w_branch_ssm, w_out, ffn_norm_g,
              w_up, conv_w, conv_b, w_down, final_norm_g):
    bsz, seq = x.shape[0], x.shape[1]
    for i in range(DEPTH):
        h = rms_norm(x, attn_norm_g[i])
        proj = h @ w_in[i] + b_in[i]
        q, k, v, u, gate_attn, gate_ssm = jnp.split(proj, SPLIT_POINTS, axis=-1)
        q = q.reshape(bsz, seq, N_Q_HEADS, HEAD_DIM_2)
        k = k.reshape(bsz, seq, N_KV_HEADS, HEAD_DIM_2)
        v = v.reshape(bsz, seq, N_KV_HEADS, HEAD_DIM_2)
        attn = sliding_window_attention(q, k, v, attn_sinks[i])
        y = s5_ssm(u, ssm_a_re[i], ssm_a_im[i], ssm_log_dt[i], ssm_b_re[i], ssm_b_im[i],
                   ssm_c_re[i], ssm_c_im[i], ssm_d[i])
        y_val, y_gate = jnp.split(jax.nn.gelu(y, approximate=False) @ w_glu[i] + b_glu[i], 2, axis=-1)
        ssm = y_val * jax.nn.sigmoid(y_gate)
        merged = (jax.nn.sigmoid(gate_attn) * (attn @ w_branch_attn[i])
                  + jax.nn.sigmoid(gate_ssm) * (ssm @ w_branch_ssm[i]))
        x = x + merged @ w_out[i]
        h = rms_norm(x, ffn_norm_g[i])
        val, gate = jnp.split(h @ w_up[i], 2, axis=-1)
        gate = causal_depthwise_conv_2(gate, conv_w[i], conv_b[i])
        x = x + (val * jax.nn.gelu(gate, approximate=False)) @ w_down[i]
    return rms_norm(x, final_norm_g)


def setup_inputs(seed=0):
    out = dict(first_inputs(seed))
    for name, value in second_inputs(seed + 1).items():
        if name != "x":
            out[name + "_2"] = value
    return out


def reference(
    x, p, g_mix_pre, w_in, w_branch_a, w_branch_b, w_out, g_mix_post, g_ffn_pre, w_up, conv_w,
    conv_b, w_down, g_ffn_post, w_ple_in, w_ple_gate, attn_norm_g_2, w_in_2, b_in_2,
    attn_sinks_2, ssm_a_re_2, ssm_a_im_2, ssm_log_dt_2, ssm_b_re_2, ssm_b_im_2, ssm_c_re_2,
    ssm_c_im_2, ssm_d_2, w_glu_2, b_glu_2, w_branch_attn_2, w_branch_ssm_2, w_out_2,
    ffn_norm_g_2, w_up_2, conv_w_2, conv_b_2, w_down_2, final_norm_g_2,
):
    x = first_block(
        x, p, g_mix_pre, w_in, w_branch_a, w_branch_b, w_out, g_mix_post, g_ffn_pre, w_up,
        conv_w, conv_b, w_down, g_ffn_post, w_ple_in, w_ple_gate,
    )
    return second_block(
        x, attn_norm_g_2, w_in_2, b_in_2, attn_sinks_2, ssm_a_re_2, ssm_a_im_2, ssm_log_dt_2,
        ssm_b_re_2, ssm_b_im_2, ssm_c_re_2, ssm_c_im_2, ssm_d_2, w_glu_2, b_glu_2,
        w_branch_attn_2, w_branch_ssm_2, w_out_2, ffn_norm_g_2, w_up_2, conv_w_2, conv_b_2,
        w_down_2, final_norm_g_2,
    )


_drawn_inputs = setup_inputs


def setup_inputs(seed=0):
    import zlib

    import numpy as np

    out = dict(_drawn_inputs(seed))
    spreads = {}
    factors = {'conv_b': 6.741,
     'attn_norm_g_2': 8.0,
     'b_in_2': 8.0,
     'attn_sinks_2': 8.0,
     'ssm_a_re_2': 64.0,
     'ssm_a_im_2': 64.0,
     'ssm_log_dt_2': 64.0,
     'ssm_b_re_2': 64.0,
     'ssm_b_im_2': 64.0,
     'ssm_c_re_2': 64.0,
     'ssm_c_im_2': 64.0,
     'b_glu_2': 8.0,
     'ffn_norm_g_2': 5.733,
     'conv_b_2': 8.0,
     'final_norm_g_2': 7.775}
    for name, (base, spread) in spreads.items():
        noise = np.random.default_rng([zlib.crc32(name.encode()), seed]).standard_normal(out[name].shape)
        drawn = base * np.exp(spread * noise) if base else spread * noise
        out[name] = __import__('jax').numpy.asarray(drawn.astype(out[name].dtype))
    for name, factor in factors.items():
        out[name] = (out[name] * factor).astype(out[name].dtype)
    return out
```

```python
import math
from contextlib import ExitStack

import numpy as np
import concourse.bass as bass
from concourse import mybir

F32 = mybir.dt.float32
F32R = mybir.dt.float32r
I32 = mybir.dt.int32
ALU = mybir.AluOpType
ACT = mybir.ActivationFunctionType
AX = mybir.AxisListType

P = 128
TOK = 256
D = 2048
DT = D // P
FF = 5632
FT = FF // P
EPS = 1e-6
NEG = -1e30

PIECE_KT = 4
GROUP = 256
RING = 4

SLOTS, DILATIONS = 4, (1, 4, 16)
QA, KA, VA, QB, KB, VB, GATE_A, GATE_B = 0, 12, 24, 36, 40, 44, 48, 64
HEADS_A, HEADS_B = 12, 4
HEADS_2, KV_2, HD_2 = 16, 2, 64
Q2, K2, V2, U2, GATE_AT, GATE_SSM, PROJ2 = 0, 8, 9, 10, 14, 30, 46
STATE_TILES, STATE_BLOCK = 16, 4

BLK = 384
TAB = {"dist": (0, BLK), "pen0": (BLK, BLK), "pen1": (2 * BLK, BLK), "pen2": (3 * BLK, BLK),
       "penw": (4 * BLK, BLK), "penb": (5 * BLK, BLK),
       "tri": (6 * BLK, P), "ident": (6 * BLK + P, P), "ones": (6 * BLK + 2 * P, P)}
TAB_COLS = 6 * BLK + 3 * P

PAR, _at = {}, 0
for _name, _n in (("g_mix_pre", 16), ("g_mix_post", 16), ("g_ffn_pre", 16), ("g_ffn_post", 16),
                  ("attn_norm_g_2", 16), ("ffn_norm_g_2", 16), ("final_norm_g_2", 16),
                  ("conv_w", 3 * 88), ("conv_b", 88), ("conv_w_2", 3 * 44), ("conv_b_2", 44),
                  ("b_in_2", 46), ("b_glu_2", 8), ("ssm_d_2", 4), ("attn_sinks_2", 16),
                  ("ssm_a_re_2", 16), ("ssm_a_im_2", 16), ("ssm_log_dt_2", 16)):
    PAR[_name] = (_at, _n)
    _at += _n
PAR_COLS = _at


class Stage:

    def __init__(self, name, slots, bodies, x, x_ready, evac):
        self.name, self.slots, self.bodies = name, slots, bodies
        self.x, self.x_ready, self.evac = x, x_ready, evac
        self.pieces = [-(-kt // PIECE_KT) for _, _, kt, _ in slots]
        self.ppb = sum(self.pieces)
        assert self.ppb % RING == 0


def place(stages):
    piece = group = 0
    done = {"act": 0, "dve": 0}
    owner = []
    for st in stages:
        st.piece0, st.group0, st.evac0 = piece, group, done[st.evac]
        n = st.bodies * len(st.slots)
        for _ in range(n):
            done[st.evac] += 1
            owner.append((st.evac, done[st.evac]))
        piece += st.bodies * st.ppb
        group += n
    for st in stages:
        st.owner = owner
    return piece, group


def build(nc, a, out):
    with ExitStack() as ctx:
        def sb(name, shape, dt=F32, scope=ctx):
            return scope.enter_context(nc.sbuf_tensor(name, shape, dt))

        def sem(name):
            return ctx.enter_context(nc.semaphore(name))

        hT = sb("hT", [P, DT, TOK])
        with ExitStack() as scope:
            m2T = sb("m2T", [P, DT, TOK], scope=scope)
        act_hi = sb("act_hi", [P, DT, TOK], F32R)
        act_lo = sb("act_lo", [P, DT, TOK], F32R)
        w_raw = sb("w_raw", [P, RING, PIECE_KT, GROUP])
        w_hi = sb("w_hi", [P, RING, PIECE_KT, GROUP], F32R)
        w_lo = sb("w_lo", [P, RING, PIECE_KT, GROUP], F32R)
        tab = sb("tab", [P, TAB_COLS])
        par = sb("par", [P, PAR_COLS])
        pT = sb("pT", [P, 2, TOK])
        small_c = sb("small_c", [P, 2])
        eps, one = small_c[:, 0:1], small_c[:, 1:2]

        def table(name):
            at, n = TAB[name]
            return tab[:, at:at + n]

        def param(name, j):
            return par[:, PAR[name][0] + j:PAR[name][0] + j + 1]

        def param_at(name, j):
            return par[:, bass.ds(PAR[name][0] + j, 1)]

        ident, ones, tri = table("ident"), table("ones"), table("tri")

        def over(kept, *buffers):
            with ExitStack() as scope:
                if kept:
                    sb(f"skip{len(names)}", [P, kept], scope=scope)
                names.append(kept)
                return [sb(*b, scope=scope) for b in buffers]

        names = []
        T = TOK
        proj1, s_buf, pT_buf, bias_t, small = over(
            0, ("proj1", [P, 80, T]), ("s_buf", [P, 2, 3 * T]), ("pT_buf", [P, 3 * T]), ("bias_t", [P, 3 * T]),
            ("small", [P, 32]))
        z_b, t_b, l_b, sp_b, lw_b = over(80 * T, *((n, [P, BLK]) for n in ("z_b", "t_b", "l_b", "sp_b", "lw_b")))
        mT, eT, sq, tmp, sg, std, rstd = over(
            0, ("mT", [P, DT, T]), ("eT", [P, DT, T]), ("sq", [P, 2, 4, T]), ("tmp", [P, 2, 4, T]), ("sg", [P, 2, T]),
            ("std", [P, T]), ("rstd", [P, T]))
        f_hi, f_lo, gate_y, gate_g, val_y = over(
            0, ("f_hi", [P, FT, T], F32R), ("f_lo", [P, FT, T], F32R), ("gate_y", [P, 2, T]), ("gate_g", [P, 2, T]),
            ("val_y", [P, 2, T]))
        p_hi, p_lo = over(2 * FT * T, ("p_hi", [P, 2, T], F32R), ("p_lo", [P, 2, T], F32R))
        proj2, kpad, vtok, vpad, y2 = over(
            0, ("proj2", [P, PROJ2, T]), ("kpad", [P, KV_2, 2, T]), ("vtok", [P, 2, P]), ("vpad", [P, KV_2, 2, 2, P]),
            ("y2", [P, 4, T]))
        kept2 = (PROJ2 + 4 + 1 + 4 + 4) * T
        s2_buf, pT2_buf, bias2_t, small2 = over(
            kept2, ("s2_buf", [P, 2, BLK]), ("pT2_buf", [P, BLK]), ("bias2_t", [P, BLK]), ("small2", [P, 32]))
        b_pad, c_pad, cz, rot, vrot, scn, xs, pr, ssm, ssm_i = over(
            kept2, ("b_pad", [P, STATE_BLOCK, 2, P]), ("c_pad", [P, STATE_BLOCK, 2, P]), ("cz", [P, 2, 2, P]),
            ("rot", [P, 2, STATE_BLOCK, T]), ("vrot", [P, 2, T]), ("scn", [P, 2, T]), ("xs", [P, 2, 2, T]),
            ("pr", [P, 4, T]), ("ssm", [P, 32, STATE_TILES]), ("ssm_i", [P, STATE_TILES], I32))
        glu_v, glu_g = over(kept2, ("glu_v", [P, 4, T]), ("glu_g", [P, 4, T]))

        bank = [ctx.enter_context(nc.psum_tensor(f"bank{i}", [P, 512], F32)) for i in range(2)]
        ps_a = [ctx.enter_context(nc.psum_tensor(f"ps_a{i}", [P, 512], F32)) for i in range(2)]
        ps_t = [ctx.enter_context(nc.psum_tensor(f"ps_t{i}", [P, 512], F32)) for i in range(2)]
        ps_o = ctx.enter_context(nc.psum_tensor("ps_o", [P, 512], F32))
        ps_n = ctx.enter_context(nc.psum_tensor("ps_n", [P, 512], F32))

        loaded = sem("loaded")
        raw_landed = [sem(f"raw_landed{i}") for i in range(RING)]
        slots_freed = sem("slots_freed")
        hi_ready, lo_ready = sem("hi_ready"), sem("lo_ready")
        piece_used = sem("piece_used")
        evacuated = {"act": sem("evac_act"), "dve": sem("evac_dve")}
        split_ready = sem("split_ready")
        f_ready = sem("f_ready")
        consts = sem("consts")
        resid_ready = sem("resid_ready")
        sq_ready, sq_used, std_ready = sem("sq_ready"), sem("sq_used"), sem("std_ready")
        gate_act = sem("gate_act")
        gates_open = sem("gates_open")
        v_turned, v_kept = sem("v_turned"), sem("v_kept")
        sc_ready, sc_read, s_max = sem("sc_ready"), sem("sc_read"), sem("s_max")
        p_exp, p_norm, p_turned, pt_kept = sem("p_exp"), sem("p_norm"), sem("p_turned"), sem("pt_kept")
        o_ready, o_kept = sem("o_ready"), sem("o_kept")
        zb_ready, zb_abs, zb_log = sem("zb_ready"), sem("zb_abs"), sem("zb_log")
        sp_ready, cum_ready, lw_ready, w_ready = sem("sp_ready"), sem("cum_ready"), sem("lw_ready"), sem("w_ready")
        ob_ready, ob_kept = sem("ob_ready"), sem("ob_kept")
        pad_ready, bc_landed = sem("pad_ready"), sem("bc_landed")
        v_ready, v_read, x_ready, x_used = sem("v_ready"), sem("v_read"), sem("x_ready"), sem("x_used")
        y_kept, y_act, ple_used = sem("y_kept"), sem("y_act"), sem("ple_used")
        stored = sem("stored")

        def cols(w, kt, x0, step, at=0):
            return (a[w].rearrange("(t p) n -> p t n", p=P), lambda i: i * step + at, kt, x0)

        def main_x(first):
            return lambda j: (split_ready, first + j + 1)

        act_x, f_x, p_x = (act_hi, act_lo), (f_hi, f_lo), (p_hi, p_lo)
        G = GROUP
        SPLIT = {}
        at = 0
        for name, n in (("mix", 4), ("y1", 2), ("merged", 4), ("ffn", 4), ("ple_in", 1), ("ple_gate", 4),
                        ("mix2", 4), ("attn2", 2), ("ssm_y", 1), ("ssm", 1), ("merged2", 4), ("ffn2", 4)):
            SPLIT[name] = at
            at += n
        branch1 = [s for k in range(2) for s in
                   (cols("w_branch_a", 4, 0, 2 * G, k * G), cols("w_branch_b", 4, 4, 2 * G, k * G))]
        branch2 = [s for k in range(4) for s in
                   (cols("w_branch_attn_2", 8, 0, 4 * G, k * G), cols("w_branch_ssm_2", 4, 12, 4 * G, k * G))]
        pair = lambda w: [cols(w, 16, 0, 2 * G), cols(w, 16, 0, 2 * G, G)]
        quad = lambda w, kt: [cols(w, kt, 0, 4 * G, k * G) for k in range(4)]
        st_in = Stage("in", pair("w_in"), 20, act_x, main_x(SPLIT["mix"]), "act")
        st_branch = Stage("branch", branch1, 4, act_x, None, "dve")
        st_out = Stage("out", pair("w_out"), 4, act_x, main_x(SPLIT["merged"]), "act")
        st_up = Stage("up", [cols("w_up", 16, 0, G), cols("w_up", 16, 0, G, FF)], 22, act_x,
                      main_x(SPLIT["ffn"]), "dve")
        st_down = Stage("down", quad("w_down", FT), 2, f_x, lambda j: (f_ready, 2 * j + 2), "act")
        st_ple = Stage("ple", quad("w_ple_in", 2), 2, p_x, main_x(SPLIT["ple_in"]), "act")
        st_gate = Stage("ple_gate", pair("w_ple_gate"), 4, act_x, main_x(SPLIT["ple_gate"]), "act")
        st_in2 = Stage("in2", pair("w_in_2"), 11, act_x, main_x(SPLIT["mix2"]), "act")
        st_in2b = Stage("in2b", [cols("w_in_2", 16, 0, 0, 22 * G)], 1, act_x, None, "act")
        st_glu = Stage("glu", [cols("w_glu_2", 4, 8, 0, k * G) for k in range(4)], 1, act_x,
                       lambda j: (split_ready, SPLIT["ssm_y"] + 1), "act")
        st_branch2 = Stage("branch2", branch2, 2, act_x, None, "dve")
        st_out2 = Stage("out2", pair("w_out_2"), 4, act_x, main_x(SPLIT["merged2"]), "dve")
        st_up2 = Stage("up2", [cols("w_up_2", 16, 0, G, FF), cols("w_up_2", 16, 0, G)], 22, act_x,
                       main_x(SPLIT["ffn2"]), "dve")
        st_down2 = Stage("down2", quad("w_down_2", FT), 2, f_x, lambda j: (f_ready, 22 + 2 * j + 2), "dve")
        stages = [st_in, st_branch, st_out, st_up, st_down, st_ple, st_gate,
                  st_in2, st_in2b, st_glu, st_branch2, st_out2, st_up2, st_down2]
        place(stages)

        def bodies(eng, st, body):
            body(0, True)
            if st.bodies > 1:
                with eng.Fori(1, st.bodies) as i:
                    body(i, False)

        def with_epilogue(eng, st, piece, epilogue):
            n = len(st.slots)

            def body(i, first):
                j0 = 0
                for s in range(n):
                    for j in range(st.pieces[s]):
                        piece(i, j0 + j, s)
                        if j == min(3, st.pieces[s] - 1) and epilogue and not (first and s == 0):
                            epilogue(i if s else i - 1, (s - 1) % n)
                    j0 += st.pieces[s]

            bodies(eng, st, body)
            if epilogue:
                epilogue(st.bodies - 1, n - 1)

        block = ctx.enter_context(nc.Block())

        @block.sync
        def _(sp):
            sp.dma_start(tab[:, :], a["tables"]).then_inc(loaded, 16)
            sp.dma_start(par[:, :], a["params"]).then_inc(loaded, 16)
            for st in stages:
                def body(i, first, st=st):
                    j0 = 0
                    at_col = [col(i) if first else sp.snap(col(i)) for _, col, _, _ in st.slots]
                    for s, (w, _, kt, _) in enumerate(st.slots):
                        c = at_col[s]
                        for j in range(st.pieces[s]):
                            q = st.piece0 + i * st.ppb + j0 + j
                            k = (j0 + j) % RING
                            n = min(PIECE_KT, kt - j * PIECE_KT)
                            if not (first and st.piece0 + j0 + j < RING):
                                sp.wait_ge(lo_ready, q - RING + 1)
                                sp.sem_inc(slots_freed, 1)
                            sp.dma_start(w_raw[:, k, 0:n, :], w[:, j * PIECE_KT:j * PIECE_KT + n, bass.ds(c, GROUP)]
                                         ).then_inc(raw_landed[k], 16)
                        j0 += st.pieces[s]
                bodies(sp, st, body)
            for c in range(4):
                sp.wait_ge(split_ready, at + c + 1)
                sp.dma_start(out[:, 4 * c:4 * c + 4, :], hT[:, 4 * c:4 * c + 4, :]).then_inc(stored, 16)
            sp.wait_ge(stored, 64)

        @block.tensor
        def _(pe):
            def mm(o, l, r, start, stop):
                return pe.matmul(o, l, r, start=start, stop=stop, skip_group_check=True)

            def stream(st):
                xh, xl = st.x

                def body(i, first):
                    j0 = 0
                    for s, (_, _, kt, x0) in enumerate(st.slots):
                        g_in = st.group0 + s if first else None
                        ps = bank[(st.group0 + s) % 2]
                        if first and g_in >= 2:
                            eng, n = st.owner[g_in - 2]
                            pe.wait_ge(evacuated[eng], n)
                        elif not first:
                            pe.wait_ge(evacuated[st.evac], st.evac0 + i * len(st.slots) + s - 1)
                        for j in range(st.pieces[s]):
                            q = st.piece0 + i * st.ppb + j0 + j
                            k = (j0 + j) % RING
                            n = min(PIECE_KT, kt - j * PIECE_KT)
                            if first and s == 0 and st.x_ready:
                                pe.wait_ge(*st.x_ready(j))
                            pe.wait_ge(hi_ready, q + 1)
                            for t in range(n):
                                x = x0 + j * PIECE_KT + t
                                for c in range(2):
                                    o = ps[:, c * TOK:(c + 1) * TOK]
                                    w = w_hi[:, k, t, c * P:(c + 1) * P]
                                    mm(o, w, xh[:, x, :], j == 0 and t == 0 and c == 0, False)
                                    mm(o, w, xl[:, x, :], False, False)
                            pe.wait_ge(lo_ready, q + 1)
                            for t in range(n):
                                x = x0 + j * PIECE_KT + t
                                for c in range(2):
                                    last = mm(ps[:, c * TOK:(c + 1) * TOK], w_lo[:, k, t, c * P:(c + 1) * P],
                                              xh[:, x, :], False, j == st.pieces[s] - 1 and t == n - 1)
                            last.then_inc(piece_used, 1)
                        j0 += st.pieces[s]
                bodies(pe, st, body)

            def sum_squares(n):
                for c in range(4):
                    pe.wait_ge(sq_ready, 4 * n + c + 1)
                    for t in range(4):
                        last = mm(ps_n[:, 0:TOK], ones, sq[:, c % 2, t, :], c == 0 and t == 0, c == 3 and t == 3)
                    last.then_inc(sq_used, 1)

            def turn_values():
                for n, tile in enumerate([VA + h for h in range(HEADS_A)] + [VB + h for h in range(HEADS_B)]):
                    if n >= 2:
                        pe.wait_ge(v_kept, n - 1)
                    for t in range(2):
                        last = pe.transpose(ps_t[n % 2][:, t * P:(t + 1) * P],
                                            proj1[:, tile, t * P:(t + 1) * P], ident)
                    last.then_inc(v_turned, 1)

            def dilated():
                units = [(h, qt) for h in range(SLOTS) for qt in range(2)]

                def scores(u):
                    h, qt = units[u]
                    if u:
                        pe.wait_ge(sc_read, u)
                    keys = P * (qt + 1)
                    for g in range(3):
                        o = ps_a[g // 2][:, (g % 2) * keys:(g % 2) * keys + keys]
                        last = mm(o, proj1[:, QA + 4 * g + h, qt * P:qt * P + P],
                                  proj1[:, KA + 4 * g + h, 0:keys], g != 1, g != 0)
                    last.then_inc(sc_ready, 1)

                def values(u):
                    h, qt = units[u]
                    n = 3 * (qt + 1)
                    pe.wait_ge(p_norm, u + 1)
                    for b in range(n):
                        last = pe.transpose(ps_t[b // 4][:, (b % 4) * P:(b % 4) * P + P],
                                            s_buf[:, u % 2, b * P:(b + 1) * P], ident)
                    last.then_inc(p_turned, 1)
                    pe.wait_ge(pt_kept, u + 1)
                    for b in range(n):
                        g, kt = b // (qt + 1), b % (qt + 1)
                        v = proj1[:, VA + 4 * g + h, kt * P:kt * P + P]
                        last = mm(ps_o[:, 0:P], v, pT_buf[:, b * P:(b + 1) * P], b == 0, b == n - 1)
                    last.then_inc(o_ready, 1)

                scores(0)
                pe.wait_ge(v_kept, HEADS_A + HEADS_B)
                for u in range(len(units)):
                    if u + 1 < len(units):
                        scores(u + 1)
                    if u:
                        pe.wait_ge(o_kept, u)
                    values(u)

            def sticks():
                for h in range(HEADS_B):
                    if h == 0:
                        pe.wait_ge(o_kept, 8)
                        pe.wait_ge(sc_read, 8)
                    else:
                        pe.wait_ge(ob_kept, h)
                    q, k = proj1[:, QB + h, :], proj1[:, KB + h, :]
                    mm(ps_a[0][:, 0:TOK], k[:, 0:P], q, True, True)
                    mm(ps_a[0][:, TOK:BLK], k[:, P:TOK], q[:, P:TOK], False, True).then_inc(zb_ready, 1)
                    pe.wait_ge(sp_ready, h + 1)
                    mm(ps_t[0][:, 0:TOK], tri, sp_b[:, 0:TOK], True, False)
                    mm(ps_t[0][:, P:TOK], ones, sp_b[:, TOK:BLK], False, True)
                    mm(ps_t[0][:, TOK:BLK], tri, sp_b[:, TOK:BLK], False, True).then_inc(cum_ready, 1)
                    pe.wait_ge(w_ready, h + 1)
                    v = proj1[:, VB + h, :]
                    mm(ps_o[:, 0:TOK], v[:, 0:P], t_b[:, 0:TOK], True, False)
                    mm(ps_o[:, P:TOK], v[:, P:TOK], t_b[:, TOK:BLK], False, True).then_inc(ob_ready, 1)

            def window():
                def scores(h):
                    if h:
                        pe.wait_ge(sc_read, 8 + h)
                    j, half = h // (HEADS_2 // KV_2), h % 2
                    q, k = proj2[:, Q2 + h // 2, :], kpad[:, j, half, :]
                    mm(ps_a[0][:, 0:P], q[:, 0:P], k[:, 0:P], True, True)
                    mm(ps_a[0][:, P:BLK], q[:, P:TOK], k, False, True).then_inc(sc_ready, 1)

                def values(h):
                    j, half = h // (HEADS_2 // KV_2), h % 2
                    pe.wait_ge(p_norm, 8 + h + 1)
                    for b in range(3):
                        last = pe.transpose(ps_t[0][:, b * P:(b + 1) * P], s2_buf[:, h % 2, b * P:(b + 1) * P], ident)
                    last.then_inc(p_turned, 1)
                    pe.wait_ge(pt_kept, 8 + h + 1)
                    if half == 0 and h:
                        pe.wait_ge(o_kept, 8 + h // 2)
                    mm(ps_o[:, 0:P], vpad[:, j, half, 0, :], pT2_buf[:, 0:P], half == 0, half == 1)
                    mm(ps_o[:, P:TOK], vpad[:, j, half, 0, :], pT2_buf[:, P:2 * P], False, False)
                    last = mm(ps_o[:, P:TOK], vpad[:, j, half, 1, :], pT2_buf[:, 2 * P:BLK], False, half == 1)
                    if half:
                        last.then_inc(o_ready, 1)

                pe.wait_ge(evacuated["act"], st_in2b.evac0 + 1)
                for t in range(2):
                    last = pe.transpose(ps_t[0][:, t * P:(t + 1) * P], proj2[:, V2, t * P:(t + 1) * P], ident)
                last.then_inc(v_turned, 1)
                pe.wait_ge(pad_ready, 1)
                scores(0)
                for h in range(HEADS_2):
                    if h + 1 < HEADS_2:
                        scores(h + 1)
                    values(h)

            def state_space():
                def drive(n):
                    b, k = n // STATE_BLOCK, n % STATE_BLOCK
                    if k == 0:
                        pe.wait_ge(bc_landed, 32 * (b + 1))
                    if n >= 2:
                        pe.wait_ge(v_read, n - 1)
                    u = proj2[:, U2 + b, :]
                    mm(ps_a[n % 2][:, 0:TOK], b_pad[:, k, 0, :], u, True, True)
                    mm(ps_a[n % 2][:, TOK:], b_pad[:, k, 1, :], u, False, True).then_inc(v_ready, 1)

                def read_out(n):
                    k = n % STATE_BLOCK
                    if k == 0 and n:
                        pe.wait_ge(y_kept, n // STATE_BLOCK)
                    pe.wait_ge(x_ready, n + 1)
                    mm(ps_o[:, 0:TOK], cz[:, n % 2, 0, :], xs[:, n % 2, 0, :], k == 0, False)
                    mm(ps_o[:, 0:TOK], cz[:, n % 2, 1, :], xs[:, n % 2, 1, :], False, k == 3).then_inc(x_used, 1)

                pe.wait_ge(o_kept, 16)
                drive(0)
                for n in range(STATE_TILES):
                    if (n + 1) % STATE_BLOCK:
                        drive(n + 1)
                    read_out(n)
                    if n + 1 < STATE_TILES and (n + 1) % STATE_BLOCK == 0:
                        drive(n + 1)

            pe.wait_ge(loaded, 64)
            sum_squares(0)
            stream(st_in)
            pe.wait_ge(evacuated["act"], 40)
            turn_values()
            dilated()
            sticks()
            pe.wait_ge(split_ready, SPLIT["y1"] + 2)
            stream(st_branch)
            stream(st_out)
            sum_squares(1)
            sum_squares(2)
            stream(st_up)
            stream(st_down)
            stream(st_ple)
            sum_squares(3)
            stream(st_gate)
            sum_squares(4)
            stream(st_in2)
            stream(st_in2b)
            window()
            state_space()
            stream(st_glu)
            pe.wait_ge(split_ready, SPLIT["ssm"] + 1)
            stream(st_branch2)
            stream(st_out2)
            sum_squares(5)
            stream(st_up2)
            stream(st_down2)
            sum_squares(6)

        @block.scalar
        def _(act):
            def stream(st, epilogue=None):
                def hi(i, j, s):
                    q = st.piece0 + i * st.ppb + j
                    k = j % RING
                    n = min(PIECE_KT, st.slots[s][2])
                    act.wait_ge(raw_landed[k], 16 * (st.piece0 // RING + j // RING + 1) + i * (16 * st.ppb // RING))
                    if not (isinstance(i, int) and q < RING):
                        act.wait_ge(piece_used, q - RING + 1)
                    act.activation(w_hi[:, k, 0:n, :], w_raw[:, k, 0:n, :], ACT.Copy).then_inc(hi_ready, 1)
                with_epilogue(act, st, hi, epilogue)

            def whole(st, i, s):
                act.wait_ge(piece_used, st.piece0 + i * st.ppb + sum(st.pieces[:s + 1]))

            def copy_to(st, dst):
                def ep(i, s):
                    whole(st, i, s)
                    t = (i * len(st.slots) + s) * 2
                    act.activation(dst[:, bass.ds(t, 2), :],
                                   bank[(st.group0 + s) % 2][:, :].rearrange("p (c t) -> p c t", c=2),
                                   ACT.Copy).then_inc(evacuated["act"], 1)
                return ep

            def biased(st, dst, name, tile0=0, func=ACT.Identity):
                def ep(i, s):
                    whole(st, i, s)
                    for c in range(2):
                        t = tile0 + (i * len(st.slots) + s) * 2 + c
                        last = act.activation(dst[:, bass.ds(t, 1), :],
                                              bank[(st.group0 + s) % 2][:, c * TOK:(c + 1) * TOK], func,
                                              bias=param_at(name, t))
                    last.then_inc(evacuated["act"], 1)
                return ep

            def squares(n, src):
                for c in range(4):
                    if 4 * n + c >= 2:
                        act.wait_ge(sq_used, 4 * n + c - 1)
                    act.activation(sq[:, c % 2, :, :], src[:, 4 * c:4 * c + 4, :], ACT.Square).then_inc(sq_ready, 1)
                act.wait_ge(sq_used, 4 * n + 4)
                act.activation(std[:, :], ps_n[:, 0:TOK], ACT.Sqrt, bias=eps[:, 0:1],
                               scale=1.0 / D).then_inc(std_ready, 1)

            def dilated():
                act.drain()
                for t in range(GATE_A, 80, 8):
                    last = act.activation(proj1[:, t:t + 8, :], proj1[:, t:t + 8, :], ACT.Sigmoid)
                last.then_inc(gates_open, 1)
                for u in range(2 * SLOTS):
                    n = 3 * P * (u % 2 + 1)
                    act.wait_ge(s_max, u + 1)
                    act.activation(s_buf[:, u % 2, 0:n], s_buf[:, u % 2, 0:n], ACT.Exp,
                                   bias=small[:, 8 + u % 2:9 + u % 2],
                                   accum_out=small[:, 16 + u % 2:17 + u % 2]).then_inc(p_exp, 1)

            def sticks():
                for h in range(HEADS_B):
                    act.wait_ge(zb_abs, h + 1)
                    act.activation(l_b[:, :], t_b[:, :], ACT.Exp, scale=-1.0)
                    act.drain()
                    act.activation(l_b[:, :], l_b[:, :], ACT.Ln, bias=one[:, 0:1]).then_inc(zb_log, 1)
                    act.wait_ge(lw_ready, h + 1)
                    act.activation(t_b[:, :], lw_b[:, :], ACT.Exp).then_inc(w_ready, 1)

            def window():
                for h in range(HEADS_2):
                    act.wait_ge(s_max, 8 + h + 1)
                    b = s2_buf[:, h % 2, :]
                    o = 16 * (h % 2)
                    act.activation(small2[:, o + 4:o + 6], small2[:, o:o + 2], ACT.Exp, bias=param("attn_sinks_2", h))
                    act.activation(b[:, 0:P], b[:, 0:P], ACT.Exp, bias=small2[:, o:o + 1],
                                   accum_out=small2[:, o + 2:o + 3])
                    act.activation(b[:, P:BLK], b[:, P:BLK], ACT.Exp, bias=small2[:, o + 1:o + 2],
                                   accum_out=small2[:, o + 3:o + 4]).then_inc(p_exp, 1)

            def gelu_gate(st, base, func):
                def ep(i, s):
                    if s == 0:
                        return
                    act.wait_ge(evacuated["dve"], st.evac0 + 2 * i + 1)
                    if not (isinstance(i, int) and base + i == 0):
                        act.wait_ge(f_ready, base + i)
                    act.activation(gate_g[:, :, :], gate_y[:, :, :], func).then_inc(gate_act, 1)
                return ep

            act.dma_start(hT[:, :, :], a["xT"]).then_inc(loaded, 16)
            act.dma_start(pT[:, :, :], a["pT"]).then_inc(loaded, 16)
            act.wait_ge(loaded, 64)
            act.wait_ge(consts, 1)
            squares(0, hT)
            stream(st_in, copy_to(st_in, proj1))
            dilated()
            sticks()
            stream(st_branch)
            stream(st_out, copy_to(st_out, mT))
            act.drain()
            squares(1, mT)
            act.wait_ge(resid_ready, 1)
            squares(2, hT)
            stream(st_up, gelu_gate(st_up, 0, ACT.Gelu_apprx_tanh))
            stream(st_down, copy_to(st_down, m2T))
            stream(st_ple, copy_to(st_ple, eT))
            act.drain()
            squares(3, m2T)

            def ple(i, s):
                whole(st_gate, i, s)
                n = i * 2 + s
                if not (isinstance(i, int) and n == 0):
                    act.wait_ge(ple_used, n)
                act.activation(sg[:, :, :], bank[(st_gate.group0 + s) % 2][:, :].rearrange("p (c t) -> p c t", c=2),
                               ACT.Sigmoid).then_inc(evacuated["act"], 1)

            stream(st_gate, ple)
            act.wait_ge(ple_used, 8)
            squares(4, hT)
            stream(st_in2, biased(st_in2, proj2, "b_in_2"))
            stream(st_in2b, biased(st_in2b, proj2, "b_in_2", 44))
            act.drain()
            for t in range(GATE_AT, PROJ2, 8):
                last = act.activation(proj2[:, t:t + 8, :], proj2[:, t:t + 8, :], ACT.Sigmoid)
            last.then_inc(gates_open, 1)
            window()
            act.wait_ge(y_kept, 4)
            act.activation(y2[:, :, :], y2[:, :, :], ACT.Gelu).then_inc(y_act, 1)

            def glu(i, s):
                whole(st_glu, i, s)
                dst, func = (glu_v, ACT.Identity) if s < 2 else (glu_g, ACT.Sigmoid)
                for c in range(2):
                    last = act.activation(dst[:, 2 * (s % 2) + c, :],
                                          bank[(st_glu.group0 + s) % 2][:, c * TOK:(c + 1) * TOK],
                                          func, bias=param("b_glu_2", 2 * s + c))
                last.then_inc(evacuated["act"], 1)

            stream(st_glu, glu)
            stream(st_branch2)
            stream(st_out2)
            act.wait_ge(evacuated["dve"], st_out2.evac0 + 8)
            squares(5, hT)
            stream(st_up2, gelu_gate(st_up2, 22, ACT.Gelu))
            stream(st_down2)
            act.wait_ge(evacuated["dve"], st_down2.evac0 + 8)
            squares(6, hT)

        @block.vector
        def _(dve):
            def stream(st, epilogue=None):
                def lo(i, j, s):
                    q = st.piece0 + i * st.ppb + j
                    k = j % RING
                    n = min(PIECE_KT, st.slots[s][2])
                    dve.wait_ge(hi_ready, q + 1)
                    dve.tensor_tensor(w_lo[:, k, 0:n, :], w_raw[:, k, 0:n, :], w_hi[:, k, 0:n, :].bitcast(F32),
                                      ALU.subtract).then_inc(lo_ready, 1)
                with_epilogue(dve, st, lo, epilogue)

            def whole(st, i, s):
                dve.wait_ge(piece_used, st.piece0 + i * st.ppb + sum(st.pieces[:s + 1]))

            def split(src, hi, lo):
                dve.tensor_copy(hi, src)
                dve.drain()
                return dve.tensor_tensor(lo, src, hi.bitcast(F32), ALU.subtract)

            def root(n):
                dve.wait_ge(std_ready, n + 1)
                dve.reciprocal(rstd[:, :], std[:, :])
                dve.drain()

            def norm_split(n, gain):
                root(n)
                for c in range(4):
                    for t in range(4):
                        dve.scalar_tensor_tensor(out=tmp[:, c % 2, t, :], in0=hT[:, 4 * c + t, :], scalar=param(gain, 4 * c + t),
                                                 in1=rstd[:, :], op0=ALU.mult, op1=ALU.mult)
                    dve.drain()
                    split(tmp[:, c % 2, :, :], act_hi[:, 4 * c:4 * c + 4, :], act_lo[:, 4 * c:4 * c + 4, :]).then_inc(split_ready, 1)

            def add_normed(n, src, gain):
                root(n)
                for c in range(4):
                    for t in range(4):
                        dve.scalar_tensor_tensor(out=tmp[:, c % 2, t, :], in0=src[:, 4 * c + t, :], scalar=param(gain, 4 * c + t),
                                                 in1=rstd[:, :], op0=ALU.mult, op1=ALU.mult)
                    dve.drain()
                    last = dve.tensor_tensor(hT[:, 4 * c:4 * c + 4, :], hT[:, 4 * c:4 * c + 4, :], tmp[:, c % 2, :, :], ALU.add)
                return last

            def dilated():
                scale = 1.0 / math.sqrt(P)
                units = [(h, qt) for h in range(SLOTS) for qt in range(2)]

                def biased_max(u):
                    h, qt = units[u]
                    keys = P * (qt + 1)
                    c0 = qt * P
                    dve.wait_ge(sc_ready, u + 1)
                    if u >= 2:
                        dve.wait_ge(p_turned, u - 1)
                    for g in range(3):
                        slope = 2.0 ** (-8.0 * (4 * g + h + 1) / HEADS_A)
                        dve.scalar_tensor_tensor(out=bias_t[:, g * keys:(g + 1) * keys],
                                                 in0=table("dist")[:, c0:c0 + keys], scalar=-slope,
                                                 in1=table(f"pen{g}")[:, c0:c0 + keys], op0=ALU.mult, op1=ALU.add)
                    dve.drain()
                    for g in range(3):
                        last = dve.scalar_tensor_tensor(
                            out=s_buf[:, u % 2, g * keys:(g + 1) * keys],
                            in0=ps_a[g // 2][:, (g % 2) * keys:(g % 2) * keys + keys], scalar=scale,
                            in1=bias_t[:, g * keys:(g + 1) * keys], op0=ALU.mult, op1=ALU.add)
                    last.then_inc(sc_read, 1)
                    dve.drain()
                    m = small[:, u % 2:u % 2 + 1]
                    dve.tensor_reduce(m, s_buf[:, u % 2, 0:3 * keys], AX.X, ALU.max)
                    dve.drain()
                    dve.tensor_scalar(small[:, 8 + u % 2:9 + u % 2], m, -1.0, None, ALU.mult).then_inc(s_max, 1)

                def normed(u):
                    n = 3 * P * (units[u][1] + 1)
                    dve.wait_ge(p_exp, u + 1)
                    r = small[:, 24 + u % 2:25 + u % 2]
                    dve.reciprocal(r, small[:, 16 + u % 2:17 + u % 2])
                    dve.drain()
                    dve.tensor_scalar(s_buf[:, u % 2, 0:n], s_buf[:, u % 2, 0:n], r, None, ALU.mult).then_inc(p_norm, 1)

                def keep(u):
                    h, qt = units[u]
                    n = 3 * P * (qt + 1)
                    dve.wait_ge(p_turned, u + 1)
                    if n > 512:
                        dve.tensor_copy(pT_buf[:, 512:n], ps_t[1][:, 0:n - 512])
                    dve.tensor_copy(pT_buf[:, 0:min(n, 512)], ps_t[0][:, 0:min(n, 512)]).then_inc(pt_kept, 1)

                def keep_out(u):
                    h, qt = units[u]
                    dve.wait_ge(o_ready, u + 1)
                    dve.tensor_copy(proj1[:, QA + h, qt * P:qt * P + P], ps_o[:, 0:P]).then_inc(o_kept, 1)

                biased_max(0)
                for u in range(len(units)):
                    normed(u)
                    if u + 1 < len(units):
                        biased_max(u + 1)
                    keep(u)
                    keep_out(u)

            def sticks():
                for h in range(HEADS_B):
                    dve.wait_ge(zb_ready, h + 1)
                    dve.scalar_tensor_tensor(out=z_b[:, :], in0=ps_a[0][:, 0:BLK], scalar=1.0 / math.sqrt(P),
                                             in1=table("penb"), op0=ALU.mult, op1=ALU.add)
                    dve.drain()
                    dve.scalar_tensor_tensor(out=t_b[:, :], in0=z_b[:, :], scalar=-1.0, in1=z_b[:, :],
                                             op0=ALU.mult, op1=ALU.max).then_inc(zb_abs, 1)
                    dve.wait_ge(zb_log, h + 1)
                    dve.scalar_tensor_tensor(out=sp_b[:, :], in0=z_b[:, :], scalar=0.0, in1=l_b[:, :],
                                             op0=ALU.max, op1=ALU.add).then_inc(sp_ready, 1)
                    dve.wait_ge(cum_ready, h + 1)
                    dve.tensor_tensor(lw_b[:, :], z_b[:, :], ps_t[0][:, 0:BLK], ALU.subtract).then_inc(lw_ready, 1)
                    dve.wait_ge(ob_ready, h + 1)
                    dve.tensor_copy(proj1[:, QB + h, :], ps_o[:, 0:TOK]).then_inc(ob_kept, 1)

            def window():
                dve.wait_ge(evacuated["act"], st_in2b.evac0 + 1)
                dve.memset(kpad[:, :, :, :], 0.0)
                dve.memset(vpad[:, :, :, :, :], 0.0)
                dve.wait_ge(v_turned, HEADS_A + HEADS_B + 1)
                dve.tensor_copy(vtok[:, :, :], ps_t[0][:, 0:TOK].rearrange("p (k c) -> p k c", k=2))
                dve.drain()
                for j in range(KV_2):
                    for half in range(2):
                        r, s = slice(HD_2 * half, HD_2 * half + HD_2), slice(HD_2 * j, HD_2 * j + HD_2)
                        dve.tensor_copy(kpad[r, j, half, :], proj2[s, K2, :])
                        last = dve.tensor_copy(vpad[:, j, half, :, r], vtok[:, :, s])
                last.then_inc(pad_ready, 1)

                def biased_max(h):
                    o = 16 * (h % 2)
                    slope = 2.0 ** (-8.0 * (h + 1) / HEADS_2)
                    b = s2_buf[:, h % 2, :]
                    dve.scalar_tensor_tensor(out=bias2_t[:, :], in0=table("dist"), scalar=-slope, in1=table("penw"),
                                             op0=ALU.mult, op1=ALU.add)
                    dve.drain()
                    dve.wait_ge(sc_ready, 8 + h + 1)
                    if h >= 2:
                        dve.wait_ge(p_turned, 8 + h - 1)
                    dve.scalar_tensor_tensor(out=b, in0=ps_a[0][:, 0:BLK], scalar=HD_2 ** -0.5, in1=bias2_t[:, :],
                                             op0=ALU.mult, op1=ALU.add).then_inc(sc_read, 1)
                    dve.drain()
                    dve.tensor_reduce(small2[:, o + 6:o + 7], b[:, 0:P], AX.X, ALU.max)
                    dve.tensor_reduce(small2[:, o + 7:o + 8], b[:, P:BLK], AX.X, ALU.max)
                    dve.drain()
                    dve.tensor_scalar(small2[:, o:o + 2], small2[:, o + 6:o + 8], param("attn_sinks_2", h), -1.0,
                                      ALU.max, ALU.mult).then_inc(s_max, 1)

                def normed(h):
                    o = 16 * (h % 2)
                    b = s2_buf[:, h % 2, :]
                    dve.wait_ge(p_exp, 8 + h + 1)
                    dve.tensor_tensor(small2[:, o + 8:o + 10], small2[:, o + 2:o + 4], small2[:, o + 4:o + 6], ALU.add)
                    dve.drain()
                    dve.reciprocal(small2[:, o + 10:o + 12], small2[:, o + 8:o + 10])
                    dve.drain()
                    dve.tensor_scalar(b[:, 0:P], b[:, 0:P], small2[:, o + 10:o + 11], None, ALU.mult)
                    dve.tensor_scalar(b[:, P:BLK], b[:, P:BLK], small2[:, o + 11:o + 12], None, ALU.mult).then_inc(p_norm, 1)

                biased_max(0)
                for h in range(HEADS_2):
                    normed(h)
                    if h + 1 < HEADS_2:
                        biased_max(h + 1)
                    dve.wait_ge(p_turned, 8 + h + 1)
                    dve.tensor_copy(pT2_buf[:, :], ps_t[0][:, 0:BLK]).then_inc(pt_kept, 1)
                    if h % 2:
                        dve.wait_ge(o_ready, 8 + h // 2 + 1)
                        dve.tensor_copy(proj2[:, Q2 + h // 2, :], ps_o[:, 0:TOK]).then_inc(o_kept, 1)

            def discretize():
                DT_, MAG, TH, CO, SI, ZR, ZI, NZR, NZI, A0, A1, A2, A3, POW = *range(13), 14
                v = lambda i: ssm[:, i, :]
                are, aim, ldt = (par[:, PAR[n][0]:PAR[n][0] + STATE_TILES]
                                 for n in ("ssm_a_re_2", "ssm_a_im_2", "ssm_log_dt_2"))

                def ts(o, x, s1, s2, op0, op1=None):
                    dve.tensor_scalar(o, x, s1, s2, op0, op1) if op1 is not None else dve.tensor_scalar(o, x, s1, None, op0)
                    dve.drain()

                def tt(o, x, y, op):
                    dve.tensor_tensor(o, x, y, op)
                    dve.drain()

                def stt(o, x, s, y, op0, op1):
                    dve.scalar_tensor_tensor(out=o, in0=x, scalar=s, in1=y, op0=op0, op1=op1)
                    dve.drain()

                def exp(o, x):
                    r, n, p = v(A0), v(A1), v(A2)
                    ts(r, x, -88.0, 88.0, ALU.max, ALU.min)
                    ts(ssm_i[:, :], r, 1.0 / math.log(2.0), None, ALU.mult)
                    dve.tensor_copy(n, ssm_i[:, :])
                    dve.drain()
                    stt(r, n, -0.693359375, r, ALU.mult, ALU.add)
                    stt(r, n, 2.12194440e-4, r, ALU.mult, ALU.add)
                    ts(p, r, 1.0 / 5040, None, ALU.mult)
                    for k in (720, 120, 24, 6, 2, 1):
                        stt(p, p, 1.0 / k, r, ALU.add, ALU.mult)
                    ts(p, p, 1.0, None, ALU.add)
                    ts(ssm_i[:, :], n, 127.0, float(1 << 23), ALU.add, ALU.mult)
                    tt(o, p, ssm_i[:, :].bitcast(F32), ALU.mult)

                exp(v(DT_), ldt)
                tt(v(A3), are, v(DT_), ALU.mult)
                exp(v(MAG), v(A3))
                tt(v(TH), aim, v(DT_), ALU.mult)
                ts(ssm_i[:, :], v(TH), 1.0 / (2 * math.pi), None, ALU.mult)
                dve.tensor_copy(v(A0), ssm_i[:, :])
                dve.drain()
                for part in (6.28125, 1.9350051879882812e-3, 3.019916050e-7):
                    stt(v(TH), v(A0), -part, v(TH), ALU.mult, ALU.add)
                ts(v(TH), v(TH), 0.5, None, ALU.mult)
                tt(v(A0), v(TH), v(TH), ALU.mult)
                for o, first in ((A1, 2), (A2, 1)):
                    top = 13 if first == 2 else 14
                    sign = lambda n: -1.0 if (n // 2) % 2 else 1.0
                    ts(v(o), v(A0), sign(top) / math.factorial(top), None, ALU.mult)
                    for n in range(top - 2, first - 1, -2):
                        if n >= 2:
                            stt(v(o), v(o), sign(n) / math.factorial(n), v(A0), ALU.add, ALU.mult)
                    if first == 2:
                        stt(v(o), v(o), 1.0, v(TH), ALU.add, ALU.mult)
                    else:
                        ts(v(o), v(o), 1.0, None, ALU.add)
                stt(v(SI), v(A1), 2.0, v(A2), ALU.mult, ALU.mult)
                tt(v(A3), v(A1), v(A1), ALU.mult)
                ts(v(CO), v(A3), -2.0, 1.0, ALU.mult, ALU.add)
                tt(v(A0), v(MAG), v(CO), ALU.mult)
                ts(v(A0), v(A0), -1.0, None, ALU.add)
                tt(v(A1), v(MAG), v(SI), ALU.mult)
                tt(v(A2), are, are, ALU.mult)
                tt(v(A3), aim, aim, ALU.mult)
                tt(v(A2), v(A2), v(A3), ALU.add)
                dve.reciprocal(v(A2), v(A2))
                dve.drain()
                tt(v(ZR), v(A0), are, ALU.mult)
                tt(v(A3), v(A1), aim, ALU.mult)
                tt(v(ZR), v(ZR), v(A3), ALU.add)
                tt(v(ZR), v(ZR), v(A2), ALU.mult)
                tt(v(ZI), v(A1), are, ALU.mult)
                tt(v(A3), v(A0), aim, ALU.mult)
                tt(v(ZI), v(ZI), v(A3), ALU.subtract)
                tt(v(ZI), v(ZI), v(A2), ALU.mult)
                ts(v(NZR), v(ZR), -1.0, None, ALU.mult)
                ts(v(NZI), v(ZI), -1.0, None, ALU.mult)
                dve.tensor_copy(v(POW), v(CO))
                dve.tensor_copy(v(POW + 1), v(SI))
                dve.drain()
                for k in range(7):
                    c, s = v(POW + 2 * k), v(POW + 2 * k + 1)
                    tt(v(A0), c, c, ALU.mult)
                    tt(v(A1), s, s, ALU.mult)
                    tt(v(POW + 2 * k + 2), v(A0), v(A1), ALU.subtract)
                    stt(v(POW + 2 * k + 3), c, 2.0, s, ALU.mult, ALU.mult)
                return MAG, ZR, ZI, NZR, NZI, POW

            def state_space():
                MAG, ZR, ZI, NZR, NZI, POW = discretize()
                B = STATE_BLOCK
                for n in range(STATE_TILES):
                    b, k = n // B, n % B
                    if k == 0:
                        dve.memset(rot[:, 0, :, 0:1], 1.0)
                        dve.memset(rot[:, 1, :, 0:1], 0.0)
                        dve.drain()
                        for e in range(8):
                            d = 1 << e
                            pc, ps = (ssm[:, POW + 2 * e + i, B * b:B * b + B].unsqueeze(2).to_broadcast([P, B, d])
                                      for i in range(2))
                            c, s = rot[:, 0, :, 0:d], rot[:, 1, :, 0:d]
                            p0, p1 = pr[:, :, 0:d], pr[:, :, P:P + d]
                            dve.tensor_tensor(p0, c, pc, ALU.mult)
                            dve.tensor_tensor(p1, s, ps, ALU.mult)
                            dve.drain()
                            dve.tensor_tensor(rot[:, 0, :, d:2 * d], p0, p1, ALU.subtract)
                            p2, p3 = (x[:, :, :].rearrange("p i (a t) -> p (i a) t", a=2)[:, :, 0:d] for x in (vrot, scn))
                            dve.tensor_tensor(p2, c, ps, ALU.mult)
                            dve.tensor_tensor(p3, s, pc, ALU.mult)
                            dve.drain()
                            dve.tensor_tensor(rot[:, 1, :, d:2 * d], p2, p3, ALU.add)
                            dve.drain()
                    col = lambda i: ssm[:, i, n:n + 1]
                    if n >= 2:
                        dve.wait_ge(x_used, n - 1)
                    if k == 0:
                        dve.wait_ge(bc_landed, 32 * (b + 1))
                    z0, z1 = cz[:, n % 2, 0, :], cz[:, n % 2, 1, :]
                    dve.tensor_scalar(z0, c_pad[:, k, 1, :], col(NZI), None, ALU.mult)
                    dve.tensor_scalar(z1, c_pad[:, k, 1, :], col(NZR), None, ALU.mult)
                    dve.drain()
                    dve.scalar_tensor_tensor(out=z0, in0=c_pad[:, k, 0, :], scalar=col(ZR), in1=z0, op0=ALU.mult, op1=ALU.add)
                    dve.scalar_tensor_tensor(out=z1, in0=c_pad[:, k, 0, :], scalar=col(NZI), in1=z1, op0=ALU.mult, op1=ALU.add)
                    dve.wait_ge(v_ready, n + 1)
                    re, im = ps_a[n % 2][:, 0:TOK], ps_a[n % 2][:, TOK:2 * TOK]
                    c, s = rot[:, 0, k, :], rot[:, 1, k, :]
                    dve.tensor_tensor(pr[:, 0, :], re, c, ALU.mult)
                    dve.tensor_tensor(pr[:, 1, :], im, s, ALU.mult)
                    dve.tensor_tensor(pr[:, 2, :], im, c, ALU.mult)
                    dve.tensor_tensor(pr[:, 3, :], re, s, ALU.mult).then_inc(v_read, 1)
                    dve.drain()
                    dve.tensor_tensor(vrot[:, 0, :], pr[:, 0, :], pr[:, 1, :], ALU.add)
                    dve.tensor_tensor(vrot[:, 1, :], pr[:, 2, :], pr[:, 3, :], ALU.subtract)
                    dve.drain()
                    for i in range(2):
                        dve.tensor_tensor_scan(scn[:, i, :], col(MAG).to_broadcast([P, TOK]), vrot[:, i, :], 0.0,
                                               ALU.mult, ALU.add)
                    dve.drain()
                    dve.tensor_tensor(pr[:, 0, :], scn[:, 0, :], c, ALU.mult)
                    dve.tensor_tensor(pr[:, 1, :], scn[:, 1, :], s, ALU.mult)
                    dve.tensor_tensor(pr[:, 2, :], scn[:, 0, :], s, ALU.mult)
                    dve.tensor_tensor(pr[:, 3, :], scn[:, 1, :], c, ALU.mult)
                    dve.drain()
                    dve.tensor_tensor(xs[:, n % 2, 0, :], pr[:, 0, :], pr[:, 1, :], ALU.subtract)
                    dve.tensor_tensor(xs[:, n % 2, 1, :], pr[:, 2, :], pr[:, 3, :], ALU.add).then_inc(x_ready, 1)
                    if k == B - 1:
                        dve.wait_ge(x_used, n + 1)
                        dve.scalar_tensor_tensor(out=y2[:, b, :], in0=proj2[:, U2 + b, :], scalar=param("ssm_d_2", b),
                                                 in1=ps_o[:, 0:TOK], op0=ALU.mult, op1=ALU.add).then_inc(y_kept, 1)

            def gated_sum(st, proj, gate0, gate1):
                n_pair = len(st.slots) // 2

                def ep(i, s):
                    whole(st, i, s)
                    t = (i * n_pair + s // 2) * 2
                    ps = bank[(st.group0 + s) % 2][:, :].rearrange("p (c t) -> p c t", c=2)
                    g0, g1 = proj[:, bass.ds(gate0 + t, 2), :], proj[:, bass.ds(gate1 + t, 2), :]
                    g = g1 if s % 2 else g0
                    dve.tensor_tensor(g, g, ps, ALU.mult).then_inc(evacuated["dve"], 1)
                    if s % 2:
                        dve.drain()
                        dve.tensor_tensor(g0, g0, g1, ALU.add)
                return ep

            def split_merged(proj, gate0):
                dve.drain()
                for c in range(4):
                    split(proj[:, gate0 + 4 * c:gate0 + 4 * c + 4, :], act_hi[:, 4 * c:4 * c + 4, :],
                          act_lo[:, 4 * c:4 * c + 4, :]).then_inc(split_ready, 1)

            def conv(dst, ps, w, b, tile, half_tiles):
                for c in range(2):
                    x, y = ps[:, c * TOK:(c + 1) * TOK], dst[:, c, :]
                    dve.tensor_scalar(y, x, param_at(w, 2 * half_tiles + tile + c), param_at(b, tile + c), ALU.mult, ALU.add)
                for back in (1, 2):
                    dve.drain()
                    for c in range(2):
                        x, y = ps[:, c * TOK:(c + 1) * TOK - back], dst[:, c, back:]
                        last = dve.scalar_tensor_tensor(out=y, in0=x, scalar=param_at(w, (2 - back) * half_tiles + tile + c),
                                                        in1=y, op0=ALU.mult, op1=ALU.add)
                return last

            def ffn(st, base, w, b, tiles, value_conv):
                def ep(i, s):
                    whole(st, i, s)
                    ps = bank[(st.group0 + s) % 2]
                    if s == 0:
                        conv(gate_y, ps, w, b, 2 * i, tiles).then_inc(evacuated["dve"], 1)
                        return
                    if value_conv:
                        conv(val_y, ps, w, b, 2 * i + FT, tiles).then_inc(evacuated["dve"], 1)
                        dve.drain()
                        dve.wait_ge(gate_act, base + i + 1)
                        dve.tensor_tensor(val_y[:, :, :], val_y[:, :, :], gate_g[:, :, :], ALU.mult)
                    else:
                        dve.wait_ge(gate_act, base + i + 1)
                        dve.tensor_tensor(val_y[:, :, :], gate_g[:, :, :], ps[:, :].rearrange("p (c t) -> p c t", c=2),
                                          ALU.mult).then_inc(evacuated["dve"], 1)
                    dve.drain()
                    split(val_y[:, :, :], f_hi[:, bass.ds(2 * i, 2), :], f_lo[:, bass.ds(2 * i, 2), :]).then_inc(f_ready, 1)
                return ep

            def add_to_residual(st):
                def ep(i, s):
                    whole(st, i, s)
                    h = hT[:, bass.ds((i * len(st.slots) + s) * 2, 2), :]
                    dve.tensor_tensor(h, h, bank[(st.group0 + s) % 2][:, :].rearrange("p (c t) -> p c t", c=2),
                                      ALU.add).then_inc(evacuated["dve"], 1)
                return ep

            def ple(i, s):
                n = i * 2 + s
                dve.wait_ge(evacuated["act"], st_gate.evac0 + n + 1)
                h = hT[:, bass.ds(2 * n, 2), :]
                dve.tensor_tensor(sg[:, :, :], sg[:, :, :], eT[:, bass.ds(2 * n, 2), :], ALU.mult)
                dve.drain()
                dve.tensor_tensor(h, h, sg[:, :, :], ALU.add).then_inc(ple_used, 1)

            dve.memset(small_c[:, 0:1], EPS)
            dve.memset(small_c[:, 1:2], 1.0).then_inc(consts, 1)
            dve.wait_ge(loaded, 64)
            norm_split(0, "g_mix_pre")
            stream(st_in)
            for n, tile in enumerate([VA + h for h in range(HEADS_A)] + [VB + h for h in range(HEADS_B)]):
                dve.wait_ge(v_turned, n + 1)
                dve.tensor_copy(proj1[:, tile, :], ps_t[n % 2][:, 0:TOK]).then_inc(v_kept, 1)
            dilated()
            sticks()
            dve.drain()
            split(proj1[:, QA:QA + 4, :], act_hi[:, 0:4, :], act_lo[:, 0:4, :]).then_inc(split_ready, 1)
            split(proj1[:, QB:QB + 4, :], act_hi[:, 4:8, :], act_lo[:, 4:8, :]).then_inc(split_ready, 1)
            dve.wait_ge(gates_open, 1)
            stream(st_branch, gated_sum(st_branch, proj1, GATE_A, GATE_B))
            split_merged(proj1, GATE_A)
            stream(st_out)
            add_normed(1, mT, "g_mix_post").then_inc(resid_ready, 1)
            norm_split(2, "g_ffn_pre")
            stream(st_up, ffn(st_up, 0, "conv_w", "conv_b", 2 * FT, True))
            dve.drain()
            split(pT[:, :, :], p_hi[:, :, :], p_lo[:, :, :]).then_inc(split_ready, 1)
            stream(st_down)
            stream(st_ple)
            add_normed(3, m2T, "g_ffn_post")
            dve.drain()
            for c in range(4):
                split(hT[:, 4 * c:4 * c + 4, :], act_hi[:, 4 * c:4 * c + 4, :],
                      act_lo[:, 4 * c:4 * c + 4, :]).then_inc(split_ready, 1)
            stream(st_gate, ple)
            norm_split(4, "attn_norm_g_2")
            stream(st_in2)
            stream(st_in2b)
            window()
            dve.drain()
            for c in range(2):
                split(proj2[:, Q2 + 4 * c:Q2 + 4 * c + 4, :], act_hi[:, 4 * c:4 * c + 4, :],
                      act_lo[:, 4 * c:4 * c + 4, :]).then_inc(split_ready, 1)
            state_space()
            dve.wait_ge(y_act, 1)
            split(y2[:, :, :], act_hi[:, 8:12, :], act_lo[:, 8:12, :]).then_inc(split_ready, 1)
            stream(st_glu)
            dve.wait_ge(evacuated["act"], st_glu.evac0 + 4)
            dve.tensor_tensor(glu_v[:, :, :], glu_v[:, :, :], glu_g[:, :, :], ALU.mult)
            dve.drain()
            split(glu_v[:, :, :], act_hi[:, 12:16, :], act_lo[:, 12:16, :]).then_inc(split_ready, 1)
            dve.wait_ge(gates_open, 2)
            stream(st_branch2, gated_sum(st_branch2, proj2, GATE_AT, GATE_SSM))
            split_merged(proj2, GATE_AT)
            stream(st_out2, add_to_residual(st_out2))
            norm_split(5, "ffn_norm_g_2")
            stream(st_up2, ffn(st_up2, 22, "conv_w_2", "conv_b_2", FT, False))
            stream(st_down2, add_to_residual(st_down2))
            root(6)
            for c in range(4):
                for t in range(4):
                    h = hT[:, 4 * c + t, :]
                    last = dve.scalar_tensor_tensor(out=h, in0=h, scalar=param("final_norm_g_2", 4 * c + t),
                                                    in1=rstd[:, :], op0=ALU.mult, op1=ALU.mult)
                last.then_inc(split_ready, 1)

        @block.gpsimd
        def _(pool):
            for b in range(STATE_TILES // STATE_BLOCK):
                if b == 0:
                    pool.wait_ge(o_kept, 16)
                else:
                    pool.wait_ge(x_used, STATE_BLOCK * b)
                pool.dma_start(b_pad[:, :, :, :], a["b_pad"][:, STATE_BLOCK * b:STATE_BLOCK * (b + 1), :, :]).then_inc(bc_landed, 16)
                pool.dma_start(c_pad[:, :, :, :], a["c_pad"][:, STATE_BLOCK * b:STATE_BLOCK * (b + 1), :, :]).then_inc(bc_landed, 16)


def tables():
    t = np.zeros((P, TAB_COLS), np.float32)
    q = np.concatenate([np.arange(P)[:, None] + np.zeros((1, P), int), P + np.arange(P)[:, None] + np.zeros((1, TOK), int)], 1)
    k = np.concatenate([np.arange(P), np.arange(TOK)])[None, :]
    d = q - k

    def put(name, v):
        at, n = TAB[name]
        t[:, at:at + n] = v

    put("dist", d)
    for g, dil in enumerate(DILATIONS):
        put(f"pen{g}", np.where((d >= 0) & (d % dil == 0) & (d <= P * dil), 0, NEG))
    put("penw", np.where((d >= 0) & (d < P), 0, NEG))
    key = np.concatenate([np.zeros(TOK, int), np.full(P, P)])[None, :] + np.arange(P)[:, None]
    qry = np.concatenate([np.arange(TOK), P + np.arange(P)])[None, :]
    put("penb", np.where(key < qry, 0, NEG))
    put("tri", np.arange(P)[:, None] >= np.arange(P)[None, :])
    put("ident", np.eye(P))
    put("ones", 1)
    return t


def params(v):
    t = np.zeros((P, PAR_COLS), np.float32)

    def put(name, x, rows=1):
        at, n = PAR[name]
        t[:, at:at + n] = np.asarray(x).reshape(rows * n // rows, P).T

    for name in PAR:
        if name == "attn_sinks_2":
            at, n = PAR[name]
            t[:, at:at + n] = np.asarray(v[name]).reshape(1, n)
        elif name == "ssm_log_dt_2":
            put(name, np.repeat(np.asarray(v[name]).reshape(-1), HD_2))
        else:
            put(name, v[name])
    return t


def padded(v):
    b = np.zeros((P, STATE_TILES, 2, P), np.float32)
    c = np.zeros((P, STATE_TILES, 2, P), np.float32)
    for i, part in enumerate(("re", "im")):
        vb, vc = np.asarray(v[f"ssm_b_{part}_2"])[0], np.asarray(v[f"ssm_c_{part}_2"])[0]
        for g in range(32):
            ch, st = slice(16 * (g % 8), 16 * (g % 8) + 16), slice(64 * (g % 2), 64 * (g % 2) + 64)
            b[ch, g // 2, i, st] = vb[g].T
            c[st, g // 2, i, ch] = vc[g].T
    return b, c


WEIGHTS = ["w_in", "w_branch_a", "w_branch_b", "w_out", "w_up", "w_down", "w_ple_in", "w_ple_gate",
           "w_in_2", "w_glu_2", "w_branch_attn_2", "w_branch_ssm_2", "w_out_2", "w_up_2", "w_down_2"]


def kernel(**inputs):
    import concourse.bacc as bacc
    from concourse.bass_utils import run_bass_kernel_spmd

    def turned(x, tiles):
        return np.ascontiguousarray(np.asarray(x).reshape(TOK, tiles, P).transpose(2, 1, 0))

    b_pad, c_pad = padded(inputs)
    arrays = {"xT": turned(inputs["x"], DT), "pT": turned(inputs["p"], 2), "tables": tables(),
              "params": params(inputs), "b_pad": b_pad, "c_pad": c_pad}
    for name in WEIGHTS:
        arrays[name] = np.ascontiguousarray(np.asarray(inputs[name])[0])
    nc = bacc.Bacc("TRN2", target_bir_lowering=False, num_devices=1)
    a = {k: nc.dram_tensor(f"in_{k}", v.shape, mybir.dt.from_np(v.dtype), kind="ExternalInput").ap()
         for k, v in arrays.items()}
    out = nc.dram_tensor("out_T", (P, DT, TOK), F32, kind="ExternalOutput").ap()
    build(nc, a, out)
    r = run_bass_kernel_spmd(nc, [{f"in_{k}": v for k, v in arrays.items()}], core_ids=[0])
    got = r.results[0]["out_T"]
    return np.ascontiguousarray(got.transpose(2, 1, 0)).reshape(1, TOK, D)
```

```python
import math
from contextlib import ExitStack

import numpy as np
import concourse.bass as bass
from concourse import mybir

F32 = mybir.dt.float32
F32R = mybir.dt.float32r
I32 = mybir.dt.int32
ALU = mybir.AluOpType
ACT = mybir.ActivationFunctionType
AX = mybir.AxisListType

P = 128
TOK = 256
D = 2048
DT = D // P
FF = 5632
FT = FF // P
EPS = 1e-6
NEG = -1e30

PIECE_KT = 4
GROUP = 256
RING = 4

SLOTS, DILATIONS = 4, (1, 4, 16)
QA, KA, VA, QB, KB, VB, GATE_A, GATE_B = 0, 12, 24, 36, 40, 44, 48, 64
HEADS_A, HEADS_B = 12, 4
HEADS_2, KV_2, HD_2 = 16, 2, 64
Q2, K2, V2, U2, GATE_AT, GATE_SSM, PROJ2 = 0, 8, 9, 10, 14, 30, 46
STATE_TILES, STATE_BLOCK, STATE_RING = 16, 4, 4

ORDER_2 = [U2, U2 + 2, K2] + list(range(Q2, K2, 2)) + list(range(GATE_AT, PROJ2, 2))

LEAD = 4
at_unit = lambda u: 8 + 4 * u
at_stick = lambda h: 43 + 6 * h
at_state = lambda n: 11 + 4 * n
at_head = lambda h: 24 + 3 * h


def which(place, count, n):
    return [u for u in range(count) if place(u) == n]


BLK = 384
TAB = {"pen0": (0, BLK), "pen1": (BLK, BLK), "pen2": (2 * BLK, BLK), "penb": (3 * BLK, BLK),
       "dist": (4 * BLK, BLK), "penw": (5 * BLK, BLK),
       "tri": (6 * BLK, P), "ident": (6 * BLK + P, P), "ones": (6 * BLK + 2 * P, P)}
TAB_COLS = 6 * BLK + 3 * P

PAR, _at = {}, 0
for _name, _n in (("g_mix_pre", 16), ("g_mix_post", 16), ("g_ffn_pre", 16), ("g_ffn_post", 16),
                  ("attn_norm_g_2", 16), ("ffn_norm_g_2", 16), ("final_norm_g_2", 16),
                  ("conv_w", 3 * 88), ("conv_b", 88), ("conv_w_2", 3 * 44), ("conv_b_2", 44),
                  ("b_in_2", 46), ("b_glu_2", 8), ("ssm_d_2", 4), ("attn_sinks_2", 16),
                  ("ssm_a_re_2", 16), ("ssm_a_im_2", 16), ("ssm_log_dt_2", 16)):
    PAR[_name] = (_at, _n)
    _at += _n
PAR_COLS = _at


class Stage:

    def __init__(self, name, slots, bodies, x, x_ready, evac):
        self.name, self.slots, self.bodies = name, slots, bodies
        self.x, self.x_ready, self.evac = x, x_ready, evac
        self.pieces = [-(-kt // PIECE_KT) for _, _, kt, _ in slots]
        self.ppb = sum(self.pieces)
        assert self.ppb % RING == 0


def place(stages):
    piece = group = 0
    done = {"act": 0, "dve": 0}
    owner = []
    for st in stages:
        st.piece0, st.group0, st.evac0 = piece, group, done[st.evac]
        n = st.bodies * len(st.slots)
        for _ in range(n):
            done[st.evac] += 1
            owner.append((st.evac, done[st.evac]))
        piece += st.bodies * st.ppb
        group += n
    for st in stages:
        st.owner = owner
    return piece, group


def build(nc, a, out):
    with ExitStack() as ctx:
        def sb(name, shape, dt=F32, scope=ctx):
            return scope.enter_context(nc.sbuf_tensor(name, shape, dt))

        def sem(name):
            return ctx.enter_context(nc.semaphore(name))

        hT = sb("hT", [P, DT, TOK])
        with ExitStack() as scope:
            m2T = sb("m2T", [P, DT, TOK], scope=scope)
        act_hi = sb("act_hi", [P, DT, TOK], F32R)
        act_lo = sb("act_lo", [P, DT, TOK], F32R)
        w_raw = sb("w_raw", [P, RING, PIECE_KT, GROUP])
        w_hi = sb("w_hi", [P, RING, PIECE_KT, GROUP], F32R)
        w_lo = sb("w_lo", [P, RING, PIECE_KT, GROUP], F32R)
        tab = sb("tab", [P, TAB_COLS])
        par = sb("par", [P, PAR_COLS])
        pT = sb("pT", [P, 2, TOK])
        rstd = sb("rstd", [P, TOK])
        small_c = sb("small_c", [P, 2])
        half_b = sb("half_b", [P, PROJ2 - GATE_AT])
        half_bias = lambda j: half_b[:, j:j + 1]
        eps, one = small_c[:, 0:1], small_c[:, 1:2]

        def table(name):
            at, n = TAB[name]
            return tab[:, at:at + n]

        def param(name, j):
            return par[:, PAR[name][0] + j:PAR[name][0] + j + 1]

        def param_at(name, j):
            return par[:, bass.ds(PAR[name][0] + j, 1)]

        ident, ones, tri = table("ident"), table("ones"), table("tri")

        def over(kept, *buffers):
            with ExitStack() as scope:
                if kept:
                    sb(f"skip{len(names)}", [P, kept], scope=scope)
                names.append(kept)
                return [sb(*b, scope=scope) for b in buffers]

        names = []
        T = TOK
        proj1, s_buf, pT_buf, bias_t, small = over(
            0, ("proj1", [P, 80, T]), ("s_buf", [P, 2, 3 * T]), ("pT_buf", [P, 3 * T]), ("bias_t", [P, 3 * T]),
            ("small", [P, 32]))
        z_b, t_b, l_b, sp_b, lw_b = over(80 * T, *((n, [P, BLK]) for n in ("z_b", "t_b", "l_b", "sp_b", "lw_b")))
        y_hi, y_lo = over(KA * T, ("y_hi", [P, 8, T], F32R), ("y_lo", [P, 8, T], F32R))
        mT, eT, tmp, sg, sq_x = over(
            0, ("mT", [P, DT, T]), ("eT", [P, DT, T]), ("tmp", [P, 2, 4, T]), ("sg", [P, 2, T]), ("sq_x", [P, 6, T]))
        sq_t = tab[:, 0:6 * T].rearrange("p (k t) -> p k t", k=6)
        squares_of = lambda n: sq_t if n else sq_x[:, :, :]
        sq_slot = lambda n, k: squares_of(n)[:, 2 * k:2 * k + 2, :]
        sq_sum = lambda n: squares_of(n)[:, 4:6, :]
        f_hi, f_lo, gate_y, gate_g, val_y = over(
            0, ("f_hi", [P, FT, T], F32R), ("f_lo", [P, FT, T], F32R), ("gate_y", [P, 2, T]), ("gate_g", [P, 2, T]),
            ("val_y", [P, 2, T]))
        p_hi, p_lo = over(2 * FT * T, ("p_hi", [P, 2, T], F32R), ("p_lo", [P, 2, T], F32R))
        proj2, kpad, vpad, s2_buf, small2, bc_pad, cz, rot, vrot, scn, xs, pr, ssm, ssm_i = over(
            0, ("proj2", [P, PROJ2, T]), ("kpad", [P, KV_2, 2, T]), ("vpad", [P, KV_2, 2, 2, P]),
            ("s2_buf", [P, 2, BLK]), ("small2", [P, 32]), ("bc_pad", [P, STATE_RING, 4, P]), ("cz", [P, 2, 2, P]),
            ("rot", [P, STATE_RING, 2, T]), ("vrot", [P, 2, T]), ("scn", [P, 2, T]), ("xs", [P, 2, 2, T]),
            ("pr", [P, 4, T]), ("ssm", [P, 30, STATE_TILES]), ("ssm_i", [P, STATE_TILES], I32))
        pT2_buf, bias2_t = tab[:, 0:BLK], tab[:, BLK:2 * BLK]
        vtok = tab[:, 2 * BLK:2 * BLK + T].rearrange("p (k c) -> p k c", k=2)
        turn_t = tab[:, 2 * BLK + T:2 * BLK + 3 * T].rearrange("p (k t) -> p k t", k=4)
        x2_hi, x2_lo, glu_v, glu_g = over(
            PROJ2 * T, ("x2_hi", [P, 16, T], F32R), ("x2_lo", [P, 16, T], F32R), ("glu_v", [P, 4, T]), ("glu_g", [P, 4, T]))

        bank = [ctx.enter_context(nc.psum_tensor(f"bank{i}", [P, 512], F32)) for i in range(2)]
        ps_a = [ctx.enter_context(nc.psum_tensor(f"ps_a{i}", [P, 512], F32)) for i in range(2)]
        ps_t = [ctx.enter_context(nc.psum_tensor(f"ps_t{i}", [P, 512], F32)) for i in range(2)]
        ps_o = ctx.enter_context(nc.psum_tensor("ps_o", [P, 512], F32))
        ps_n = ctx.enter_context(nc.psum_tensor("ps_n", [P, 512], F32))

        loaded = sem("loaded")
        raw_landed = [sem(f"raw_landed{i}") for i in range(RING)]
        slots_freed = sem("slots_freed")
        hi_ready, lo_ready = sem("hi_ready"), sem("lo_ready")
        piece_used = sem("piece_used")
        evacuated = {"act": sem("evac_act"), "dve": sem("evac_dve")}
        split_ready = sem("split_ready")
        f_ready = sem("f_ready")
        consts, halved = sem("consts"), sem("halved")
        resid_ready = sem("resid_ready")
        sq_ready, sq_used = sem("sq_ready"), sem("sq_used")
        sum_ready, std_ready = sem("sum_ready"), sem("std_ready")
        gate_act = sem("gate_act")
        gates_open = sem("gates_open")
        biased_ready = sem("biased_ready")
        v_turned, v_kept = sem("v_turned"), sem("v_kept")
        sc_ready, sc_read, s_max = sem("sc_ready"), sem("sc_read"), sem("s_max")
        p_exp, p_norm, p_turned, pt_kept = sem("p_exp"), sem("p_norm"), sem("p_turned"), sem("pt_kept")
        o_ready, o_kept = sem("o_ready"), sem("o_kept")
        zb_ready, zb_abs, zb_log = sem("zb_ready"), sem("zb_abs"), sem("zb_log")
        sp_ready, cum_ready, lw_ready, w_ready = sem("sp_ready"), sem("cum_ready"), sem("lw_ready"), sem("w_ready")
        ob_ready, ob_kept = sem("ob_ready"), sem("ob_kept")
        pad_ready, bc_landed = sem("pad_ready"), [sem(f"bc_landed{i}") for i in range(STATE_RING)]
        powers_ready, rot_ready = sem("powers_ready"), sem("rot_ready")
        v_ready, v_read, x_ready, x_used = sem("v_ready"), sem("v_read"), sem("x_ready"), sem("x_used")
        y_kept, y_act, ple_used = sem("y_kept"), sem("y_act"), sem("ple_used")
        stored = sem("stored")

        def cols(w, kt, x0, step, at=0):
            return (a[w].rearrange("(t p) n -> p t n", p=P), lambda i: i * step + at, kt, x0)

        def main_x(first):
            return lambda j: (split_ready, first + j + 1)

        act_x, f_x, p_x = (act_hi, act_lo), (f_hi, f_lo), (p_hi, p_lo)
        G = GROUP
        SPLIT = {}
        at = 0
        for name, n in (("mix", 4), ("y1", 2), ("merged", 4), ("ffn", 4), ("ple_in", 1), ("ple_gate", 4),
                        ("mix2", 4), ("ssm_y", 1), ("attn2", 2), ("ssm", 1), ("merged2", 4), ("ffn2", 4)):
            SPLIT[name] = at
            at += n
        tiles = lambda w, ts: [cols(w, 16, 0, 0, t * P) for t in ts]
        branch1 = [s for k in range(2) for s in
                   (cols("w_branch_a", 4, 0, 2 * G, k * G), cols("w_branch_b", 4, 4, 2 * G, k * G))]
        branch2 = [s for k in range(4) for s in
                   (cols("w_branch_attn_2", 8, 0, 4 * G, k * G), cols("w_branch_ssm_2", 4, 12, 4 * G, k * G))]
        pair = lambda w: [cols(w, 16, 0, 2 * G), cols(w, 16, 0, 2 * G, G)]
        quad = lambda w, kt: [cols(w, kt, 0, 4 * G, k * G) for k in range(4)]
        st_in = Stage("in", pair("w_in"), QB // 4, act_x, main_x(SPLIT["mix"]), "dve")
        st_mix = Stage("mix", tiles("w_in", range(QB, QB + 36, 2)), 1, act_x, None, "dve")
        st_rest = Stage("rest", [cols("w_in", 16, 0, 2 * G, (QB + 36) * P), cols("w_in", 16, 0, 2 * G, (QB + 38) * P)],
                        2, act_x, None, "dve")
        st_branch = Stage("branch", branch1, 4, (y_hi, y_lo), lambda j: (split_ready, SPLIT["y1"] + 2), "dve")
        st_out = Stage("out", pair("w_out"), 4, act_x, main_x(SPLIT["merged"]), "act")
        st_up = Stage("up", [cols("w_up", 16, 0, G), cols("w_up", 16, 0, G, FF)], 22, act_x,
                      main_x(SPLIT["ffn"]), "dve")
        st_down = Stage("down", quad("w_down", FT), 2, f_x, lambda j: (f_ready, 2 * j + 2), "act")
        st_ple = Stage("ple", quad("w_ple_in", 2), 2, p_x, main_x(SPLIT["ple_in"]), "act")
        st_gate = Stage("ple_gate", pair("w_ple_gate"), 4, act_x, main_x(SPLIT["ple_gate"]), "act")
        st_in2 = Stage("in2", tiles("w_in_2", ORDER_2[:20]), 1, act_x, main_x(SPLIT["mix2"]), "dve")
        st_in2b = Stage("in2b", tiles("w_in_2", ORDER_2[20:21]), 1, act_x, None, "dve")
        st_glu = Stage("glu", [cols("w_glu_2", 4, 8, 0, k * G) for k in range(4)], 1, (x2_hi, x2_lo),
                       lambda j: (split_ready, SPLIT["ssm_y"] + 1), "act")
        st_in2c = Stage("in2c", tiles("w_in_2", ORDER_2[21:]), 1, act_x, None, "dve")
        st_branch2 = Stage("branch2", branch2, 2, (x2_hi, x2_lo), lambda j: (split_ready, SPLIT["ssm"] + 1), "dve")
        st_out2 = Stage("out2", pair("w_out_2"), 4, act_x, main_x(SPLIT["merged2"]), "dve")
        st_up2 = Stage("up2", [cols("w_up_2", 16, 0, G, FF), cols("w_up_2", 16, 0, G)], 22, act_x,
                       main_x(SPLIT["ffn2"]), "dve")
        st_down2 = Stage("down2", quad("w_down_2", FT), 2, f_x, lambda j: (f_ready, 22 + 2 * j + 2), "dve")
        stages = [st_in, st_mix, st_rest, st_branch, st_out, st_up, st_down, st_ple, st_gate,
                  st_in2, st_in2b, st_glu, st_in2c, st_branch2, st_out2, st_up2, st_down2]
        place(stages)

        def bodies(eng, st, body):
            body(0, True)
            if st.bodies > 1:
                with eng.Fori(1, st.bodies) as i:
                    body(i, False)

        def with_epilogue(eng, st, piece, epilogue, beside=None):
            n = len(st.slots)

            def body(i, first):
                j0 = 0
                for s in range(n):
                    for j in range(st.pieces[s]):
                        piece(i, j0 + j, s)
                        if first and beside:
                            beside(j0 + j)
                        if j == min(3, st.pieces[s] - 1) and epilogue and not (first and s == 0):
                            epilogue(i if s else i - 1, (s - 1) % n)
                    j0 += st.pieces[s]

            bodies(eng, st, body)
            if epilogue:
                epilogue(st.bodies - 1, n - 1)

        block = ctx.enter_context(nc.Block())

        @block.sync
        def _(sp):
            sp.dma_start(tab[:, :], a["tables"]).then_inc(loaded, 16)
            sp.dma_start(par[:, :], a["params"]).then_inc(loaded, 16)
            for st in stages:
                def states(n):
                    for m in which(lambda m: max(at_state(m) - 2, 0) if m >= STATE_RING else 2 + m, STATE_TILES, n):
                        if m >= STATE_RING:
                            sp.wait_ge(x_used, m - STATE_RING + 1)
                        else:
                            sp.wait_ge(ple_used, 8)
                        sp.dma_start(bc_pad[:, m % STATE_RING, :, :], a["bc_pad"][:, m, :, :]
                                     ).then_inc(bc_landed[m % STATE_RING], 16)

                def body(i, first, st=st):
                    j0 = 0
                    at_col = [col(i) if first else sp.snap(col(i)) for _, col, _, _ in st.slots]
                    for s, (w, _, kt, _) in enumerate(st.slots):
                        c = at_col[s]
                        for j in range(st.pieces[s]):
                            q = st.piece0 + i * st.ppb + j0 + j
                            k = (j0 + j) % RING
                            n = min(PIECE_KT, kt - j * PIECE_KT)
                            if not (first and st.piece0 + j0 + j < RING):
                                sp.wait_ge(lo_ready, q - RING + 1)
                                sp.sem_inc(slots_freed, 1)
                            sp.dma_start(w_raw[:, k, 0:n, :], w[:, j * PIECE_KT:j * PIECE_KT + n, bass.ds(c, GROUP)]
                                         ).then_inc(raw_landed[k], 16)
                            if st is st_in2:
                                states(j0 + j)
                        j0 += st.pieces[s]
                bodies(sp, st, body)
            for c in range(4):
                sp.wait_ge(split_ready, at + c + 1)
                sp.dma_start(out[:, 4 * c:4 * c + 4, :], hT[:, 4 * c:4 * c + 4, :]).then_inc(stored, 16)
            sp.wait_ge(stored, 64)

        @block.tensor
        def _(pe):
            def mm(o, l, r, start, stop):
                return pe.matmul(o, l, r, start=start, stop=stop, skip_group_check=True)

            def stream(st, beside=None):
                xh, xl = st.x

                def body(i, first):
                    j0 = 0
                    for s, (_, _, kt, x0) in enumerate(st.slots):
                        g_in = st.group0 + s if first else None
                        ps = bank[(st.group0 + s) % 2]
                        if first and g_in >= 2:
                            eng, n = st.owner[g_in - 2]
                            pe.wait_ge(evacuated[eng], n)
                        elif not first:
                            pe.wait_ge(evacuated[st.evac], st.evac0 + i * len(st.slots) + s - 1)
                        for j in range(st.pieces[s]):
                            q = st.piece0 + i * st.ppb + j0 + j
                            k = (j0 + j) % RING
                            n = min(PIECE_KT, kt - j * PIECE_KT)
                            if first and s == 0 and st.x_ready:
                                pe.wait_ge(*st.x_ready(j))
                            pe.wait_ge(hi_ready, q + 1)
                            for t in range(n):
                                x = x0 + j * PIECE_KT + t
                                for c in range(2):
                                    o = ps[:, c * TOK:(c + 1) * TOK]
                                    w = w_hi[:, k, t, c * P:(c + 1) * P]
                                    mm(o, w, xh[:, x, :], j == 0 and t == 0 and c == 0, False)
                                    mm(o, w, xl[:, x, :], False, False)
                            pe.wait_ge(lo_ready, q + 1)
                            for t in range(n):
                                x = x0 + j * PIECE_KT + t
                                for c in range(2):
                                    last = mm(ps[:, c * TOK:(c + 1) * TOK], w_lo[:, k, t, c * P:(c + 1) * P],
                                              xh[:, x, :], False, j == st.pieces[s] - 1 and t == n - 1)
                            last.then_inc(piece_used, 1)
                            if first and beside:
                                beside(j0 + j)
                        j0 += st.pieces[s]
                bodies(pe, st, body)

            def sum_squares(n):
                pe.wait_ge(sq_used, 8 * (n + 1))
                mm(ps_n[:, 0:TOK], ones, sq_sum(n)[:, 0, :], True, False)
                mm(ps_n[:, 0:TOK], ones, sq_sum(n)[:, 1, :], False, True).then_inc(sum_ready, 1)

            def sums_beside(n):
                return lambda piece: sum_squares(n) if piece == 3 else None

            def turn_values(n):
                tile = (VA + 2 * n) if n < HEADS_A // 2 else VB + 2 * n - HEADS_A
                if n >= 2:
                    pe.wait_ge(v_kept, n - 1)
                for t in range(4):
                    last = pe.transpose(ps_t[n % 2][:, t * P:(t + 1) * P],
                                        proj1[:, tile + t // 2, (t % 2) * P:(t % 2) * P + P], ident)
                last.then_inc(v_turned, 1)

            def mixer_1(n):
                if n == 4:
                    pe.wait_ge(evacuated["dve"], st_mix.evac0)
                if n in (4, 5, 6):
                    turn_values(2 * n - 8)
                    turn_values(2 * n - 7)
                for u in which(at_unit, 8, n):
                    h, qt = u // 2, u % 2
                    if u:
                        pe.wait_ge(sc_read, u)
                    keys = P * (qt + 1)
                    for g in range(3):
                        o = ps_a[g // 2][:, (g % 2) * keys:(g % 2) * keys + keys]
                        last = mm(o, proj1[:, QA + 4 * g + h, qt * P:qt * P + P],
                                  proj1[:, KA + 4 * g + h, 0:keys], g != 1, g != 0)
                    last.then_inc(sc_ready, 1)
                for u in which(lambda u: at_unit(u) + 3, 8, n):
                    pe.wait_ge(p_norm, u + 1)
                    if u == 0:
                        pe.wait_ge(v_kept, 6)
                    for b in range(3 * (u % 2 + 1)):
                        last = pe.transpose(ps_t[b // 4][:, (b % 4) * P:(b % 4) * P + P],
                                            s_buf[:, u % 2, b * P:(b + 1) * P], ident)
                    last.then_inc(p_turned, 1)
                for u in which(lambda u: at_unit(u) + 5, 8, n):
                    h, qt = u // 2, u % 2
                    pe.wait_ge(pt_kept, u + 1)
                    if u:
                        pe.wait_ge(o_kept, u)
                    for b in range(3 * (qt + 1)):
                        g, kt = b // (qt + 1), b % (qt + 1)
                        last = mm(ps_o[:, 0:P], proj1[:, VA + 4 * g + h, kt * P:kt * P + P],
                                  pT_buf[:, b * P:(b + 1) * P], b == 0, b == 3 * (qt + 1) - 1)
                    last.then_inc(o_ready, 1)
                if n == at_stick(0) - 1:
                    pe.wait_ge(pt_kept, 8)
                    turn_values(6)
                    turn_values(7)
                for h in which(at_stick, HEADS_B, n):
                    if h == 0:
                        pe.wait_ge(sc_read, 8)
                        pe.wait_ge(v_kept, 8)
                    q, k = proj1[:, QB + h, :], proj1[:, KB + h, :]
                    mm(ps_a[0][:, 0:TOK], k[:, 0:P], q, True, True)
                    mm(ps_a[0][:, TOK:BLK], k[:, P:TOK], q[:, P:TOK], False, True).then_inc(zb_ready, 1)
                for h in which(lambda h: at_stick(h) + 3, HEADS_B, n):
                    pe.wait_ge(sp_ready, h + 1)
                    mm(ps_t[0][:, 0:TOK], tri, sp_b[:, 0:TOK], True, False)
                    mm(ps_t[0][:, P:TOK], ones, sp_b[:, TOK:BLK], False, True)
                    mm(ps_t[0][:, TOK:BLK], tri, sp_b[:, TOK:BLK], False, True).then_inc(cum_ready, 1)
                for h in which(lambda h: at_stick(h) + 5, HEADS_B, n):
                    pe.wait_ge(w_ready, h + 1)
                    if h == 0:
                        pe.wait_ge(o_kept, 8)
                    else:
                        pe.wait_ge(ob_kept, h)
                    v = proj1[:, VB + h, :]
                    mm(ps_o[:, 0:TOK], v[:, 0:P], t_b[:, 0:TOK], True, False)
                    mm(ps_o[:, P:TOK], v[:, P:TOK], t_b[:, TOK:BLK], False, True).then_inc(ob_ready, 1)

            def mixer_2(n):
                if n == 3:
                    sum_squares(4)
                for m in which(at_state, STATE_TILES, n):
                    if m == 0:
                        pe.wait_ge(biased_ready, 2)
                    pe.wait_ge(bc_landed[m % STATE_RING], 16 * (m // STATE_RING + 1))
                    if m >= 2:
                        pe.wait_ge(v_read, m - 1)
                    u = proj2[:, U2 + m // STATE_BLOCK, :]
                    mm(ps_a[m % 2][:, 0:TOK], bc_pad[:, m % STATE_RING, 0, :], u, True, True)
                    mm(ps_a[m % 2][:, TOK:], bc_pad[:, m % STATE_RING, 1, :], u, False, True).then_inc(v_ready, 1)
                for m in which(lambda m: at_state(m) + 3, STATE_TILES, n):
                    k = m % STATE_BLOCK
                    if k == 0 and m:
                        pe.wait_ge(y_kept, m // STATE_BLOCK)
                    pe.wait_ge(x_ready, m + 1)
                    mm(ps_o[:, 0:TOK], cz[:, m % 2, 0, :], xs[:, m % 2, 0, :], k == 0, False)
                    mm(ps_o[:, 0:TOK], cz[:, m % 2, 1, :], xs[:, m % 2, 1, :], False, k == 3).then_inc(x_used, 1)
                if n == at_head(0) - 4:
                    pe.wait_ge(biased_ready, 3)
                    for t in range(2):
                        last = pe.transpose(ps_t[0][:, t * P:(t + 1) * P], proj2[:, V2, t * P:(t + 1) * P], ident)
                    last.then_inc(v_turned, 1)
                for h in which(at_head, HEADS_2, n):
                    if h == 0:
                        pe.wait_ge(pad_ready, 1)
                    else:
                        pe.wait_ge(sc_read, 8 + h)
                    pe.wait_ge(biased_ready, 4 + h // 4)
                    j, half = h // (HEADS_2 // KV_2), h % 2
                    q, k = proj2[:, Q2 + h // 2, :], kpad[:, j, half, :]
                    mm(ps_t[0][:, 0:P], q[:, 0:P], k[:, 0:P], True, True)
                    mm(ps_t[0][:, P:BLK], q[:, P:TOK], k, False, True).then_inc(sc_ready, 1)
                for h in which(lambda h: at_head(h) + 3, HEADS_2, n):
                    pe.wait_ge(p_norm, 8 + h + 1)
                    for b in range(3):
                        last = pe.transpose(ps_t[1][:, b * P:(b + 1) * P], s2_buf[:, h % 2, b * P:(b + 1) * P], ident)
                    last.then_inc(p_turned, 1)
                for h in which(lambda h: at_head(h) + 5, HEADS_2, n):
                    j, half = h // (HEADS_2 // KV_2), h % 2
                    pe.wait_ge(pt_kept, 8 + h + 1)
                    if half == 0 and h:
                        pe.wait_ge(o_kept, 8 + h // 2)
                    mm(ps_n[:, 0:P], vpad[:, j, half, 0, :], pT2_buf[:, 0:P], half == 0, half == 1)
                    mm(ps_n[:, P:TOK], vpad[:, j, half, 0, :], pT2_buf[:, P:2 * P], False, False)
                    last = mm(ps_n[:, P:TOK], vpad[:, j, half, 1, :], pT2_buf[:, 2 * P:BLK], False, half == 1)
                    if half:
                        last.then_inc(o_ready, 1)

            pe.wait_ge(loaded, 64)
            stream(st_in, sums_beside(0))
            stream(st_mix, mixer_1)
            stream(st_rest)
            stream(st_branch)
            stream(st_out)
            sum_squares(1)
            stream(st_up, sums_beside(2))
            stream(st_down)
            stream(st_ple)
            sum_squares(3)
            stream(st_gate)
            stream(st_in2, mixer_2)
            stream(st_in2b)
            stream(st_glu)
            stream(st_in2c)
            stream(st_branch2)
            stream(st_out2)
            stream(st_up2, sums_beside(5))
            stream(st_down2)
            sum_squares(6)

        @block.scalar
        def _(act):
            def stream(st, epilogue=None, beside=None):
                def hi(i, j, s):
                    q = st.piece0 + i * st.ppb + j
                    k = j % RING
                    n = min(PIECE_KT, st.slots[s][2])
                    act.wait_ge(raw_landed[k], 16 * (st.piece0 // RING + j // RING + 1) + i * (16 * st.ppb // RING))
                    if not (isinstance(i, int) and q < RING):
                        act.wait_ge(piece_used, q - RING + 1)
                    act.activation(w_hi[:, k, 0:n, :], w_raw[:, k, 0:n, :], ACT.Copy).then_inc(hi_ready, 1)
                with_epilogue(act, st, hi, epilogue, beside)

            def whole(st, i, s):
                act.wait_ge(piece_used, st.piece0 + i * st.ppb + sum(st.pieces[:s + 1]))

            def square(n, j, k, src):
                if not (n == 0 and isinstance(j, int) and j < 2):
                    act.wait_ge(sq_used, 8 * n + j - 1)
                act.activation(sq_slot(n, k), src, ACT.Square).then_inc(sq_ready, 1)

            def copy_to(st, dst, norm=None):
                def ep(i, s):
                    whole(st, i, s)
                    pair = i * len(st.slots) + s
                    ps = bank[(st.group0 + s) % 2][:, :].rearrange("p (c t) -> p c t", c=2)
                    if norm is not None:
                        square(norm, pair, s % 2, ps)
                    act.activation(dst[:, bass.ds(2 * pair, 2), :], ps, ACT.Copy).then_inc(evacuated["act"], 1)
                return ep

            def square_residual(st, n, done, done0):
                def ep(i, s):
                    pair = i * len(st.slots) + s
                    act.wait_ge(done, done0 + pair + 1)
                    square(n, pair, s % 2, hT[:, bass.ds(2 * pair, 2), :])
                return ep

            def root(n):
                act.wait_ge(sum_ready, n + 1)
                act.activation(rstd[:, :], ps_n[:, 0:TOK], ACT.Sqrt, bias=eps[:, 0:1],
                               scale=1.0 / D).then_inc(std_ready, 1)

            def norm_beside(n, squared):
                def beside(piece):
                    if not squared and piece < 4:
                        if n == 2:
                            act.wait_ge(resid_ready, piece + 1)
                        for j in (2 * piece, 2 * piece + 1):
                            square(n, j, j % 2, hT[:, 2 * j:2 * j + 2, :])
                    if piece == 7:
                        root(n)
                return beside

            def open_gates(st):
                def ep(i, s):
                    n = (st.group0 - st_mix.group0) + i * len(st.slots) + s
                    if st is st_mix and s < 6:
                        return
                    act.wait_ge(evacuated["dve"], st_mix.evac0 + n + 1)
                    x = proj1[:, bass.ds(QB + 2 * n, 2), :]
                    act.activation(x, x, ACT.Tanh, scale=0.5).then_inc(gates_open, 1)
                return ep

            def add_bias(st):
                def ep(i, s):
                    tile = ORDER_2[{st_in2: 0, st_in2b: 20, st_in2c: 21}[st] + s]
                    gate = tile >= GATE_AT
                    act.wait_ge(evacuated["dve"], st.evac0 + s + 1)
                    for c in range(2):
                        x = proj2[:, tile + c, :]
                        if gate:
                            last = act.activation(x, x, ACT.Tanh, scale=0.5, bias=half_bias(tile + c - GATE_AT))
                        else:
                            last = act.activation(x, x, ACT.Identity, bias=param("b_in_2", tile + c))
                    last.then_inc(biased_ready, 1)
                return ep

            def mixer_1(n):
                for u in which(lambda u: at_unit(u) + LEAD + 1, 8, n):
                    k = 3 * P * (u % 2 + 1)
                    act.wait_ge(s_max, u + 1)
                    act.activation(s_buf[:, u % 2, 0:k], s_buf[:, u % 2, 0:k], ACT.Exp,
                                   bias=small[:, 8 + u % 2:9 + u % 2],
                                   accum_out=small[:, 16 + u % 2:17 + u % 2]).then_inc(p_exp, 1)
                for h in which(lambda h: at_stick(h) + LEAD + 1, HEADS_B, n):
                    act.wait_ge(zb_abs, h + 1)
                    act.activation(l_b[:, :], t_b[:, :], ACT.Exp, scale=-1.0)
                    act.drain()
                    act.activation(l_b[:, :], l_b[:, :], ACT.Ln, bias=one[:, 0:1]).then_inc(zb_log, 1)
                for h in which(lambda h: at_stick(h) + LEAD + 4, HEADS_B, n):
                    act.wait_ge(lw_ready, h + 1)
                    act.activation(t_b[:, :], lw_b[:, :], ACT.Exp).then_inc(w_ready, 1)

            def mixer_2(n):
                if n == 7:
                    root(4)
                for h in which(lambda h: at_head(h) + LEAD + 1, HEADS_2, n):
                    act.wait_ge(s_max, 8 + h + 1)
                    b = s2_buf[:, h % 2, :]
                    o = 16 * (h % 2)
                    act.activation(small2[:, o + 4:o + 6], small2[:, o:o + 2], ACT.Exp, bias=param("attn_sinks_2", h))
                    act.activation(b[:, 0:P], b[:, 0:P], ACT.Exp, bias=small2[:, o:o + 1],
                                   accum_out=small2[:, o + 2:o + 3])
                    act.activation(b[:, P:BLK], b[:, P:BLK], ACT.Exp, bias=small2[:, o + 1:o + 2],
                                   accum_out=small2[:, o + 3:o + 4]).then_inc(p_exp, 1)

            def gelu_gate(st, base, func):
                def ep(i, s):
                    if s == 0:
                        return
                    act.wait_ge(evacuated["dve"], st.evac0 + 2 * i + 1)
                    if not (isinstance(i, int) and base + i == 0):
                        act.wait_ge(f_ready, base + i)
                    act.activation(gate_g[:, :, :], gate_y[:, :, :], func).then_inc(gate_act, 1)
                return ep

            act.dma_start(hT[:, :, :], a["xT"]).then_inc(loaded, 16)
            act.dma_start(pT[:, :, :], a["pT"]).then_inc(loaded, 16)
            act.wait_ge(loaded, 64)
            act.wait_ge(consts, 1)
            stream(st_in, None, norm_beside(0, False))
            stream(st_mix, open_gates(st_mix), mixer_1)
            stream(st_rest, open_gates(st_rest))
            stream(st_branch)
            stream(st_out, copy_to(st_out, mT, 1))
            root(1)
            stream(st_up, gelu_gate(st_up, 0, ACT.Gelu_apprx_tanh), norm_beside(2, False))
            stream(st_down, copy_to(st_down, m2T, 3))
            stream(st_ple, copy_to(st_ple, eT))
            root(3)

            def ple(i, s):
                whole(st_gate, i, s)
                n = i * 2 + s
                if not (isinstance(i, int) and n == 0):
                    act.wait_ge(ple_used, n)
                act.activation(sg[:, :, :], bank[(st_gate.group0 + s) % 2][:, :].rearrange("p (c t) -> p c t", c=2),
                               ACT.Sigmoid).then_inc(evacuated["act"], 1)
                if s or not isinstance(i, int) or i:
                    square(4, n - 1, (s - 1) % 2, hT[:, bass.ds(2 * n - 2, 2), :])

            stream(st_gate, ple)
            act.wait_ge(ple_used, 8)
            square(4, 7, 1, hT[:, 14:16, :])
            act.wait_ge(halved, 1)
            stream(st_in2, add_bias(st_in2), mixer_2)
            stream(st_in2b, add_bias(st_in2b))
            act.wait_ge(y_kept, 4)
            y = proj2[:, U2:U2 + 4, :]
            act.activation(y, y, ACT.Gelu).then_inc(y_act, 1)

            def glu(i, s):
                whole(st_glu, i, s)
                dst, func = (glu_v, ACT.Identity) if s < 2 else (glu_g, ACT.Sigmoid)
                for c in range(2):
                    last = act.activation(dst[:, 2 * (s % 2) + c, :],
                                          bank[(st_glu.group0 + s) % 2][:, c * TOK:(c + 1) * TOK],
                                          func, bias=param("b_glu_2", 2 * s + c))
                last.then_inc(evacuated["act"], 1)

            stream(st_glu, glu)
            stream(st_in2c, add_bias(st_in2c))
            stream(st_branch2)
            stream(st_out2, square_residual(st_out2, 5, evacuated["dve"], st_out2.evac0))
            stream(st_up2, gelu_gate(st_up2, 22, ACT.Gelu), norm_beside(5, True))
            stream(st_down2, square_residual(st_down2, 6, evacuated["dve"], st_down2.evac0))
            root(6)

        @block.vector
        def _(dve):
            def stream(st, epilogue=None, beside=None):
                def lo(i, j, s):
                    q = st.piece0 + i * st.ppb + j
                    k = j % RING
                    n = min(PIECE_KT, st.slots[s][2])
                    dve.wait_ge(hi_ready, q + 1)
                    dve.tensor_tensor(w_lo[:, k, 0:n, :], w_raw[:, k, 0:n, :], w_hi[:, k, 0:n, :].bitcast(F32),
                                      ALU.subtract).then_inc(lo_ready, 1)
                with_epilogue(dve, st, lo, epilogue, beside)

            def whole(st, i, s):
                dve.wait_ge(piece_used, st.piece0 + i * st.ppb + sum(st.pieces[:s + 1]))

            def split(src, hi, lo):
                dve.tensor_copy(hi, src)
                dve.drain()
                return dve.tensor_tensor(lo, src, hi.bitcast(F32), ALU.subtract)

            def root(n):
                dve.wait_ge(std_ready, n + 1)
                dve.reciprocal(rstd[:, :], rstd[:, :])
                dve.drain()

            def root_beside(n):
                return lambda piece: root(n) if piece == 7 else None

            over_tokens = rstd[:, :].unsqueeze(1).to_broadcast([P, 2, TOK])

            def gain_split(gain, c):
                for t in range(4 * c, 4 * c + 4):
                    dve.tensor_scalar(act_hi[:, t, :], hT[:, t, :], param(gain, t), None, ALU.mult)
                dve.drain()
                for t in range(4 * c, 4 * c + 4):
                    last = dve.scalar_tensor_tensor(out=act_lo[:, t, :], in0=hT[:, t, :], scalar=param(gain, t),
                                                    in1=act_hi[:, t, :].bitcast(F32), op0=ALU.mult, op1=ALU.subtract)
                last.then_inc(split_ready, 1)

            def add_normed(src, gain, c):
                for t in range(4):
                    dve.scalar_tensor_tensor(out=tmp[:, c % 2, t, :], in0=src[:, 4 * c + t, :], scalar=param(gain, 4 * c + t),
                                             in1=rstd[:, :], op0=ALU.mult, op1=ALU.mult)
                dve.drain()
                last = dve.tensor_tensor(hT[:, 4 * c:4 * c + 4, :], hT[:, 4 * c:4 * c + 4, :], tmp[:, c % 2, :, :], ALU.add)
                return last

            def scaled_to(st, dst, pair0=0):
                def ep(i, s):
                    whole(st, i, s)
                    t = (pair0 + i * len(st.slots) + s) * 2
                    dve.tensor_tensor(dst[:, bass.ds(t, 2), :],
                                      bank[(st.group0 + s) % 2][:, :].rearrange("p (c t) -> p c t", c=2),
                                      over_tokens, ALU.mult).then_inc(evacuated["dve"], 1)
                return ep

            def mixer_1(n):
                scale = 1.0 / math.sqrt(P)
                for p in which(lambda p: LEAD + 4 + p // 2 if p < 6 else at_stick(0) + LEAD - 1, 8, n):
                    tile = (VA + 2 * p) if p < HEADS_A // 2 else VB + 2 * p - HEADS_A
                    dve.wait_ge(v_turned, p + 1)
                    dve.tensor_copy(proj1[:, tile:tile + 2, :], ps_t[p % 2][:, :].rearrange("p (c t) -> p c t", c=2)
                                    ).then_inc(v_kept, 1)
                for u in which(lambda u: at_unit(u) + LEAD, 8, n):
                    h, qt = u // 2, u % 2
                    keys = P * (qt + 1)
                    c0 = qt * P
                    for g in range(3):
                        slope = 2.0 ** (-8.0 * (4 * g + h + 1) / HEADS_A)
                        dve.scalar_tensor_tensor(out=bias_t[:, g * keys:(g + 1) * keys],
                                                 in0=table("dist")[:, c0:c0 + keys], scalar=-slope,
                                                 in1=table(f"pen{g}")[:, c0:c0 + keys], op0=ALU.mult, op1=ALU.add)
                    dve.drain()
                    dve.wait_ge(sc_ready, u + 1)
                    if u >= 2:
                        dve.wait_ge(p_turned, u - 1)
                    for g in range(3):
                        last = dve.scalar_tensor_tensor(
                            out=s_buf[:, u % 2, g * keys:(g + 1) * keys],
                            in0=ps_a[g // 2][:, (g % 2) * keys:(g % 2) * keys + keys], scalar=scale,
                            in1=bias_t[:, g * keys:(g + 1) * keys], op0=ALU.mult, op1=ALU.add)
                    last.then_inc(sc_read, 1)
                    dve.drain()
                    m = small[:, u % 2:u % 2 + 1]
                    dve.tensor_reduce(m, s_buf[:, u % 2, 0:3 * keys], AX.X, ALU.max)
                    dve.drain()
                    dve.tensor_scalar(small[:, 8 + u % 2:9 + u % 2], m, -1.0, None, ALU.mult).then_inc(s_max, 1)
                for u in which(lambda u: at_unit(u) + LEAD + 2, 8, n):
                    k = 3 * P * (u % 2 + 1)
                    dve.wait_ge(p_exp, u + 1)
                    r = small[:, 24 + u % 2:25 + u % 2]
                    dve.reciprocal(r, small[:, 16 + u % 2:17 + u % 2])
                    dve.drain()
                    dve.tensor_scalar(s_buf[:, u % 2, 0:k], s_buf[:, u % 2, 0:k], r, None, ALU.mult).then_inc(p_norm, 1)
                for u in which(lambda u: at_unit(u) + LEAD + 4, 8, n):
                    k = 3 * P * (u % 2 + 1)
                    dve.wait_ge(p_turned, u + 1)
                    if k > 512:
                        dve.tensor_copy(pT_buf[:, 512:k], ps_t[1][:, 0:k - 512])
                    dve.tensor_copy(pT_buf[:, 0:min(k, 512)], ps_t[0][:, 0:min(k, 512)]).then_inc(pt_kept, 1)
                for u in which(lambda u: at_unit(u) + LEAD + 6, 8, n):
                    dve.wait_ge(o_ready, u + 1)
                    dve.tensor_copy(proj1[:, QA + u // 2, (u % 2) * P:(u % 2) * P + P], ps_o[:, 0:P]).then_inc(o_kept, 1)
                for h in which(lambda h: at_stick(h) + LEAD + 6, HEADS_B, n):
                    dve.wait_ge(ob_ready, h + 1)
                    dve.tensor_copy(proj1[:, QB + h, :], ps_o[:, 0:TOK]).then_inc(ob_kept, 1)
                for h in which(lambda h: at_stick(h) + LEAD, HEADS_B, n):
                    dve.wait_ge(zb_ready, h + 1)
                    dve.scalar_tensor_tensor(out=z_b[:, :], in0=ps_a[0][:, 0:BLK], scalar=scale,
                                             in1=table("penb"), op0=ALU.mult, op1=ALU.add)
                    dve.drain()
                    dve.scalar_tensor_tensor(out=t_b[:, :], in0=z_b[:, :], scalar=-1.0, in1=z_b[:, :],
                                             op0=ALU.mult, op1=ALU.max).then_inc(zb_abs, 1)
                for h in which(lambda h: at_stick(h) + LEAD + 2, HEADS_B, n):
                    dve.wait_ge(zb_log, h + 1)
                    dve.scalar_tensor_tensor(out=sp_b[:, :], in0=z_b[:, :], scalar=0.0, in1=l_b[:, :],
                                             op0=ALU.max, op1=ALU.add).then_inc(sp_ready, 1)
                for h in which(lambda h: at_stick(h) + LEAD + 3, HEADS_B, n):
                    dve.wait_ge(cum_ready, h + 1)
                    dve.tensor_tensor(lw_b[:, :], z_b[:, :], ps_t[0][:, 0:BLK], ALU.subtract).then_inc(lw_ready, 1)

            MAG, ZR, ZI, NZR, NZI, POW = 1, 5, 6, 7, 8, 14

            def discretize(part):
                DT_, TH, CO, SI, A0, A1, A2, A3 = 0, 2, 3, 4, 9, 10, 11, 12
                v = lambda i: ssm[:, i, :]
                are, aim, ldt = (par[:, PAR[n][0]:PAR[n][0] + STATE_TILES]
                                 for n in ("ssm_a_re_2", "ssm_a_im_2", "ssm_log_dt_2"))

                def ts(o, x, s1, s2, op0, op1=None):
                    dve.tensor_scalar(o, x, s1, s2, op0, op1) if op1 is not None else dve.tensor_scalar(o, x, s1, None, op0)
                    dve.drain()

                def tt(o, x, y, op):
                    dve.tensor_tensor(o, x, y, op)
                    dve.drain()

                def stt(o, x, s, y, op0, op1):
                    dve.scalar_tensor_tensor(out=o, in0=x, scalar=s, in1=y, op0=op0, op1=op1)
                    dve.drain()

                def exp(o, x):
                    r, n, p = v(A0), v(A1), v(A2)
                    ts(r, x, -88.0, 88.0, ALU.max, ALU.min)
                    ts(ssm_i[:, :], r, 1.0 / math.log(2.0), None, ALU.mult)
                    dve.tensor_copy(n, ssm_i[:, :])
                    dve.drain()
                    stt(r, n, -0.693359375, r, ALU.mult, ALU.add)
                    stt(r, n, 2.12194440e-4, r, ALU.mult, ALU.add)
                    ts(p, r, 1.0 / 5040, None, ALU.mult)
                    for k in (720, 120, 24, 6, 2, 1):
                        stt(p, p, 1.0 / k, r, ALU.add, ALU.mult)
                    ts(p, p, 1.0, None, ALU.add)
                    ts(ssm_i[:, :], n, 127.0, float(1 << 23), ALU.add, ALU.mult)
                    tt(o, p, ssm_i[:, :].bitcast(F32), ALU.mult)

                if part == 0:
                    exp(v(DT_), ldt)
                    tt(v(A3), are, v(DT_), ALU.mult)
                    exp(v(MAG), v(A3))
                    tt(v(TH), aim, v(DT_), ALU.mult)
                if part == 1:
                    ts(ssm_i[:, :], v(TH), 1.0 / (2 * math.pi), None, ALU.mult)
                    dve.tensor_copy(v(A0), ssm_i[:, :])
                    dve.drain()
                    for part in (6.28125, 1.9350051879882812e-3, 3.019916050e-7):
                        stt(v(TH), v(A0), -part, v(TH), ALU.mult, ALU.add)
                    ts(v(TH), v(TH), 0.5, None, ALU.mult)
                    tt(v(A0), v(TH), v(TH), ALU.mult)
                    for o, first in ((A1, 2), (A2, 1)):
                        top = 13 if first == 2 else 14
                        sign = lambda n: -1.0 if (n // 2) % 2 else 1.0
                        ts(v(o), v(A0), sign(top) / math.factorial(top), None, ALU.mult)
                        for n in range(top - 2, first - 1, -2):
                            if n >= 2:
                                stt(v(o), v(o), sign(n) / math.factorial(n), v(A0), ALU.add, ALU.mult)
                        if first == 2:
                            stt(v(o), v(o), 1.0, v(TH), ALU.add, ALU.mult)
                        else:
                            ts(v(o), v(o), 1.0, None, ALU.add)
                    stt(v(SI), v(A1), 2.0, v(A2), ALU.mult, ALU.mult)
                    tt(v(A3), v(A1), v(A1), ALU.mult)
                    ts(v(CO), v(A3), -2.0, 1.0, ALU.mult, ALU.add)
                if part == 2:
                    dve.tensor_copy(v(POW), v(CO))
                    dve.tensor_copy(v(POW + 1), v(SI))
                    dve.drain()
                    for k in range(7):
                        c, s = v(POW + 2 * k), v(POW + 2 * k + 1)
                        tt(v(A0), c, c, ALU.mult)
                        tt(v(A1), s, s, ALU.mult)
                        tt(v(POW + 2 * k + 2), v(A0), v(A1), ALU.subtract)
                        stt(v(POW + 2 * k + 3), c, 2.0, s, ALU.mult, ALU.mult)
                    dve.sem_inc(powers_ready, 1)
                if part == 3:
                    tt(v(A0), v(MAG), v(CO), ALU.mult)
                    ts(v(A0), v(A0), -1.0, None, ALU.add)
                    tt(v(A1), v(MAG), v(SI), ALU.mult)
                    tt(v(A2), are, are, ALU.mult)
                    tt(v(A3), aim, aim, ALU.mult)
                    tt(v(A2), v(A2), v(A3), ALU.add)
                    dve.reciprocal(v(A2), v(A2))
                    dve.drain()
                    tt(v(ZR), v(A0), are, ALU.mult)
                    tt(v(A3), v(A1), aim, ALU.mult)
                    tt(v(ZR), v(ZR), v(A3), ALU.add)
                    tt(v(ZR), v(ZR), v(A2), ALU.mult)
                    tt(v(ZI), v(A1), are, ALU.mult)
                    tt(v(A3), v(A0), aim, ALU.mult)
                    tt(v(ZI), v(ZI), v(A3), ALU.subtract)
                    tt(v(ZI), v(ZI), v(A2), ALU.mult)
                    ts(v(NZR), v(ZR), -1.0, None, ALU.mult)
                    ts(v(NZI), v(ZI), -1.0, None, ALU.mult)

            def mixer_2(n):
                if n == 7:
                    root(4)
                if n in (8, 9, 10, 11):
                    discretize(n - 8)
                for m in which(lambda m: at_state(m) + LEAD, STATE_TILES, n):
                    state_tile(m)
                for b in which(lambda b: at_state(STATE_BLOCK * b + 3) + LEAD + 4, 4, n):
                    dve.wait_ge(x_used, STATE_BLOCK * b + 4)
                    u = proj2[:, U2 + b, :]
                    dve.scalar_tensor_tensor(out=u, in0=u, scalar=param("ssm_d_2", b), in1=ps_o[:, 0:TOK],
                                             op0=ALU.mult, op1=ALU.add).then_inc(y_kept, 1)
                if n == at_head(0):
                    dve.memset(kpad[:, :, :, :], 0.0)
                    dve.memset(vpad[:, :, :, :, :], 0.0)
                    dve.wait_ge(v_turned, 9)
                    dve.tensor_copy(vtok, ps_t[0][:, 0:TOK].rearrange("p (k c) -> p k c", k=2))
                    dve.drain()
                    for j in range(KV_2):
                        for half in range(2):
                            r, s = slice(HD_2 * half, HD_2 * half + HD_2), slice(HD_2 * j, HD_2 * j + HD_2)
                            dve.tensor_copy(kpad[r, j, half, :], proj2[s, K2, :])
                            last = dve.tensor_copy(vpad[:, j, half, :, r], vtok[:, :, s])
                    last.then_inc(pad_ready, 1)
                for h in which(lambda h: at_head(h) + LEAD, HEADS_2, n):
                    o = 16 * (h % 2)
                    slope = 2.0 ** (-8.0 * (h + 1) / HEADS_2)
                    b = s2_buf[:, h % 2, :]
                    dve.scalar_tensor_tensor(out=bias2_t, in0=table("dist"), scalar=-slope, in1=table("penw"),
                                             op0=ALU.mult, op1=ALU.add)
                    dve.drain()
                    dve.wait_ge(sc_ready, 8 + h + 1)
                    if h >= 2:
                        dve.wait_ge(p_turned, 8 + h - 1)
                    dve.scalar_tensor_tensor(out=b, in0=ps_t[0][:, 0:BLK], scalar=HD_2 ** -0.5, in1=bias2_t,
                                             op0=ALU.mult, op1=ALU.add).then_inc(sc_read, 1)
                    dve.drain()
                    dve.tensor_reduce(small2[:, o + 6:o + 7], b[:, 0:P], AX.X, ALU.max)
                    dve.tensor_reduce(small2[:, o + 7:o + 8], b[:, P:BLK], AX.X, ALU.max)
                    dve.drain()
                    dve.tensor_scalar(small2[:, o:o + 2], small2[:, o + 6:o + 8], param("attn_sinks_2", h), -1.0,
                                      ALU.max, ALU.mult).then_inc(s_max, 1)
                for h in which(lambda h: at_head(h) + LEAD + 2, HEADS_2, n):
                    o = 16 * (h % 2)
                    b = s2_buf[:, h % 2, :]
                    dve.wait_ge(p_exp, 8 + h + 1)
                    dve.tensor_tensor(small2[:, o + 8:o + 10], small2[:, o + 2:o + 4], small2[:, o + 4:o + 6], ALU.add)
                    dve.drain()
                    dve.reciprocal(small2[:, o + 10:o + 12], small2[:, o + 8:o + 10])
                    dve.drain()
                    dve.tensor_scalar(b[:, 0:P], b[:, 0:P], small2[:, o + 10:o + 11], None, ALU.mult)
                    dve.tensor_scalar(b[:, P:BLK], b[:, P:BLK], small2[:, o + 11:o + 12], None, ALU.mult).then_inc(p_norm, 1)
                for h in which(lambda h: at_head(h) + LEAD + 4, HEADS_2, n):
                    dve.wait_ge(p_turned, 8 + h + 1)
                    dve.tensor_copy(pT2_buf, ps_t[1][:, 0:BLK]).then_inc(pt_kept, 1)
                for h in which(lambda h: at_head(h) + LEAD + 6, HEADS_2, n):
                    if h % 2:
                        dve.wait_ge(o_ready, 8 + h // 2 + 1)
                        dve.tensor_copy(proj2[:, Q2 + h // 2, :], ps_n[:, 0:TOK]).then_inc(o_kept, 1)

            def state_tile(n):
                k = n % STATE_RING
                col = lambda i: ssm[:, i, n:n + 1]
                bc = bc_pad[:, k, :, :]
                if n >= 2:
                    dve.wait_ge(x_used, n - 1)
                dve.wait_ge(bc_landed[k], 16 * (n // STATE_RING + 1))
                z0, z1 = cz[:, n % 2, 0, :], cz[:, n % 2, 1, :]
                dve.tensor_scalar(z0, bc[:, 3, :], col(NZI), None, ALU.mult)
                dve.tensor_scalar(z1, bc[:, 3, :], col(NZR), None, ALU.mult)
                dve.drain()
                dve.scalar_tensor_tensor(out=z0, in0=bc[:, 2, :], scalar=col(ZR), in1=z0, op0=ALU.mult, op1=ALU.add)
                dve.scalar_tensor_tensor(out=z1, in0=bc[:, 2, :], scalar=col(NZI), in1=z1, op0=ALU.mult, op1=ALU.add)
                dve.wait_ge(rot_ready, n + 1)
                dve.wait_ge(v_ready, n + 1)
                re, im = ps_a[n % 2][:, 0:TOK], ps_a[n % 2][:, TOK:2 * TOK]
                c, s = rot[:, k, 0, :], rot[:, k, 1, :]
                dve.tensor_tensor(pr[:, 0, :], re, c, ALU.mult)
                dve.tensor_tensor(pr[:, 1, :], im, s, ALU.mult)
                dve.tensor_tensor(pr[:, 2, :], im, c, ALU.mult)
                dve.tensor_tensor(pr[:, 3, :], re, s, ALU.mult).then_inc(v_read, 1)
                dve.drain()
                dve.tensor_tensor(vrot[:, 0, :], pr[:, 0, :], pr[:, 1, :], ALU.add)
                dve.tensor_tensor(vrot[:, 1, :], pr[:, 2, :], pr[:, 3, :], ALU.subtract)
                dve.drain()
                for i in range(2):
                    dve.tensor_tensor_scan(scn[:, i, :], col(MAG).to_broadcast([P, TOK]), vrot[:, i, :], 0.0,
                                           ALU.mult, ALU.add)
                dve.drain()
                dve.tensor_tensor(pr[:, 0, :], scn[:, 0, :], c, ALU.mult)
                dve.tensor_tensor(pr[:, 1, :], scn[:, 1, :], s, ALU.mult)
                dve.tensor_tensor(pr[:, 2, :], scn[:, 0, :], s, ALU.mult)
                dve.tensor_tensor(pr[:, 3, :], scn[:, 1, :], c, ALU.mult)
                dve.drain()
                dve.tensor_tensor(xs[:, n % 2, 0, :], pr[:, 0, :], pr[:, 1, :], ALU.subtract)
                dve.tensor_tensor(xs[:, n % 2, 1, :], pr[:, 2, :], pr[:, 3, :], ALU.add).then_inc(x_ready, 1)

            def gated_sum(st, proj, gate0, gate1, open_gate, opened):
                n_pair = len(st.slots) // 2

                def ep(i, s):
                    whole(st, i, s)
                    if s == 0 and isinstance(i, int) and i == 0:
                        dve.wait_ge(open_gate, opened)
                    t = (i * n_pair + s // 2) * 2
                    ps = bank[(st.group0 + s) % 2][:, :].rearrange("p (c t) -> p c t", c=2)
                    g0, g1 = proj[:, bass.ds(gate0 + t, 2), :], proj[:, bass.ds(gate1 + t, 2), :]
                    g = g1 if s % 2 else g0
                    dve.scalar_tensor_tensor(out=g, in0=g, scalar=1.0, in1=ps, op0=ALU.add, op1=ALU.mult
                                             ).then_inc(evacuated["dve"], 1)
                    if s % 2:
                        dve.drain()
                        dve.tensor_tensor(g0, g0, g1, ALU.add)
                        dve.drain()
                        hi, lo = act_hi[:, bass.ds(t, 2), :], act_lo[:, bass.ds(t, 2), :]
                        dve.tensor_scalar(hi, g0, 0.5, None, ALU.mult)
                        dve.drain()
                        last = dve.scalar_tensor_tensor(out=lo, in0=g0, scalar=0.5, in1=hi.bitcast(F32),
                                                        op0=ALU.mult, op1=ALU.subtract)
                        if s % 4 == 3:
                            last.then_inc(split_ready, 1)
                return ep

            def conv(dst, ps, w, b, tile, half_tiles):
                for c in range(2):
                    x, y = ps[:, c * TOK:(c + 1) * TOK], dst[:, c, :]
                    dve.tensor_scalar(y, x, param_at(w, 2 * half_tiles + tile + c), param_at(b, tile + c), ALU.mult, ALU.add)
                for back in (1, 2):
                    dve.drain()
                    for c in range(2):
                        x, y = ps[:, c * TOK:(c + 1) * TOK - back], dst[:, c, back:]
                        last = dve.scalar_tensor_tensor(out=y, in0=x, scalar=param_at(w, (2 - back) * half_tiles + tile + c),
                                                        in1=y, op0=ALU.mult, op1=ALU.add)
                return last

            def scaled_pairs(st, at):
                def ep(i, s):
                    whole(st, i, s)
                    t = ORDER_2[at + s]
                    dve.tensor_tensor(proj2[:, t:t + 2, :], bank[(st.group0 + s) % 2][:, :].rearrange("p (c t) -> p c t", c=2),
                                      over_tokens, ALU.mult).then_inc(evacuated["dve"], 1)
                return ep

            def ffn(st, base, w, b, tiles, value_conv):
                def ep(i, s):
                    whole(st, i, s)
                    ps = bank[(st.group0 + s) % 2]
                    pair = ps[:, :].rearrange("p (c t) -> p c t", c=2)
                    if s == 0 or value_conv:
                        dve.tensor_tensor(pair, pair, over_tokens, ALU.mult)
                        dve.drain()
                    if s == 0:
                        conv(gate_y, ps, w, b, 2 * i, tiles).then_inc(evacuated["dve"], 1)
                        return
                    if value_conv:
                        conv(val_y, ps, w, b, 2 * i + FT, tiles).then_inc(evacuated["dve"], 1)
                        dve.drain()
                        dve.wait_ge(gate_act, base + i + 1)
                        dve.tensor_tensor(val_y[:, :, :], val_y[:, :, :], gate_g[:, :, :], ALU.mult)
                    else:
                        dve.tensor_tensor(val_y[:, :, :], pair, over_tokens, ALU.mult).then_inc(evacuated["dve"], 1)
                        dve.drain()
                        dve.wait_ge(gate_act, base + i + 1)
                        dve.tensor_tensor(val_y[:, :, :], val_y[:, :, :], gate_g[:, :, :], ALU.mult)
                    dve.drain()
                    split(val_y[:, :, :], f_hi[:, bass.ds(2 * i, 2), :], f_lo[:, bass.ds(2 * i, 2), :]).then_inc(f_ready, 1)
                return ep

            def add_to_residual(st):
                def ep(i, s):
                    whole(st, i, s)
                    h = hT[:, bass.ds((i * len(st.slots) + s) * 2, 2), :]
                    dve.tensor_tensor(h, h, bank[(st.group0 + s) % 2][:, :].rearrange("p (c t) -> p c t", c=2),
                                      ALU.add).then_inc(evacuated["dve"], 1)
                return ep

            def ple(i, s):
                n = i * 2 + s
                dve.wait_ge(evacuated["act"], st_gate.evac0 + n + 1)
                h = hT[:, bass.ds(2 * n, 2), :]
                dve.tensor_tensor(sg[:, :, :], sg[:, :, :], eT[:, bass.ds(2 * n, 2), :], ALU.mult)
                dve.drain()
                dve.tensor_tensor(h, h, sg[:, :, :], ALU.add).then_inc(ple_used, 1)

            dve.memset(small_c[:, 0:1], EPS)
            dve.memset(small_c[:, 1:2], 1.0).then_inc(consts, 1)
            dve.wait_ge(loaded, 64)
            at_b = PAR["b_in_2"][0] + GATE_AT
            dve.tensor_scalar(half_b[:, :], par[:, at_b:at_b + PROJ2 - GATE_AT], 0.5, None, ALU.mult).then_inc(halved, 1)
            for c in range(4):
                gain_split("g_mix_pre", c)
            stream(st_in, scaled_to(st_in, proj1), root_beside(0))
            stream(st_mix, scaled_to(st_mix, proj1, QB // 2), mixer_1)
            dve.drain()
            split(proj1[:, QA:QA + 4, :], y_hi[:, 0:4, :], y_lo[:, 0:4, :]).then_inc(split_ready, 1)
            split(proj1[:, QB:QB + 4, :], y_hi[:, 4:8, :], y_lo[:, 4:8, :]).then_inc(split_ready, 1)
            stream(st_rest, scaled_to(st_rest, proj1, QB // 2 + 18))
            stream(st_branch, gated_sum(st_branch, proj1, GATE_A, GATE_B, gates_open, 16))
            stream(st_out)
            root(1)
            for c in range(4):
                add_normed(mT, "g_mix_post", c).then_inc(resid_ready, 1)
                dve.drain()
                gain_split("g_ffn_pre", c)
            stream(st_up, ffn(st_up, 0, "conv_w", "conv_b", 2 * FT, True), root_beside(2))
            dve.drain()
            split(pT[:, :, :], p_hi[:, :, :], p_lo[:, :, :]).then_inc(split_ready, 1)
            stream(st_down)
            stream(st_ple)
            root(3)
            for c in range(4):
                add_normed(m2T, "g_ffn_post", c)
                dve.drain()
                split(hT[:, 4 * c:4 * c + 4, :], act_hi[:, 4 * c:4 * c + 4, :],
                      act_lo[:, 4 * c:4 * c + 4, :]).then_inc(split_ready, 1)
            stream(st_gate, ple)
            dve.drain()
            for c in range(4):
                gain_split("attn_norm_g_2", c)
            stream(st_in2, scaled_pairs(st_in2, 0), mixer_2)
            stream(st_in2b, scaled_pairs(st_in2b, 20))
            dve.wait_ge(y_act, 1)
            split(proj2[:, U2:U2 + 4, :], x2_hi[:, 8:12, :], x2_lo[:, 8:12, :]).then_inc(split_ready, 1)
            for c in range(2):
                split(proj2[:, Q2 + 4 * c:Q2 + 4 * c + 4, :], x2_hi[:, 4 * c:4 * c + 4, :],
                      x2_lo[:, 4 * c:4 * c + 4, :]).then_inc(split_ready, 1)
            stream(st_glu)

            def gate_glu(piece):
                if piece == 2:
                    dve.wait_ge(evacuated["act"], st_glu.evac0 + 4)
                    dve.tensor_tensor(glu_v[:, :, :], glu_v[:, :, :], glu_g[:, :, :], ALU.mult)
                    dve.drain()
                    split(glu_v[:, :, :], x2_hi[:, 12:16, :], x2_lo[:, 12:16, :]).then_inc(split_ready, 1)

            stream(st_in2c, scaled_pairs(st_in2c, 21), gate_glu)
            stream(st_branch2, gated_sum(st_branch2, proj2, GATE_AT, GATE_SSM, biased_ready, 23))
            stream(st_out2, add_to_residual(st_out2))
            dve.drain()
            for c in range(4):
                gain_split("ffn_norm_g_2", c)
            stream(st_up2, ffn(st_up2, 22, "conv_w_2", "conv_b_2", FT, False), root_beside(5))
            stream(st_down2, add_to_residual(st_down2))
            root(6)
            for c in range(4):
                for t in range(4):
                    h = hT[:, 4 * c + t, :]
                    last = dve.scalar_tensor_tensor(out=h, in0=h, scalar=param("final_norm_g_2", 4 * c + t),
                                                    in1=rstd[:, :], op0=ALU.mult, op1=ALU.mult)
                last.then_inc(split_ready, 1)

        @block.gpsimd
        def _(pool):
            def add_squares(n):
                for j in range(8):
                    pool.wait_ge(sq_ready, 8 * n + j + 1)
                    if j == 0:
                        if n:
                            pool.wait_ge(sum_ready, n)
                        pool.tensor_copy(sq_sum(n), sq_slot(n, 0)).then_inc(sq_used, 1)
                    else:
                        pool.wait_ge(sq_used, 8 * n + j)
                        pool.tensor_tensor(sq_sum(n), sq_sum(n), sq_slot(n, j % 2), ALU.add).then_inc(sq_used, 1)

            def rotations(n):
                r = rot[:, n % STATE_RING, :, :]
                pool.memset(r[:, 0, 0:1], 1.0)
                pool.memset(r[:, 1, 0:1], 0.0)
                for e in range(8):
                    d = 1 << e
                    pc, ps = ssm[:, POW + 2 * e, n:n + 1], ssm[:, POW + 2 * e + 1, n:n + 1]
                    c, s = r[:, 0, 0:d], r[:, 1, 0:d]
                    t = [turn_t[:, i, 0:d] for i in range(4)]
                    pool.drain()
                    pool.tensor_scalar(t[0], c, pc, None, ALU.mult)
                    pool.tensor_scalar(t[1], s, ps, None, ALU.mult)
                    pool.tensor_scalar(t[2], c, ps, None, ALU.mult)
                    pool.tensor_scalar(t[3], s, pc, None, ALU.mult)
                    pool.drain()
                    pool.tensor_tensor(r[:, 0, d:2 * d], t[0], t[1], ALU.subtract)
                    last = pool.tensor_tensor(r[:, 1, d:2 * d], t[2], t[3], ALU.add)
                last.then_inc(rot_ready, 1)

            POW = 14
            for n in range(5):
                add_squares(n)
            pool.wait_ge(powers_ready, 1)
            for n in range(STATE_TILES):
                if n >= STATE_RING:
                    pool.wait_ge(x_ready, n - STATE_RING + 1)
                rotations(n)
            for n in (5, 6):
                add_squares(n)


def tables():
    t = np.zeros((P, TAB_COLS), np.float32)
    q = np.concatenate([np.arange(P)[:, None] + np.zeros((1, P), int), P + np.arange(P)[:, None] + np.zeros((1, TOK), int)], 1)
    k = np.concatenate([np.arange(P), np.arange(TOK)])[None, :]
    d = q - k

    def put(name, v):
        at, n = TAB[name]
        t[:, at:at + n] = v

    put("dist", d)
    for g, dil in enumerate(DILATIONS):
        put(f"pen{g}", np.where((d >= 0) & (d % dil == 0) & (d <= P * dil), 0, NEG))
    put("penw", np.where((d >= 0) & (d < P), 0, NEG))
    key = np.concatenate([np.zeros(TOK, int), np.full(P, P)])[None, :] + np.arange(P)[:, None]
    qry = np.concatenate([np.arange(TOK), P + np.arange(P)])[None, :]
    put("penb", np.where(key < qry, 0, NEG))
    put("tri", np.arange(P)[:, None] >= np.arange(P)[None, :])
    put("ident", np.eye(P))
    put("ones", 1)
    return t


def params(v):
    t = np.zeros((P, PAR_COLS), np.float32)

    def put(name, x, rows=1):
        at, n = PAR[name]
        t[:, at:at + n] = np.asarray(x).reshape(rows * n // rows, P).T

    for name in PAR:
        if name == "attn_sinks_2":
            at, n = PAR[name]
            t[:, at:at + n] = np.asarray(v[name]).reshape(1, n)
        elif name == "ssm_log_dt_2":
            put(name, np.repeat(np.asarray(v[name]).reshape(-1), HD_2))
        else:
            put(name, v[name])
    return t


def padded(v):
    bc = np.zeros((P, STATE_TILES, 4, P), np.float32)
    for i, part in enumerate(("re", "im")):
        vb, vc = np.asarray(v[f"ssm_b_{part}_2"])[0], np.asarray(v[f"ssm_c_{part}_2"])[0]
        for g in range(32):
            ch, st = slice(16 * (g % 8), 16 * (g % 8) + 16), slice(64 * (g % 2), 64 * (g % 2) + 64)
            bc[ch, g // 2, i, st] = vb[g].T
            bc[st, g // 2, 2 + i, ch] = vc[g].T
    return bc


WEIGHTS = ["w_in", "w_branch_a", "w_branch_b", "w_out", "w_up", "w_down", "w_ple_in", "w_ple_gate",
           "w_in_2", "w_glu_2", "w_branch_attn_2", "w_branch_ssm_2", "w_out_2", "w_up_2", "w_down_2"]


def kernel(**inputs):
    import concourse.bacc as bacc
    from concourse.bass_utils import run_bass_kernel_spmd

    def turned(x, tiles):
        return np.ascontiguousarray(np.asarray(x).reshape(TOK, tiles, P).transpose(2, 1, 0))

    arrays = {"xT": turned(inputs["x"], DT), "pT": turned(inputs["p"], 2), "tables": tables(),
              "params": params(inputs), "bc_pad": padded(inputs)}
    for name in WEIGHTS:
        arrays[name] = np.ascontiguousarray(np.asarray(inputs[name])[0])
    nc = bacc.Bacc("TRN2", target_bir_lowering=False, num_devices=1)
    a = {k: nc.dram_tensor(f"in_{k}", v.shape, mybir.dt.from_np(v.dtype), kind="ExternalInput").ap()
         for k, v in arrays.items()}
    out = nc.dram_tensor("out_T", (P, DT, TOK), F32, kind="ExternalOutput").ap()
    build(nc, a, out)
    r = run_bass_kernel_spmd(nc, [{f"in_{k}": v for k, v in arrays.items()}], core_ids=[0])
    got = r.results[0]["out_T"]
    return np.ascontiguousarray(got.transpose(2, 1, 0)).reshape(1, TOK, D)
```

```python
import math
from contextlib import ExitStack

import numpy as np
import concourse.bass as bass
from concourse import mybir

F32 = mybir.dt.float32
F32R = mybir.dt.float32r
I32 = mybir.dt.int32
ALU = mybir.AluOpType
ACT = mybir.ActivationFunctionType
AX = mybir.AxisListType

P = 128
TOK = 256
D = 2048
DT = D // P
FF = 5632
FT = FF // P
EPS = 1e-6
NEG = -1e30

PIECE_KT = 4
GROUP = 256
RING = 4

DILATIONS = (1, 4, 16)
QA, KA, VA, QB, KB, VB, GATE_A, GATE_B = 0, 12, 24, 36, 40, 44, 48, 64
HEADS_A, HEADS_B = 12, 4
HEADS_2, KV_2, HD_2 = 16, 2, 64
Q2, K2, V2, U2, GATE_AT, GATE_SSM, PROJ2 = 0, 8, 9, 10, 14, 30, 46
STATE_TILES, STATE_BLOCK, STATE_RING = 16, 4, 4

ORDER_2 = [U2, U2 + 2, K2] + list(range(Q2, K2, 2)) + list(range(GATE_AT, PROJ2, 2))

LEAD = 4
at_unit = lambda u: 8 + 4 * u
at_stick = lambda h: 43 + 6 * h
at_state = lambda n: 11 + 4 * n
at_head = lambda h: 22 + 3 * h


def which(place, count, n):
    return [u for u in range(count) if place(u) == n]


BLK = 384
TAB = {"dist0": (0, BLK), "dist1": (BLK, BLK), "dist2": (2 * BLK, BLK), "penb": (3 * BLK, BLK),
       "distw": (4 * BLK, BLK),
       "tri": (5 * BLK, P), "ident": (5 * BLK + P, P), "ones": (5 * BLK + 2 * P, P)}
TAB_COLS = 5 * BLK + 3 * P

PAR, _at = {}, 0
for _name, _n in (("g_mix_pre", 16), ("g_mix_post", 16), ("g_ffn_pre", 16), ("g_ffn_post", 16),
                  ("attn_norm_g_2", 16), ("ffn_norm_g_2", 16), ("final_norm_g_2", 16),
                  ("conv_w", 3 * 88), ("conv_b", 88), ("conv_w_2", 3 * 44), ("conv_b_2", 44),
                  ("b_in_2", 46), ("b_glu_2", 8), ("ssm_d_2", 4), ("attn_sinks_2", 16),
                  ("ssm_a_re_2", 16), ("ssm_a_im_2", 16), ("ssm_log_dt_2", 16)):
    PAR[_name] = (_at, _n)
    _at += _n
PAR_COLS = _at


class Stage:

    def __init__(self, name, slots, bodies, x, x_ready, evac):
        self.name, self.slots, self.bodies = name, slots, bodies
        self.x, self.x_ready, self.evac = x, x_ready, evac
        self.pieces = [-(-kt // PIECE_KT) for _, _, kt, _ in slots]
        self.ppb = sum(self.pieces)
        assert self.ppb % RING == 0


def place(stages):
    piece = group = 0
    done = {"act": 0, "dve": 0}
    owner = []
    for st in stages:
        st.piece0, st.group0, st.evac0 = piece, group, done[st.evac]
        n = st.bodies * len(st.slots)
        for _ in range(n):
            done[st.evac] += 1
            owner.append((st.evac, done[st.evac]))
        piece += st.bodies * st.ppb
        group += n
    for st in stages:
        st.owner = owner
    return piece, group


def build(nc, a, out):
    with ExitStack() as ctx:
        def sb(name, shape, dt=F32, scope=ctx):
            return scope.enter_context(nc.sbuf_tensor(name, shape, dt))

        def sem(name):
            return ctx.enter_context(nc.semaphore(name))

        hT = sb("hT", [P, DT, TOK])
        with ExitStack() as scope:
            m2T = sb("m2T", [P, DT, TOK], scope=scope)
        act_hi = sb("act_hi", [P, DT, TOK], F32R)
        act_lo = sb("act_lo", [P, DT, TOK], F32R)
        w_raw = sb("w_raw", [P, RING, PIECE_KT, GROUP])
        w_hi = sb("w_hi", [P, RING, PIECE_KT, GROUP], F32R)
        w_lo = sb("w_lo", [P, RING, PIECE_KT, GROUP], F32R)
        tab = sb("tab", [P, TAB_COLS])
        par = sb("par", [P, PAR_COLS])
        pT = sb("pT", [P, 2, TOK])
        rstd = sb("rstd", [P, TOK])
        small_c = sb("small_c", [P, 2])
        half_b = sb("half_b", [P, PROJ2 - GATE_AT])
        sinks = sb("sinks", [P, HEADS_2])
        ssm, ssm_i = sb("ssm", [P, 30, STATE_TILES]), sb("ssm_i", [P, STATE_TILES], I32)
        half_bias = lambda j: half_b[:, j:j + 1]
        eps, one = small_c[:, 0:1], small_c[:, 1:2]

        def table(name):
            at, n = TAB[name]
            return tab[:, at:at + n]

        def param(name, j):
            return par[:, PAR[name][0] + j:PAR[name][0] + j + 1]

        def param_at(name, j):
            return par[:, bass.ds(PAR[name][0] + j, 1)]

        ident, ones, tri = table("ident"), table("ones"), table("tri")

        def over(kept, *buffers):
            with ExitStack() as scope:
                if kept:
                    sb(f"skip{len(names)}", [P, kept], scope=scope)
                names.append(kept)
                return [sb(*b, scope=scope) for b in buffers]

        names = []
        T = TOK
        proj1, s_buf, pT_buf, small = over(
            0, ("proj1", [P, 80, T]), ("s_buf", [P, 2, 3 * T]), ("pT_buf", [P, 3 * T]),
            ("small", [P, 32]))
        z_b, t_b, l_b, sp_b, lw_b = over(80 * T, *((n, [P, BLK]) for n in ("z_b", "t_b", "l_b", "sp_b", "lw_b")))
        y_hi, y_lo = over(KA * T, ("y_hi", [P, 8, T], F32R), ("y_lo", [P, 8, T], F32R))
        mT, eT, tmp, sg, sq_x = over(
            0, ("mT", [P, DT, T]), ("eT", [P, DT, T]), ("tmp", [P, 2, 4, T]), ("sg", [P, 2, T]), ("sq_x", [P, 6, T]))
        sq_t = tab[:, 0:6 * T].rearrange("p (k t) -> p k t", k=6)
        squares_of = lambda n: sq_t if n else sq_x[:, :, :]
        sq_slot = lambda n, k: squares_of(n)[:, 2 * k:2 * k + 2, :]
        sq_sum = lambda n: squares_of(n)[:, 4:6, :]
        f_hi, f_lo, gate_y, gate_g, val_y = over(
            0, ("f_hi", [P, FT, T], F32R), ("f_lo", [P, FT, T], F32R), ("gate_y", [P, 2, T]), ("gate_g", [P, 2, T]),
            ("val_y", [P, 2, T]))
        p_hi, p_lo = over(2 * FT * T, ("p_hi", [P, 2, T], F32R), ("p_lo", [P, 2, T], F32R))
        proj2, kpad, vpad, s2_buf, small2, bc_pad, cz, rot, turns, vrot, scn, xs, pr = over(
            0, ("proj2", [P, PROJ2, T]), ("kpad", [P, KV_2, 2, T]), ("vpad", [P, KV_2, 2, 2, P]),
            ("s2_buf", [P, 2, BLK]), ("small2", [P, 32]), ("bc_pad", [P, STATE_RING, 4, P]), ("cz", [P, 2, 2, P]),
            ("rot", [P, 2, 2, T]), ("turns", [P, 2, 2, STATE_TILES, 16]), ("vrot", [P, 2, T]), ("scn", [P, 2, T]), ("xs", [P, 2, 2, T]),
            ("pr", [P, 4, T]))
        pT2_buf = tab[:, 0:BLK]
        vtok = tab[:, 2 * BLK:2 * BLK + T].rearrange("p (k c) -> p k c", k=2)
        cz_t = tab[:, BLK:BLK + 2 * P].rearrange("p (k c) -> p k c", k=2)
        turn_t = tab[:, 2 * BLK + T:2 * BLK + 3 * T].rearrange("p (k t) -> p k t", k=2)
        x2_hi, x2_lo, glu_v, glu_g = over(
            PROJ2 * T, ("x2_hi", [P, 16, T], F32R), ("x2_lo", [P, 16, T], F32R), ("glu_v", [P, 4, T]), ("glu_g", [P, 4, T]))

        bank = [ctx.enter_context(nc.psum_tensor(f"bank{i}", [P, 512], F32)) for i in range(2)]
        ps_a = [ctx.enter_context(nc.psum_tensor(f"ps_a{i}", [P, 512], F32)) for i in range(2)]
        ps_t = [ctx.enter_context(nc.psum_tensor(f"ps_t{i}", [P, 512], F32)) for i in range(2)]
        ps_o = ctx.enter_context(nc.psum_tensor("ps_o", [P, 512], F32))
        ps_n = ctx.enter_context(nc.psum_tensor("ps_n", [P, 512], F32))

        x_landed = [sem(f"x_landed{i}") for i in range(4)]
        par_landed, tab_landed, p_landed = sem("par_landed"), sem("tab_landed"), sem("p_landed")
        raw_landed = [sem(f"raw_landed{i}") for i in range(RING)]
        slots_freed = sem("slots_freed")
        hi_ready, lo_ready = sem("hi_ready"), sem("lo_ready")
        piece_used = sem("piece_used")
        evacuated = {"act": sem("evac_act"), "dve": sem("evac_dve")}
        x_hi_ready = sem("x_hi_ready")
        split_ready = sem("split_ready")
        f_ready = sem("f_ready")
        consts, halved = sem("consts"), sem("halved")
        normed_ready = sem("normed_ready")
        resid_ready = sem("resid_ready")
        sq_ready, sq_used = sem("sq_ready"), sem("sq_used")
        sum_ready, std_ready = sem("sum_ready"), sem("std_ready")
        gate_act = sem("gate_act")
        gates_open = sem("gates_open")
        biased_ready = sem("biased_ready")
        v_turned, v_kept = sem("v_turned"), sem("v_kept")
        sc_ready, sc_read, s_max = sem("sc_ready"), sem("sc_read"), sem("s_max")
        p_exp, recip_ready, p_norm = sem("p_exp"), sem("recip_ready"), sem("p_norm")
        p_turned, pt_kept = sem("p_turned"), sem("pt_kept")
        o_ready, o_kept = sem("o_ready"), sem("o_kept")
        zb_ready, zb_abs, zb_log = sem("zb_ready"), sem("zb_abs"), sem("zb_log")
        sp_ready, cum_ready, lw_ready, w_ready = sem("sp_ready"), sem("cum_ready"), sem("lw_ready"), sem("w_ready")
        ob_ready, ob_kept = sem("ob_ready"), sem("ob_kept")
        pad_ready, bc_landed = sem("pad_ready"), [sem(f"bc_landed{i}") for i in range(STATE_RING)]
        turns_ready, rot_ready = sem("turns_ready"), sem("rot_ready")
        scans_ready, x_im_ready = sem("scans_ready"), sem("x_im_ready")
        v_ready, v_read, x_ready, x_used = sem("v_ready"), sem("v_read"), sem("x_ready"), sem("x_used")
        y_kept, y_act, ple_used = sem("y_kept"), sem("y_act"), sem("ple_used")
        stored = sem("stored")

        def cols(w, kt, x0, step, at=0):
            return (a[w], lambda i: i * (step // G * P) + at // G * P, kt, x0)

        def main_x(first):
            return lambda j: (split_ready, first + j + 1)

        act_x, f_x, p_x = (act_hi, act_lo), (f_hi, f_lo), (p_hi, p_lo)
        G = GROUP
        SPLIT = {}
        at = 0
        for name, n in (("mix", 4), ("y1", 2), ("merged", 4), ("ffn", 4), ("ple_in", 1), ("ple_gate", 4),
                        ("mix2", 4), ("ssm_y", 1), ("attn2", 2), ("ssm", 1), ("merged2", 4), ("ffn2", 4)):
            SPLIT[name] = at
            at += n
        tiles = lambda w, ts: [cols(w, 16, 0, 0, t * P) for t in ts]
        branch1 = [s for k in range(2) for s in
                   (cols("w_branch_a", 4, 0, 2 * G, k * G), cols("w_branch_b", 4, 4, 2 * G, k * G))]
        branch2 = [s for k in range(4) for s in
                   (cols("w_branch_attn_2", 8, 0, 4 * G, k * G), cols("w_branch_ssm_2", 4, 12, 4 * G, k * G))]
        pair = lambda w: [cols(w, 16, 0, 2 * G), cols(w, 16, 0, 2 * G, G)]
        quad = lambda w, kt: [cols(w, kt, 0, 4 * G, k * G) for k in range(4)]
        st_in = Stage("in", pair("w_in"), QB // 4, act_x, main_x(SPLIT["mix"]), "dve")
        st_mix = Stage("mix", tiles("w_in", range(QB, QB + 36, 2)), 1, act_x, None, "dve")
        st_rest = Stage("rest", [cols("w_in", 16, 0, 2 * G, (QB + 36) * P), cols("w_in", 16, 0, 2 * G, (QB + 38) * P)],
                        2, act_x, None, "dve")
        st_branch = Stage("branch", branch1, 4, (y_hi, y_lo), lambda j: (split_ready, SPLIT["y1"] + 2), "dve")
        st_out = Stage("out", pair("w_out"), 4, act_x, main_x(SPLIT["merged"]), "act")
        st_up = Stage("up", [cols("w_up", 16, 0, G), cols("w_up", 16, 0, G, FF)], 22, act_x,
                      main_x(SPLIT["ffn"]), "dve")
        st_down = Stage("down", quad("w_down", FT), 2, f_x, lambda j: (f_ready, 2 * j + 2), "act")
        st_ple = Stage("ple", quad("w_ple_in", 2), 2, p_x, main_x(SPLIT["ple_in"]), "act")
        st_gate = Stage("ple_gate", pair("w_ple_gate"), 4, act_x, main_x(SPLIT["ple_gate"]), "act")
        st_in2 = Stage("in2", tiles("w_in_2", ORDER_2[:20]), 1, act_x, main_x(SPLIT["mix2"]), "dve")
        st_in2b = Stage("in2b", tiles("w_in_2", ORDER_2[20:21]), 1, act_x, None, "dve")
        st_glu = Stage("glu", [cols("w_glu_2", 4, 8, 0, k * G) for k in range(4)], 1, (x2_hi, x2_lo),
                       lambda j: (split_ready, SPLIT["ssm_y"] + 1), "act")
        st_in2c = Stage("in2c", tiles("w_in_2", ORDER_2[21:]), 1, act_x, None, "dve")
        st_branch2 = Stage("branch2", branch2, 2, (x2_hi, x2_lo), lambda j: (split_ready, SPLIT["ssm"] + 1), "dve")
        st_out2 = Stage("out2", pair("w_out_2"), 4, act_x, main_x(SPLIT["merged2"]), "dve")
        st_up2 = Stage("up2", [cols("w_up_2", 16, 0, G, FF), cols("w_up_2", 16, 0, G)], 22, act_x,
                       main_x(SPLIT["ffn2"]), "dve")
        st_down2 = Stage("down2", quad("w_down_2", FT), 2, f_x, lambda j: (f_ready, 22 + 2 * j + 2), "dve")
        stages = [st_in, st_mix, st_rest, st_branch, st_out, st_up, st_down, st_ple, st_gate,
                  st_in2, st_in2b, st_glu, st_in2c, st_branch2, st_out2, st_up2, st_down2]
        place(stages)

        def bodies(eng, st, body):
            body(0, True)
            if st.bodies > 1:
                with eng.Fori(1, st.bodies) as i:
                    body(i, False)

        def with_epilogue(eng, st, piece, epilogue, beside=None, carried=None, carry_at=3):
            n = len(st.slots)

            def body(i, first):
                j0 = 0
                for s in range(n):
                    for j in range(st.pieces[s]):
                        piece(i, j0 + j, s)
                        if first and beside:
                            beside(j0 + j)
                        if first and s == 0 and carried and j == min(carry_at, st.pieces[s] - 1):
                            carried()
                        if j == min(3, st.pieces[s] - 1) and epilogue and not (first and s == 0):
                            epilogue(i if s else i - 1, (s - 1) % n)
                    j0 += st.pieces[s]

            bodies(eng, st, body)
            return (lambda: epilogue(st.bodies - 1, n - 1)) if epilogue else None

        block = ctx.enter_context(nc.Block())

        @block.sync
        def _(sp):
            for st in stages:
                def states(n):
                    for m in which(lambda m: max(at_state(m) - 2, 0) if m >= STATE_RING else 2 + m, STATE_TILES, n):
                        if m >= STATE_RING:
                            sp.wait_ge(x_used, m - STATE_RING + 1)
                        else:
                            sp.wait_ge(ple_used, 8)
                        sp.dma_start(bc_pad[:, m % STATE_RING, :, :], a["bc_pad"][:, m, :, :]
                                     ).then_inc(bc_landed[m % STATE_RING], 16)

                def body(i, first, st=st):
                    j0 = 0
                    at_row = [col(i) if first else sp.snap(col(i)) for _, col, _, _ in st.slots]
                    for s, (w, _, kt, _) in enumerate(st.slots):
                        c = at_row[s]
                        for j in range(st.pieces[s]):
                            q = st.piece0 + i * st.ppb + j0 + j
                            k = (j0 + j) % RING
                            n = min(PIECE_KT, kt - j * PIECE_KT)
                            if not (first and st.piece0 + j0 + j < RING):
                                sp.wait_ge(lo_ready, q - RING + 1)
                                sp.sem_inc(slots_freed, 1)
                            c0 = j * PIECE_KT * GROUP
                            sp.dma_start(w_raw[:, k, 0:n, :].rearrange("p k n -> p (k n)"),
                                         w[bass.ds(c, P), c0:c0 + n * GROUP]).then_inc(raw_landed[k], 16)
                            if st is st_in2:
                                states(j0 + j)
                            if st is st_in and first and j0 + j == 1:
                                sp.dma_start(tab[:, :], a["tables"]).then_inc(tab_landed, 16)
                            if st is st_mix and j0 + j == 0:
                                sp.dma_start(pT[:, :, :], a["pT"]).then_inc(p_landed, 16)
                        j0 += st.pieces[s]
                bodies(sp, st, body)
            for c in range(4):
                sp.wait_ge(split_ready, at + c + 1)
                sp.dma_start(out[:, 4 * c:4 * c + 4, :], hT[:, 4 * c:4 * c + 4, :]).then_inc(stored, 16)
            sp.wait_ge(stored, 64)

        @block.tensor
        def _(pe):
            def mm(o, l, r, start, stop):
                return pe.matmul(o, l, r, start=start, stop=stop, skip_group_check=True)

            def stream(st, beside=None):
                xh, xl = st.x

                def body(i, first):
                    j0 = 0
                    for s, (_, _, kt, x0) in enumerate(st.slots):
                        g_in = st.group0 + s if first else None
                        ps = bank[(st.group0 + s) % 2]
                        if first and g_in >= 2:
                            eng, n = st.owner[g_in - 2]
                            pe.wait_ge(evacuated[eng], n)
                        elif not first:
                            pe.wait_ge(evacuated[st.evac], st.evac0 + i * len(st.slots) + s - 1)
                        for j in range(st.pieces[s]):
                            q = st.piece0 + i * st.ppb + j0 + j
                            k = (j0 + j) % RING
                            n = min(PIECE_KT, kt - j * PIECE_KT)
                            if first and s == 0 and st.x_ready:
                                pe.wait_ge(*st.x_ready(j))
                            pe.wait_ge(hi_ready, q + 1)
                            for t in range(n):
                                x = x0 + j * PIECE_KT + t
                                for c in range(2):
                                    o = ps[:, c * TOK:(c + 1) * TOK]
                                    w = w_hi[:, k, t, c * P:(c + 1) * P]
                                    mm(o, w, xh[:, x, :], j == 0 and t == 0 and c == 0, False)
                                    mm(o, w, xl[:, x, :], False, False)
                            pe.wait_ge(lo_ready, q + 1)
                            for t in range(n):
                                x = x0 + j * PIECE_KT + t
                                for c in range(2):
                                    last = mm(ps[:, c * TOK:(c + 1) * TOK], w_lo[:, k, t, c * P:(c + 1) * P],
                                              xh[:, x, :], False, j == st.pieces[s] - 1 and t == n - 1)
                            last.then_inc(piece_used, 1)
                            if first and beside:
                                beside(j0 + j)
                        j0 += st.pieces[s]
                bodies(pe, st, body)

            def sum_squares(n):
                if n == 0:
                    pe.wait_ge(tab_landed, 16)
                pe.wait_ge(sq_used, 8 * (n + 1))
                mm(ps_n[:, 0:TOK], ones, sq_sum(n)[:, 0, :], True, False)
                mm(ps_n[:, 0:TOK], ones, sq_sum(n)[:, 1, :], False, True).then_inc(sum_ready, 1)

            def sums_beside(n):
                return lambda piece: sum_squares(n) if piece == 3 else None

            def turn_values(n):
                tile = (VA + 2 * n) if n < HEADS_A // 2 else VB + 2 * n - HEADS_A
                if n >= 2:
                    pe.wait_ge(v_kept, n - 1)
                for t in range(4):
                    last = pe.transpose(ps_t[n % 2][:, t * P:(t + 1) * P],
                                        proj1[:, tile + t // 2, (t % 2) * P:(t % 2) * P + P], ident)
                last.then_inc(v_turned, 1)

            def mixer_1(n):
                if n == 4:
                    pe.wait_ge(evacuated["dve"], st_mix.evac0)
                if n in (4, 5, 6):
                    turn_values(2 * n - 8)
                    turn_values(2 * n - 7)
                for u in which(at_unit, 8, n):
                    h, qt = u // 2, u % 2
                    if u:
                        pe.wait_ge(sc_read, u)
                    keys = P * (qt + 1)
                    for g in range(3):
                        o = ps_a[g // 2][:, (g % 2) * keys:(g % 2) * keys + keys]
                        last = mm(o, proj1[:, QA + 4 * g + h, qt * P:qt * P + P],
                                  proj1[:, KA + 4 * g + h, 0:keys], g != 1, g != 0)
                    last.then_inc(sc_ready, 1)
                for u in which(lambda u: at_unit(u) + 4, 8, n):
                    pe.wait_ge(p_norm, u + 1)
                    if u == 0:
                        pe.wait_ge(v_kept, 6)
                    for b in range(3 * (u % 2 + 1)):
                        last = pe.transpose(ps_t[b // 4][:, (b % 4) * P:(b % 4) * P + P],
                                            s_buf[:, u % 2, b * P:(b + 1) * P], ident)
                    last.then_inc(p_turned, 1)
                for u in which(lambda u: at_unit(u) + 6, 8, n):
                    h, qt = u // 2, u % 2
                    pe.wait_ge(pt_kept, u + 1)
                    if u:
                        pe.wait_ge(o_kept, u)
                    for b in range(3 * (qt + 1)):
                        g, kt = b // (qt + 1), b % (qt + 1)
                        last = mm(ps_o[:, 0:P], proj1[:, VA + 4 * g + h, kt * P:kt * P + P],
                                  pT_buf[:, b * P:(b + 1) * P], b == 0, b == 3 * (qt + 1) - 1)
                    last.then_inc(o_ready, 1)
                if n == at_stick(0) - 1:
                    pe.wait_ge(pt_kept, 8)
                    turn_values(6)
                    turn_values(7)
                for h in which(at_stick, HEADS_B, n):
                    if h == 0:
                        pe.wait_ge(sc_read, 8)
                    q, k = proj1[:, QB + h, :], proj1[:, KB + h, :]
                    mm(ps_a[0][:, 0:TOK], k[:, 0:P], q, True, True)
                    mm(ps_a[0][:, TOK:BLK], k[:, P:TOK], q[:, P:TOK], False, True).then_inc(zb_ready, 1)
                for h in which(lambda h: at_stick(h) + 3, HEADS_B, n):
                    pe.wait_ge(sp_ready, h + 1)
                    if h == 0:
                        pe.wait_ge(v_kept, 8)
                    mm(ps_t[0][:, 0:TOK], tri, sp_b[:, 0:TOK], True, False)
                    mm(ps_t[0][:, P:TOK], ones, sp_b[:, TOK:BLK], False, True)
                    mm(ps_t[0][:, TOK:BLK], tri, sp_b[:, TOK:BLK], False, True).then_inc(cum_ready, 1)
                for h in which(lambda h: at_stick(h) + 5, HEADS_B, n):
                    pe.wait_ge(w_ready, h + 1)
                    if h == 0:
                        pe.wait_ge(o_kept, 8)
                    else:
                        pe.wait_ge(ob_kept, h)
                    v = proj1[:, VB + h, :]
                    mm(ps_o[:, 0:TOK], v[:, 0:P], t_b[:, 0:TOK], True, False)
                    mm(ps_o[:, P:TOK], v[:, P:TOK], t_b[:, TOK:BLK], False, True).then_inc(ob_ready, 1)

            def mixer_2(n):
                if n == 3:
                    sum_squares(4)
                for m in which(at_state, STATE_TILES, n):
                    if m == 0:
                        pe.wait_ge(biased_ready, 2)
                    pe.wait_ge(bc_landed[m % STATE_RING], 16 * (m // STATE_RING + 1))
                    if m >= 2:
                        pe.wait_ge(v_read, m - 1)
                    u = proj2[:, U2 + m // STATE_BLOCK, :]
                    mm(ps_a[m % 2][:, 0:TOK], bc_pad[:, m % STATE_RING, 0, :], u, True, True)
                    mm(ps_a[m % 2][:, TOK:], bc_pad[:, m % STATE_RING, 1, :], u, False, True).then_inc(v_ready, 1)
                for m in which(lambda m: at_state(m) + 5, STATE_TILES, n):
                    k = m % STATE_BLOCK
                    if k == 0 and m:
                        pe.wait_ge(y_kept, m // STATE_BLOCK)
                    pe.wait_ge(x_ready, m + 1)
                    pe.wait_ge(x_im_ready, m + 1)
                    mm(ps_o[:, 0:TOK], cz[:, m % 2, 0, :], xs[:, m % 2, 0, :], k == 0, False)
                    mm(ps_o[:, 0:TOK], cz[:, m % 2, 1, :], xs[:, m % 2, 1, :], False, k == 3).then_inc(x_used, 1)
                if n == at_head(0) - 4:
                    pe.wait_ge(biased_ready, 3)
                    for t in range(2):
                        last = pe.transpose(ps_t[0][:, t * P:(t + 1) * P], proj2[:, V2, t * P:(t + 1) * P], ident)
                    last.then_inc(v_turned, 1)
                for h in which(at_head, HEADS_2, n):
                    if h == 0:
                        pe.wait_ge(pad_ready, 1)
                    else:
                        pe.wait_ge(sc_read, 8 + h)
                    pe.wait_ge(biased_ready, 4 + h // 4)
                    j, half = h // (HEADS_2 // KV_2), h % 2
                    q, k = proj2[:, Q2 + h // 2, :], kpad[:, j, half, :]
                    mm(ps_t[0][:, 0:P], q[:, 0:P], k[:, 0:P], True, True)
                    mm(ps_t[0][:, P:BLK], q[:, P:TOK], k, False, True).then_inc(sc_ready, 1)
                for h in which(lambda h: at_head(h) + 4, HEADS_2, n):
                    pe.wait_ge(p_norm, 8 + h + 1)
                    for b in range(3):
                        last = pe.transpose(ps_t[1][:, b * P:(b + 1) * P], s2_buf[:, h % 2, b * P:(b + 1) * P], ident)
                    last.then_inc(p_turned, 1)
                for h in which(lambda h: at_head(h) + 6, HEADS_2, n):
                    j, half = h // (HEADS_2 // KV_2), h % 2
                    pe.wait_ge(pt_kept, 8 + h + 1)
                    if half == 0 and h:
                        pe.wait_ge(o_kept, 8 + h // 2)
                    mm(ps_n[:, 0:P], vpad[:, j, half, 0, :], pT2_buf[:, 0:P], half == 0, half == 1)
                    mm(ps_n[:, P:TOK], vpad[:, j, half, 0, :], pT2_buf[:, P:2 * P], False, False)
                    last = mm(ps_n[:, P:TOK], vpad[:, j, half, 1, :], pT2_buf[:, 2 * P:BLK], False, half == 1)
                    if half:
                        last.then_inc(o_ready, 1)

            stream(st_in, sums_beside(0))
            stream(st_mix, mixer_1)
            stream(st_rest)
            stream(st_branch)
            stream(st_out)
            sum_squares(1)
            stream(st_up, sums_beside(2))
            stream(st_down)
            stream(st_ple, lambda piece: sum_squares(3) if piece == 1 else None)
            stream(st_gate)
            stream(st_in2, mixer_2)
            stream(st_in2b)
            stream(st_glu)
            stream(st_in2c)
            stream(st_branch2)
            stream(st_out2)
            stream(st_up2, sums_beside(5))
            stream(st_down2)
            sum_squares(6)

        @block.scalar
        def _(act):
            def stream(st, epilogue=None, beside=None, carried=None, carry_at=3):
                def hi(i, j, s):
                    q = st.piece0 + i * st.ppb + j
                    k = j % RING
                    n = min(PIECE_KT, st.slots[s][2])
                    act.wait_ge(raw_landed[k], 16 * (st.piece0 // RING + j // RING + 1) + i * (16 * st.ppb // RING))
                    if not (isinstance(i, int) and q < RING):
                        act.wait_ge(piece_used, q - RING + 1)
                    act.activation(w_hi[:, k, 0:n, :], w_raw[:, k, 0:n, :], ACT.Copy).then_inc(hi_ready, 1)
                return with_epilogue(act, st, hi, epilogue, beside, carried, carry_at)

            def whole(st, i, s):
                act.wait_ge(piece_used, st.piece0 + i * st.ppb + sum(st.pieces[:s + 1]))

            def square(n, j, k, src):
                if not (n == 0 and isinstance(j, int) and j < 2):
                    act.wait_ge(sq_used, 8 * n + j - 1)
                act.activation(sq_slot(n, k), src, ACT.Square).then_inc(sq_ready, 1)

            def copy_to(st, dst, norm=None):
                def ep(i, s):
                    whole(st, i, s)
                    pair = i * len(st.slots) + s
                    ps = bank[(st.group0 + s) % 2][:, :].rearrange("p (c t) -> p c t", c=2)
                    if norm is not None:
                        square(norm, pair, s % 2, ps)
                    act.activation(dst[:, bass.ds(2 * pair, 2), :], ps, ACT.Copy).then_inc(evacuated["act"], 1)
                return ep

            def square_residual(st, n, done, done0):
                def ep(i, s):
                    pair = i * len(st.slots) + s
                    act.wait_ge(done, done0 + pair + 1)
                    square(n, pair, s % 2, hT[:, bass.ds(2 * pair, 2), :])
                return ep

            def root(n):
                act.wait_ge(sum_ready, n + 1)
                act.activation(rstd[:, :], ps_n[:, 0:TOK], ACT.Sqrt, bias=eps[:, 0:1],
                               scale=1.0 / D).then_inc(std_ready, 1)

            def round_up(n, c):
                ready, st, gain = {0: ((x_landed[c], 16), st_in, "g_mix_pre"),
                                   2: ((resid_ready, c + 1), st_up, "g_ffn_pre"),
                                   3: ((resid_ready, 4 + c + 1), st_gate, None),
                                   4: ((ple_used, 2 * c + 2), st_in2, "attn_norm_g_2"),
                                   5: ((evacuated["dve"], st_out2.evac0 + 2 * c + 2), st_up2, "ffn_norm_g_2")}[n]
                act.wait_ge(*ready)
                if n:
                    act.wait_ge(piece_used, st.piece0)
                if gain is None:
                    act.activation(act_hi[:, 4 * c:4 * c + 4, :], hT[:, 4 * c:4 * c + 4, :], ACT.Copy).then_inc(x_hi_ready, 1)
                    return
                for t in range(4 * c, 4 * c + 4):
                    last = act.activation(act_hi[:, t, :], hT[:, t, :], ACT.Copy, scale=param(gain, t))
                last.then_inc(x_hi_ready, 1)

            def norm_beside(n):
                def beside(piece):
                    if piece < 4:
                        round_up(n, piece)
                        if n in (0, 2):
                            for j in (2 * piece, 2 * piece + 1):
                                square(n, j, j % 2, hT[:, 2 * j:2 * j + 2, :])
                    if piece == 7:
                        root(n)
                return beside

            def open_gates(st):
                def ep(i, s):
                    n = (st.group0 - st_mix.group0) + i * len(st.slots) + s
                    if st is st_mix and s < 6:
                        return
                    act.wait_ge(evacuated["dve"], st_mix.evac0 + n + 1)
                    x = proj1[:, bass.ds(QB + 2 * n, 2), :]
                    act.activation(x, x, ACT.Tanh, scale=0.5).then_inc(gates_open, 1)
                return ep

            def add_bias(st):
                def ep(i, s):
                    tile = ORDER_2[{st_in2: 0, st_in2b: 20, st_in2c: 21}[st] + s]
                    gate = tile >= GATE_AT
                    act.wait_ge(evacuated["dve"], st.evac0 + s + 1)
                    for c in range(2):
                        x = proj2[:, tile + c, :]
                        if gate:
                            last = act.activation(x, x, ACT.Tanh, scale=0.5, bias=half_bias(tile + c - GATE_AT))
                        else:
                            last = act.activation(x, x, ACT.Identity, bias=param("b_in_2", tile + c))
                    last.then_inc(biased_ready, 1)
                return ep

            def mixer_1(n):
                scale = 1.0 / math.sqrt(P)
                for p in which(lambda p: LEAD + 4 + p // 2 if p < 6 else at_stick(0) + LEAD - 1, 8, n):
                    tile = (VA + 2 * p) if p < HEADS_A // 2 else VB + 2 * p - HEADS_A
                    act.wait_ge(v_turned, p + 1)
                    act.activation(proj1[:, tile:tile + 2, :], ps_t[p % 2][:, :].rearrange("p (c t) -> p c t", c=2),
                                   ACT.Copy).then_inc(v_kept, 1)
                for u in which(lambda u: at_unit(u) + LEAD + 1, 8, n):
                    k = 3 * P * (u % 2 + 1)
                    act.wait_ge(s_max, u + 1)
                    act.activation(s_buf[:, u % 2, 0:k], s_buf[:, u % 2, 0:k], ACT.Exp,
                                   bias=small[:, 8 + u % 2:9 + u % 2], scale=scale,
                                   accum_out=small[:, 16 + u % 2:17 + u % 2]).then_inc(p_exp, 1)
                for u in which(lambda u: at_unit(u) + LEAD + 3, 8, n):
                    k = 3 * P * (u % 2 + 1)
                    act.wait_ge(recip_ready, u + 1)
                    act.activation(s_buf[:, u % 2, 0:k], s_buf[:, u % 2, 0:k], ACT.Copy,
                                   scale=small[:, 24 + u % 2:25 + u % 2]).then_inc(p_norm, 1)
                for u in which(lambda u: at_unit(u) + LEAD + 5, 8, n):
                    k = 3 * P * (u % 2 + 1)
                    act.wait_ge(p_turned, u + 1)
                    if k > 512:
                        act.activation(pT_buf[:, 512:k], ps_t[1][:, 0:k - 512], ACT.Copy)
                    act.activation(pT_buf[:, 0:min(k, 512)], ps_t[0][:, 0:min(k, 512)], ACT.Copy).then_inc(pt_kept, 1)
                for u in which(lambda u: at_unit(u) + LEAD + 7, 8, n):
                    act.wait_ge(o_ready, u + 1)
                    act.activation(proj1[:, QA + u // 2, (u % 2) * P:(u % 2) * P + P], ps_o[:, 0:P],
                                   ACT.Copy).then_inc(o_kept, 1)
                for h in which(lambda h: at_stick(h) + LEAD + 6, HEADS_B, n):
                    act.wait_ge(ob_ready, h + 1)
                    act.activation(proj1[:, QB + h, :], ps_o[:, 0:TOK], ACT.Copy).then_inc(ob_kept, 1)
                for h in which(lambda h: at_stick(h) + LEAD + 1, HEADS_B, n):
                    act.wait_ge(zb_abs, h + 1)
                    act.activation(l_b[:, :], t_b[:, :], ACT.Exp, scale=-1.0)
                    act.drain()
                    act.activation(l_b[:, :], l_b[:, :], ACT.Ln, bias=one[:, 0:1]).then_inc(zb_log, 1)
                for h in which(lambda h: at_stick(h) + LEAD + 4, HEADS_B, n):
                    act.wait_ge(lw_ready, h + 1)
                    act.activation(t_b[:, :], lw_b[:, :], ACT.Exp).then_inc(w_ready, 1)

            def mixer_2(n):
                if n < 4:
                    round_up(4, n)
                if n == 3:
                    square(4, 7, 1, hT[:, 14:16, :])
                if n == 7:
                    root(4)
                for h in which(lambda h: at_head(h) + LEAD + 1, HEADS_2, n):
                    act.wait_ge(s_max, 8 + h + 1)
                    b = s2_buf[:, h % 2, :]
                    o = 16 * (h % 2)
                    act.activation(small2[:, o + 4:o + 6], small2[:, o:o + 2], ACT.Exp, bias=param("attn_sinks_2", h))
                    act.activation(b[:, 0:P], b[:, 0:P], ACT.Exp, bias=small2[:, o:o + 1], scale=HD_2 ** -0.5,
                                   accum_out=small2[:, o + 2:o + 3])
                    act.activation(b[:, P:BLK], b[:, P:BLK], ACT.Exp, bias=small2[:, o + 1:o + 2], scale=HD_2 ** -0.5,
                                   accum_out=small2[:, o + 3:o + 4]).then_inc(p_exp, 1)
                for h in which(lambda h: at_head(h) + LEAD + 3, HEADS_2, n):
                    b, o = s2_buf[:, h % 2, :], 16 * (h % 2)
                    act.wait_ge(recip_ready, 8 + h + 1)
                    act.activation(b[:, 0:P], b[:, 0:P], ACT.Copy, scale=small2[:, o + 10:o + 11])
                    act.activation(b[:, P:BLK], b[:, P:BLK], ACT.Copy, scale=small2[:, o + 11:o + 12]).then_inc(p_norm, 1)
                for h in which(lambda h: at_head(h) + LEAD + 5, HEADS_2, n):
                    act.wait_ge(p_turned, 8 + h + 1)
                    act.activation(pT2_buf, ps_t[1][:, 0:BLK], ACT.Copy).then_inc(pt_kept, 1)
                for h in which(lambda h: at_head(h) + LEAD + 7, HEADS_2, n):
                    if h % 2:
                        act.wait_ge(o_ready, 8 + h // 2 + 1)
                        act.activation(proj2[:, Q2 + h // 2, :], ps_n[:, 0:TOK], ACT.Copy).then_inc(o_kept, 1)

            def gelu_gate(st, base, func):
                def ep(i, s):
                    if s == 0:
                        return
                    act.wait_ge(evacuated["dve"], st.evac0 + 2 * i + 1)
                    if not (isinstance(i, int) and base + i == 0):
                        act.wait_ge(f_ready, base + i)
                    act.activation(gate_g[:, :, :], gate_y[:, :, :], func).then_inc(gate_act, 1)
                return ep

            for c in range(4):
                act.dma_start(hT[:, 4 * c:4 * c + 4, :], a["xT"][:, 4 * c:4 * c + 4, :]).then_inc(x_landed[c], 16)
                if c == 0:
                    act.dma_start(par[:, :], a["params"]).then_inc(par_landed, 16)
            act.wait_ge(par_landed, 16)
            act.wait_ge(consts, 1)
            stream(st_in, None, norm_beside(0))
            last = stream(st_mix, open_gates(st_mix), mixer_1)
            last = stream(st_rest, open_gates(st_rest), None, last)
            stream(st_branch, None, None, last)
            last = stream(st_out, copy_to(st_out, mT, 1))
            last()
            root(1)
            last = stream(st_up, gelu_gate(st_up, 0, ACT.Gelu_apprx_tanh), norm_beside(2))
            last = stream(st_down, copy_to(st_down, m2T, 3), None, last)
            last = stream(st_ple, copy_to(st_ple, eT), lambda piece: root(3) if piece == 3 else None, last)
            last()

            def ple(i, s):
                whole(st_gate, i, s)
                n = i * 2 + s
                if not (isinstance(i, int) and n == 0):
                    act.wait_ge(ple_used, n)
                act.activation(sg[:, :, :], bank[(st_gate.group0 + s) % 2][:, :].rearrange("p (c t) -> p c t", c=2),
                               ACT.Sigmoid).then_inc(evacuated["act"], 1)
                if s or not isinstance(i, int) or i:
                    square(4, n - 1, (s - 1) % 2, hT[:, bass.ds(2 * n - 2, 2), :])

            last = stream(st_gate, ple, lambda piece: round_up(3, piece) if piece < 4 else None)
            last()
            act.wait_ge(halved, 1)
            last = stream(st_in2, add_bias(st_in2), mixer_2)
            last = stream(st_in2b, add_bias(st_in2b), None, last)
            act.wait_ge(y_kept, 4)
            y = proj2[:, U2:U2 + 4, :]
            act.activation(y, y, ACT.Gelu).then_inc(y_act, 1)

            def glu(i, s):
                whole(st_glu, i, s)
                dst, func = (glu_v, ACT.Identity) if s < 2 else (glu_g, ACT.Sigmoid)
                for c in range(2):
                    last = act.activation(dst[:, 2 * (s % 2) + c, :],
                                          bank[(st_glu.group0 + s) % 2][:, c * TOK:(c + 1) * TOK],
                                          func, bias=param("b_glu_2", 2 * s + c))
                last.then_inc(evacuated["act"], 1)

            last = stream(st_glu, glu, None, last)
            last = stream(st_in2c, add_bias(st_in2c), None, last, 0)
            stream(st_branch2, None, None, last)
            last = stream(st_out2, square_residual(st_out2, 5, evacuated["dve"], st_out2.evac0))
            last = stream(st_up2, gelu_gate(st_up2, 22, ACT.Gelu), norm_beside(5), last)
            last = stream(st_down2, square_residual(st_down2, 6, evacuated["dve"], st_down2.evac0), None, last)
            last()
            root(6)

        @block.vector
        def _(dve):
            def stream(st, epilogue=None, beside=None, carried=None, carry_at=3):
                def lo(i, j, s):
                    q = st.piece0 + i * st.ppb + j
                    k = j % RING
                    n = min(PIECE_KT, st.slots[s][2])
                    dve.wait_ge(hi_ready, q + 1)
                    dve.tensor_tensor(w_lo[:, k, 0:n, :], w_raw[:, k, 0:n, :], w_hi[:, k, 0:n, :].bitcast(F32),
                                      ALU.subtract).then_inc(lo_ready, 1)
                return with_epilogue(dve, st, lo, epilogue, beside, carried, carry_at)

            def whole(st, i, s):
                dve.wait_ge(piece_used, st.piece0 + i * st.ppb + sum(st.pieces[:s + 1]))

            def split(src, hi, lo):
                dve.tensor_copy(hi, src)
                dve.drain()
                return dve.tensor_tensor(lo, src, hi.bitcast(F32), ALU.subtract)

            def root(n):
                dve.wait_ge(std_ready, n + 1)
                dve.reciprocal(rstd[:, :], rstd[:, :])
                dve.drain()

            over_tokens = rstd[:, :].unsqueeze(1).to_broadcast([P, 2, TOK])

            def round_off(n, c):
                dve.wait_ge(x_hi_ready, {0: 0, 2: 4, 3: 8, 4: 12, 5: 16}[n] + c + 1)
                gain = {0: "g_mix_pre", 2: "g_ffn_pre", 3: None, 4: "attn_norm_g_2", 5: "ffn_norm_g_2"}[n]
                if gain is None:
                    x = slice(4 * c, 4 * c + 4)
                    dve.tensor_tensor(act_lo[:, x, :], hT[:, x, :], act_hi[:, x, :].bitcast(F32),
                                      ALU.subtract).then_inc(split_ready, 1)
                    return
                for t in range(4 * c, 4 * c + 4):
                    last = dve.scalar_tensor_tensor(out=act_lo[:, t, :], in0=hT[:, t, :], scalar=param(gain, t),
                                                    in1=act_hi[:, t, :].bitcast(F32), op0=ALU.mult, op1=ALU.subtract)
                last.then_inc(split_ready, 1)

            def round_off_beside(n, ahead=None):
                def beside(piece):
                    if piece < 3:
                        if ahead and piece < 2:
                            ahead(piece + 2)
                        round_off(n, piece + 1)
                    if piece == 7 and n != 3:
                        root(n)
                return beside

            def normed(src, gain, c):
                for t in range(4):
                    last = dve.scalar_tensor_tensor(out=tmp[:, c % 2, t, :], in0=src[:, 4 * c + t, :], scalar=param(gain, 4 * c + t),
                                             in1=rstd[:, :], op0=ALU.mult, op1=ALU.mult)
                last.then_inc(normed_ready, 1)

            def scaled_to(st, dst, pair0=0):
                def ep(i, s):
                    whole(st, i, s)
                    t = (pair0 + i * len(st.slots) + s) * 2
                    dve.tensor_tensor(dst[:, bass.ds(t, 2), :],
                                      bank[(st.group0 + s) % 2][:, :].rearrange("p (c t) -> p c t", c=2),
                                      over_tokens, ALU.mult).then_inc(evacuated["dve"], 1)
                return ep

            def mixer_1(n):
                scale = 1.0 / math.sqrt(P)
                for u in which(lambda u: at_unit(u) + LEAD, 8, n):
                    h, qt = u // 2, u % 2
                    keys = P * (qt + 1)
                    c0 = qt * P
                    dve.wait_ge(sc_ready, u + 1)
                    if u >= 2:
                        dve.wait_ge(p_turned, u - 1)
                    for g in range(3):
                        slope = 2.0 ** (-8.0 * (4 * g + h + 1) / HEADS_A)
                        last = dve.scalar_tensor_tensor(
                            out=s_buf[:, u % 2, g * keys:(g + 1) * keys],
                            in0=table(f"dist{g}")[:, c0:c0 + keys], scalar=-slope / scale,
                            in1=ps_a[g // 2][:, (g % 2) * keys:(g % 2) * keys + keys], op0=ALU.mult, op1=ALU.add)
                    last.then_inc(sc_read, 1)
                    dve.drain()
                    m = small[:, u % 2:u % 2 + 1]
                    dve.tensor_reduce(m, s_buf[:, u % 2, 0:3 * keys], AX.X, ALU.max)
                    dve.drain()
                    dve.tensor_scalar(small[:, 8 + u % 2:9 + u % 2], m, -scale, None, ALU.mult).then_inc(s_max, 1)
                for u in which(lambda u: at_unit(u) + LEAD + 2, 8, n):
                    dve.wait_ge(p_exp, u + 1)
                    dve.reciprocal(small[:, 24 + u % 2:25 + u % 2], small[:, 16 + u % 2:17 + u % 2]).then_inc(recip_ready, 1)
                for h in which(lambda h: at_stick(h) + LEAD, HEADS_B, n):
                    dve.wait_ge(zb_ready, h + 1)
                    dve.scalar_tensor_tensor(out=z_b[:, :], in0=ps_a[0][:, 0:BLK], scalar=scale,
                                             in1=table("penb"), op0=ALU.mult, op1=ALU.add)
                    dve.drain()
                    dve.scalar_tensor_tensor(out=t_b[:, :], in0=z_b[:, :], scalar=-1.0, in1=z_b[:, :],
                                             op0=ALU.mult, op1=ALU.max).then_inc(zb_abs, 1)
                for h in which(lambda h: at_stick(h) + LEAD + 2, HEADS_B, n):
                    dve.wait_ge(zb_log, h + 1)
                    dve.scalar_tensor_tensor(out=sp_b[:, :], in0=z_b[:, :], scalar=0.0, in1=l_b[:, :],
                                             op0=ALU.max, op1=ALU.add).then_inc(sp_ready, 1)
                for h in which(lambda h: at_stick(h) + LEAD + 3, HEADS_B, n):
                    dve.wait_ge(cum_ready, h + 1)
                    dve.tensor_tensor(lw_b[:, :], z_b[:, :], ps_t[0][:, 0:BLK], ALU.subtract).then_inc(lw_ready, 1)

            MAG, ZR, ZI, NZR, NZI, POW = 1, 5, 6, 7, 8, 14

            def discretize(part):
                DT_, TH, CO, SI, A0, A1, A2, A3 = 0, 2, 3, 4, 9, 10, 11, 12
                v = lambda i: ssm[:, i, :]
                are, aim, ldt = (par[:, PAR[n][0]:PAR[n][0] + STATE_TILES]
                                 for n in ("ssm_a_re_2", "ssm_a_im_2", "ssm_log_dt_2"))

                def ts(o, x, s1, s2, op0, op1=None):
                    dve.tensor_scalar(o, x, s1, s2, op0, op1) if op1 is not None else dve.tensor_scalar(o, x, s1, None, op0)
                    dve.drain()

                def tt(o, x, y, op):
                    dve.tensor_tensor(o, x, y, op)
                    dve.drain()

                def stt(o, x, s, y, op0, op1):
                    dve.scalar_tensor_tensor(out=o, in0=x, scalar=s, in1=y, op0=op0, op1=op1)
                    dve.drain()

                def exp(o, x):
                    r, n, p = v(A0), v(A1), v(A2)
                    ts(r, x, -88.0, 88.0, ALU.max, ALU.min)
                    ts(ssm_i[:, :], r, 1.0 / math.log(2.0), None, ALU.mult)
                    dve.tensor_copy(n, ssm_i[:, :])
                    dve.drain()
                    stt(r, n, -0.693359375, r, ALU.mult, ALU.add)
                    stt(r, n, 2.12194440e-4, r, ALU.mult, ALU.add)
                    ts(p, r, 1.0 / 5040, None, ALU.mult)
                    for k in (720, 120, 24, 6, 2, 1):
                        stt(p, p, 1.0 / k, r, ALU.add, ALU.mult)
                    ts(p, p, 1.0, None, ALU.add)
                    ts(ssm_i[:, :], n, 127.0, float(1 << 23), ALU.add, ALU.mult)
                    tt(o, p, ssm_i[:, :].bitcast(F32), ALU.mult)

                if part == 0:
                    exp(v(DT_), ldt)
                    tt(v(A3), are, v(DT_), ALU.mult)
                    exp(v(MAG), v(A3))
                    tt(v(TH), aim, v(DT_), ALU.mult)
                if part == 1:
                    ts(ssm_i[:, :], v(TH), 1.0 / (2 * math.pi), None, ALU.mult)
                    dve.tensor_copy(v(A0), ssm_i[:, :])
                    dve.drain()
                    for part in (6.28125, 1.9350051879882812e-3, 3.019916050e-7):
                        stt(v(TH), v(A0), -part, v(TH), ALU.mult, ALU.add)
                    ts(v(TH), v(TH), 0.5, None, ALU.mult)
                    tt(v(A0), v(TH), v(TH), ALU.mult)
                    for o, first in ((A1, 2), (A2, 1)):
                        top = 13 if first == 2 else 14
                        sign = lambda n: -1.0 if (n // 2) % 2 else 1.0
                        ts(v(o), v(A0), sign(top) / math.factorial(top), None, ALU.mult)
                        for n in range(top - 2, first - 1, -2):
                            if n >= 2:
                                stt(v(o), v(o), sign(n) / math.factorial(n), v(A0), ALU.add, ALU.mult)
                        if first == 2:
                            stt(v(o), v(o), 1.0, v(TH), ALU.add, ALU.mult)
                        else:
                            ts(v(o), v(o), 1.0, None, ALU.add)
                    stt(v(SI), v(A1), 2.0, v(A2), ALU.mult, ALU.mult)
                    tt(v(A3), v(A1), v(A1), ALU.mult)
                    ts(v(CO), v(A3), -2.0, 1.0, ALU.mult, ALU.add)
                if part == 2:
                    dve.tensor_copy(v(POW), v(CO))
                    dve.tensor_copy(v(POW + 1), v(SI))
                    dve.drain()
                    for k in range(7):
                        c, s = v(POW + 2 * k), v(POW + 2 * k + 1)
                        tt(v(A0), c, c, ALU.mult)
                        tt(v(A1), s, s, ALU.mult)
                        tt(v(POW + 2 * k + 2), v(A0), v(A1), ALU.subtract)
                        stt(v(POW + 2 * k + 3), c, 2.0, s, ALU.mult, ALU.mult)
                if part == 3:
                    tt(v(A0), v(MAG), v(CO), ALU.mult)
                    ts(v(A0), v(A0), -1.0, None, ALU.add)
                    tt(v(A1), v(MAG), v(SI), ALU.mult)
                    tt(v(A2), are, are, ALU.mult)
                    tt(v(A3), aim, aim, ALU.mult)
                    tt(v(A2), v(A2), v(A3), ALU.add)
                    dve.reciprocal(v(A2), v(A2))
                    dve.drain()
                    tt(v(ZR), v(A0), are, ALU.mult)
                    tt(v(A3), v(A1), aim, ALU.mult)
                    tt(v(ZR), v(ZR), v(A3), ALU.add)
                    tt(v(ZR), v(ZR), v(A2), ALU.mult)
                    tt(v(ZI), v(A1), are, ALU.mult)
                    tt(v(A3), v(A0), aim, ALU.mult)
                    tt(v(ZI), v(ZI), v(A3), ALU.subtract)
                    tt(v(ZI), v(ZI), v(A2), ALU.mult)
                    ts(v(NZR), v(ZR), -1.0, None, ALU.mult)
                    ts(v(NZI), v(ZI), -1.0, None, ALU.mult)

            def turn_tables(half):
                if half == 0:
                    dve.memset(turns[:, 0, :, :, 0:1], 1.0)
                    dve.memset(turns[:, 1, :, :, 0:1], 0.0)
                    dve.drain()
                for e in (2 * half, 2 * half + 1):
                    d = 1 << e
                    pc, ps = (ssm[:, POW + 2 * e + i:POW + 2 * e + i + 9:8, :].unsqueeze(3)
                              .to_broadcast([P, 2, STATE_TILES, d]) for i in range(2))
                    c, s = turns[:, 0, :, :, 0:d], turns[:, 1, :, :, 0:d]
                    t = [pr[:, i, 0:32 * d].rearrange("p (a n t) -> p a n t", a=2, t=d) for i in range(4)]
                    dve.tensor_tensor(t[0], c, pc, ALU.mult)
                    dve.tensor_tensor(t[1], s, ps, ALU.mult)
                    dve.tensor_tensor(t[2], c, ps, ALU.mult)
                    dve.tensor_tensor(t[3], s, pc, ALU.mult)
                    dve.drain()
                    dve.tensor_tensor(turns[:, 0, :, :, d:2 * d], t[0], t[1], ALU.subtract)
                    last = dve.tensor_tensor(turns[:, 1, :, :, d:2 * d], t[2], t[3], ALU.add)
                    if e < 3:
                        dve.drain()
                if half:
                    last.then_inc(turns_ready, 1)

            def mixer_2(n):
                if n == 0:
                    last_ple()
                    dve.drain()
                round_off_beside(4)(n)
                if n in (8, 9):
                    turn_tables(n - 8)
                for step in range(3):
                    for m in which(lambda m: at_state(m) + LEAD + step, STATE_TILES, n):
                        state_tile(m, step)
                for b in which(lambda b: at_state(STATE_BLOCK * b + 3) + LEAD + 4, 4, n):
                    dve.wait_ge(x_used, STATE_BLOCK * b + 4)
                    u = proj2[:, U2 + b, :]
                    dve.scalar_tensor_tensor(out=u, in0=u, scalar=param("ssm_d_2", b), in1=ps_o[:, 0:TOK],
                                             op0=ALU.mult, op1=ALU.add).then_inc(y_kept, 1)
                if n == at_head(0):
                    dve.memset(kpad[:, :, :, :], 0.0)
                    dve.memset(vpad[:, :, :, :, :], 0.0)
                    dve.wait_ge(v_turned, 9)
                    dve.tensor_copy(vtok, ps_t[0][:, 0:TOK].rearrange("p (k c) -> p k c", k=2))
                    dve.drain()
                    for j in range(KV_2):
                        for half in range(2):
                            r, s = slice(HD_2 * half, HD_2 * half + HD_2), slice(HD_2 * j, HD_2 * j + HD_2)
                            dve.tensor_copy(kpad[r, j, half, :], proj2[s, K2, :])
                            last = dve.tensor_copy(vpad[:, j, half, :, r], vtok[:, :, s])
                    last.then_inc(pad_ready, 1)
                for h in which(lambda h: at_head(h) + LEAD, HEADS_2, n):
                    o = 16 * (h % 2)
                    slope = 2.0 ** (-8.0 * (h + 1) / HEADS_2)
                    b = s2_buf[:, h % 2, :]
                    dve.wait_ge(sc_ready, 8 + h + 1)
                    if h >= 2:
                        dve.wait_ge(p_turned, 8 + h - 1)
                    dve.scalar_tensor_tensor(out=b, in0=table("distw"), scalar=-slope * HD_2 ** 0.5, in1=ps_t[0][:, 0:BLK],
                                             op0=ALU.mult, op1=ALU.add).then_inc(sc_read, 1)
                    dve.drain()
                    dve.tensor_reduce(small2[:, o + 6:o + 7], b[:, 0:P], AX.X, ALU.max)
                    dve.tensor_reduce(small2[:, o + 7:o + 8], b[:, P:BLK], AX.X, ALU.max)
                    dve.drain()
                    dve.tensor_scalar(small2[:, o:o + 2], small2[:, o + 6:o + 8], sinks[:, h:h + 1], -HD_2 ** -0.5,
                                      ALU.max, ALU.mult).then_inc(s_max, 1)
                for h in which(lambda h: at_head(h) + LEAD + 2, HEADS_2, n):
                    o = 16 * (h % 2)
                    dve.wait_ge(p_exp, 8 + h + 1)
                    dve.tensor_tensor(small2[:, o + 8:o + 10], small2[:, o + 2:o + 4], small2[:, o + 4:o + 6], ALU.add)
                    dve.drain()
                    dve.reciprocal(small2[:, o + 10:o + 12], small2[:, o + 8:o + 10]).then_inc(recip_ready, 1)

            def state_tile(n, step):
                c, s = rot[:, n % 2, 0, :], rot[:, n % 2, 1, :]
                if step == 0:
                    dve.drain()
                    dve.wait_ge(rot_ready, n + 1)
                    dve.wait_ge(v_ready, n + 1)
                    re, im = ps_a[n % 2][:, 0:TOK], ps_a[n % 2][:, TOK:2 * TOK]
                    dve.tensor_tensor(pr[:, 0, :], re, c, ALU.mult)
                    dve.tensor_tensor(pr[:, 1, :], im, s, ALU.mult)
                    dve.tensor_tensor(pr[:, 2, :], im, c, ALU.mult)
                    dve.tensor_tensor(pr[:, 3, :], re, s, ALU.mult).then_inc(v_read, 1)
                    dve.drain()
                    dve.tensor_tensor(vrot[:, 0, :], pr[:, 0, :], pr[:, 1, :], ALU.add)
                    dve.tensor_tensor(vrot[:, 1, :], pr[:, 2, :], pr[:, 3, :], ALU.subtract)
                if step == 1:
                    dve.drain()
                    if n:
                        dve.wait_ge(x_im_ready, n)
                    for i in range(2):
                        last = dve.tensor_tensor_scan(scn[:, i, :], ssm[:, MAG, n:n + 1].to_broadcast([P, TOK]),
                                                      vrot[:, i, :], 0.0, ALU.mult, ALU.add)
                    last.then_inc(scans_ready, 1)
                if step == 2:
                    dve.drain()
                    dve.tensor_tensor(pr[:, 0, :], scn[:, 0, :], c, ALU.mult)
                    dve.tensor_tensor(pr[:, 1, :], scn[:, 1, :], s, ALU.mult)
                    dve.drain()
                    if n >= 2:
                        dve.wait_ge(x_used, n - 1)
                    dve.tensor_tensor(xs[:, n % 2, 0, :], pr[:, 0, :], pr[:, 1, :], ALU.subtract).then_inc(x_ready, 1)
            def gated_sum(st, proj, gate0, gate1, open_gate, opened):
                n_pair = len(st.slots) // 2

                def ep(i, s):
                    whole(st, i, s)
                    if s == 0 and isinstance(i, int) and i == 0:
                        dve.wait_ge(open_gate, opened)
                    t = (i * n_pair + s // 2) * 2
                    ps = bank[(st.group0 + s) % 2][:, :].rearrange("p (c t) -> p c t", c=2)
                    g0, g1 = proj[:, bass.ds(gate0 + t, 2), :], proj[:, bass.ds(gate1 + t, 2), :]
                    g = g1 if s % 2 else g0
                    dve.scalar_tensor_tensor(out=g, in0=g, scalar=1.0, in1=ps, op0=ALU.add, op1=ALU.mult
                                             ).then_inc(evacuated["dve"], 1)
                    if s % 2:
                        dve.drain()
                        dve.tensor_tensor(g0, g0, g1, ALU.add)
                        dve.drain()
                        hi, lo = act_hi[:, bass.ds(t, 2), :], act_lo[:, bass.ds(t, 2), :]
                        dve.tensor_scalar(hi, g0, 0.5, None, ALU.mult)
                        dve.drain()
                        last = dve.scalar_tensor_tensor(out=lo, in0=g0, scalar=0.5, in1=hi.bitcast(F32),
                                                        op0=ALU.mult, op1=ALU.subtract)
                        if s % 4 == 3:
                            last.then_inc(split_ready, 1)
                return ep

            def conv(dst, ps, w, b, tile, half_tiles):
                for c in range(2):
                    x, y = ps[:, c * TOK:(c + 1) * TOK], dst[:, c, :]
                    dve.tensor_scalar(y, x, param_at(w, 2 * half_tiles + tile + c), param_at(b, tile + c), ALU.mult, ALU.add)
                for back in (1, 2):
                    dve.drain()
                    for c in range(2):
                        x, y = ps[:, c * TOK:(c + 1) * TOK - back], dst[:, c, back:]
                        last = dve.scalar_tensor_tensor(out=y, in0=x, scalar=param_at(w, (2 - back) * half_tiles + tile + c),
                                                        in1=y, op0=ALU.mult, op1=ALU.add)
                return last

            def scaled_pairs(st, at):
                def ep(i, s):
                    whole(st, i, s)
                    t = ORDER_2[at + s]
                    dve.tensor_tensor(proj2[:, t:t + 2, :], bank[(st.group0 + s) % 2][:, :].rearrange("p (c t) -> p c t", c=2),
                                      over_tokens, ALU.mult).then_inc(evacuated["dve"], 1)
                return ep

            def ffn(st, base, w, b, tiles, value_conv):
                def ep(i, s):
                    whole(st, i, s)
                    ps = bank[(st.group0 + s) % 2]
                    pair = ps[:, :].rearrange("p (c t) -> p c t", c=2)
                    if s == 0 or value_conv:
                        dve.tensor_tensor(pair, pair, over_tokens, ALU.mult)
                        dve.drain()
                    if s == 0:
                        conv(gate_y, ps, w, b, 2 * i, tiles).then_inc(evacuated["dve"], 1)
                        return
                    if value_conv:
                        conv(val_y, ps, w, b, 2 * i + FT, tiles).then_inc(evacuated["dve"], 1)
                        dve.drain()
                        dve.wait_ge(gate_act, base + i + 1)
                        dve.tensor_tensor(val_y[:, :, :], val_y[:, :, :], gate_g[:, :, :], ALU.mult)
                    else:
                        dve.tensor_tensor(val_y[:, :, :], pair, over_tokens, ALU.mult).then_inc(evacuated["dve"], 1)
                        dve.drain()
                        dve.wait_ge(gate_act, base + i + 1)
                        dve.tensor_tensor(val_y[:, :, :], val_y[:, :, :], gate_g[:, :, :], ALU.mult)
                    dve.drain()
                    split(val_y[:, :, :], f_hi[:, bass.ds(2 * i, 2), :], f_lo[:, bass.ds(2 * i, 2), :]).then_inc(f_ready, 1)
                return ep

            def add_to_residual(st):
                def ep(i, s):
                    whole(st, i, s)
                    h = hT[:, bass.ds((i * len(st.slots) + s) * 2, 2), :]
                    dve.tensor_tensor(h, h, bank[(st.group0 + s) % 2][:, :].rearrange("p (c t) -> p c t", c=2),
                                      ALU.add).then_inc(evacuated["dve"], 1)
                return ep

            def ple(i, s):
                n = i * 2 + s
                dve.wait_ge(evacuated["act"], st_gate.evac0 + n + 1)
                h = hT[:, bass.ds(2 * n, 2), :]
                dve.tensor_tensor(sg[:, :, :], sg[:, :, :], eT[:, bass.ds(2 * n, 2), :], ALU.mult)
                dve.drain()
                dve.tensor_tensor(h, h, sg[:, :, :], ALU.add).then_inc(ple_used, 1)

            dve.memset(small_c[:, 0:1], EPS)
            dve.memset(small_c[:, 1:2], 1.0).then_inc(consts, 1)
            dve.wait_ge(par_landed, 16)
            dve.tensor_scalar(sinks[:, :], par[:, PAR["attn_sinks_2"][0]:PAR["attn_sinks_2"][0] + HEADS_2], HD_2 ** 0.5,
                              None, ALU.mult)
            at_b = PAR["b_in_2"][0] + GATE_AT
            dve.tensor_scalar(half_b[:, :], par[:, at_b:at_b + PROJ2 - GATE_AT], 0.5, None, ALU.mult).then_inc(halved, 1)
            round_off(0, 0)
            last = stream(st_in, scaled_to(st_in, proj1), round_off_beside(0))
            last = stream(st_mix, scaled_to(st_mix, proj1, QB // 2), mixer_1, last)
            dve.wait_ge(ob_kept, HEADS_B)
            split(proj1[:, QA:QA + 4, :], y_hi[:, 0:4, :], y_lo[:, 0:4, :]).then_inc(split_ready, 1)
            split(proj1[:, QB:QB + 4, :], y_hi[:, 4:8, :], y_lo[:, 4:8, :]).then_inc(split_ready, 1)
            last = stream(st_rest, scaled_to(st_rest, proj1, QB // 2 + 18), None, last)
            last = stream(st_branch, gated_sum(st_branch, proj1, GATE_A, GATE_B, gates_open, 16), None, last)
            stream(st_out, None, None, last, 0)
            root(1)

            def mixed(c):
                normed(mT, "g_mix_post", c)

            mixed(0)
            mixed(1)
            round_off(2, 0)
            last = stream(st_up, ffn(st_up, 0, "conv_w", "conv_b", 2 * FT, True), round_off_beside(2, mixed))

            def beside_down(n):
                if n == 4:
                    dve.wait_ge(p_landed, 16)
                    dve.drain()
                    split(pT[:, :, :], p_hi[:, :, :], p_lo[:, :, :]).then_inc(split_ready, 1)
                if n in (8, 16, 24, 32):
                    discretize(n // 8 - 1)

            last = stream(st_down, None, beside_down, last)
            stream(st_ple, None, lambda piece: root(3) if piece == 3 else None)

            def fed(c):
                normed(m2T, "g_ffn_post", c)

            fed(0)
            fed(1)
            round_off(3, 0)
            last_ple = stream(st_gate, ple, round_off_beside(3, fed))
            round_off(4, 0)
            last = stream(st_in2, scaled_pairs(st_in2, 0), mixer_2)
            last = stream(st_in2b, scaled_pairs(st_in2b, 20), None, last)
            dve.wait_ge(y_act, 1)
            split(proj2[:, U2:U2 + 4, :], x2_hi[:, 8:12, :], x2_lo[:, 8:12, :]).then_inc(split_ready, 1)
            dve.wait_ge(o_kept, 16)
            for c in range(2):
                split(proj2[:, Q2 + 4 * c:Q2 + 4 * c + 4, :], x2_hi[:, 4 * c:4 * c + 4, :],
                      x2_lo[:, 4 * c:4 * c + 4, :]).then_inc(split_ready, 1)
            stream(st_glu, None, None, last)

            def gate_glu(piece):
                if piece == 2:
                    dve.wait_ge(evacuated["act"], st_glu.evac0 + 4)
                    dve.tensor_tensor(glu_v[:, :, :], glu_v[:, :, :], glu_g[:, :, :], ALU.mult)
                    dve.drain()
                    split(glu_v[:, :, :], x2_hi[:, 12:16, :], x2_lo[:, 12:16, :]).then_inc(split_ready, 1)

            last = stream(st_in2c, scaled_pairs(st_in2c, 21), gate_glu)
            last = stream(st_branch2, gated_sum(st_branch2, proj2, GATE_AT, GATE_SSM, biased_ready, 23), None, last)
            last_out = stream(st_out2, add_to_residual(st_out2), None, last, 0)
            round_off(5, 0)

            def up_beside(piece):
                if piece == 0:
                    last_out()
                    dve.drain()
                round_off_beside(5)(piece)

            last = stream(st_up2, ffn(st_up2, 22, "conv_w_2", "conv_b_2", FT, False), up_beside)
            last = stream(st_down2, add_to_residual(st_down2), None, last)
            last()
            root(6)
            for c in range(4):
                for t in range(4):
                    h = hT[:, 4 * c + t, :]
                    last = dve.scalar_tensor_tensor(out=h, in0=h, scalar=param("final_norm_g_2", 4 * c + t),
                                                    in1=rstd[:, :], op0=ALU.mult, op1=ALU.mult)
                last.then_inc(split_ready, 1)

        @block.gpsimd
        def _(pool):
            def add_squares(n):
                for j in range(8):
                    pool.wait_ge(sq_ready, 8 * n + j + 1)
                    if j == 0:
                        if n:
                            pool.wait_ge(sum_ready, n)
                        pool.tensor_copy(sq_sum(n), sq_slot(n, 0)).then_inc(sq_used, 1)
                    else:
                        pool.wait_ge(sq_used, 8 * n + j)
                        pool.tensor_tensor(sq_sum(n), sq_sum(n), sq_slot(n, j % 2), ALU.add).then_inc(sq_used, 1)

            ZR, ZI, NZI = 5, 6, 8

            def rotations(n):
                c, s = (rot[:, n % 2, i, :].rearrange("p (a b) -> p a b", b=16) for i in range(2))
                cb, sb_ = (turns[:, i, 0, n, :].unsqueeze(1).to_broadcast([P, 16, 16]) for i in range(2))
                ca, sa = (turns[:, i, 1, n, :].unsqueeze(2).to_broadcast([P, 16, 16]) for i in range(2))
                t = [turn_t[:, i, :].rearrange("p (a b) -> p a b", b=16) for i in range(2)]
                pool.drain()
                pool.tensor_tensor(c, ca, cb, ALU.mult)
                pool.tensor_tensor(t[0], sa, sb_, ALU.mult)
                pool.tensor_tensor(s, sa, cb, ALU.mult)
                pool.tensor_tensor(t[1], ca, sb_, ALU.mult)
                col = lambda i: ssm[:, i, n:n + 1]
                bc, z0, z1 = bc_pad[:, n % STATE_RING, :, :], cz[:, n % 2, 0, :], cz[:, n % 2, 1, :]
                y = [cz_t[:, i, :] for i in range(2)]
                pool.wait_ge(bc_landed[n % STATE_RING], 16 * (n // STATE_RING + 1))
                if n >= 2:
                    pool.wait_ge(x_used, n - 1)
                pool.tensor_scalar(z0, bc[:, 2, :], col(ZR), None, ALU.mult)
                pool.tensor_scalar(z1, bc[:, 2, :], col(NZI), None, ALU.mult)
                pool.tensor_scalar(y[0], bc[:, 3, :], col(ZI), None, ALU.mult)
                pool.tensor_scalar(y[1], bc[:, 3, :], col(ZR), None, ALU.mult)
                pool.drain()
                pool.tensor_tensor(c, c, t[0], ALU.subtract)
                pool.tensor_tensor(s, s, t[1], ALU.add)
                pool.tensor_tensor(z0, z0, y[0], ALU.subtract)
                pool.tensor_tensor(z1, z1, y[1], ALU.subtract).then_inc(rot_ready, 1)

            def imaginary(n):
                c, s = rot[:, n % 2, 0, :], rot[:, n % 2, 1, :]
                pool.wait_ge(scans_ready, n + 1)
                pool.drain()
                pool.tensor_tensor(turn_t[:, 0, :], scn[:, 0, :], s, ALU.mult)
                pool.tensor_tensor(turn_t[:, 1, :], scn[:, 1, :], c, ALU.mult)
                pool.drain()
                if n >= 2:
                    pool.wait_ge(x_used, n - 1)
                pool.tensor_tensor(xs[:, n % 2, 1, :], turn_t[:, 0, :], turn_t[:, 1, :], ALU.add).then_inc(x_im_ready, 1)

            def add_normed(n):
                for c in range(4):
                    x = slice(4 * c, 4 * c + 4)
                    pool.wait_ge(normed_ready, 4 * n + c + 1)
                    pool.tensor_tensor(hT[:, x, :], hT[:, x, :], tmp[:, c % 2, :, :], ALU.add).then_inc(resid_ready, 1)

            add_squares(0)
            add_squares(1)
            add_normed(0)
            add_squares(2)
            add_squares(3)
            add_normed(1)
            add_squares(4)
            pool.wait_ge(turns_ready, 1)
            for n in range(STATE_TILES):
                if n >= 2:
                    pool.wait_ge(x_ready, n - 1)
                rotations(n)
                if n:
                    imaginary(n - 1)
            imaginary(STATE_TILES - 1)
            for n in (5, 6):
                add_squares(n)


def tables():
    t = np.zeros((P, TAB_COLS), np.float32)
    q = np.concatenate([np.arange(P)[:, None] + np.zeros((1, P), int), P + np.arange(P)[:, None] + np.zeros((1, TOK), int)], 1)
    k = np.concatenate([np.arange(P), np.arange(TOK)])[None, :]
    d = q - k

    def put(name, v):
        at, n = TAB[name]
        t[:, at:at + n] = v

    for g, dil in enumerate(DILATIONS):
        put(f"dist{g}", np.where((d >= 0) & (d % dil == 0) & (d <= P * dil), d, -NEG))
    put("distw", np.where((d >= 0) & (d < P), d, -NEG))
    key = np.concatenate([np.zeros(TOK, int), np.full(P, P)])[None, :] + np.arange(P)[:, None]
    qry = np.concatenate([np.arange(TOK), P + np.arange(P)])[None, :]
    put("penb", np.where(key < qry, 0, NEG))
    put("tri", np.arange(P)[:, None] >= np.arange(P)[None, :])
    put("ident", np.eye(P))
    put("ones", 1)
    return t


def params(v):
    t = np.zeros((P, PAR_COLS), np.float32)

    def put(name, x, rows=1):
        at, n = PAR[name]
        t[:, at:at + n] = np.asarray(x).reshape(rows * n // rows, P).T

    for name in PAR:
        if name == "attn_sinks_2":
            at, n = PAR[name]
            t[:, at:at + n] = np.asarray(v[name]).reshape(1, n)
        elif name == "ssm_log_dt_2":
            put(name, np.repeat(np.asarray(v[name]).reshape(-1), HD_2))
        else:
            put(name, v[name])
    return t


def padded(v):
    bc = np.zeros((P, STATE_TILES, 4, P), np.float32)
    for i, part in enumerate(("re", "im")):
        vb, vc = np.asarray(v[f"ssm_b_{part}_2"])[0], np.asarray(v[f"ssm_c_{part}_2"])[0]
        for g in range(32):
            ch, st = slice(16 * (g % 8), 16 * (g % 8) + 16), slice(64 * (g % 2), 64 * (g % 2) + 64)
            bc[ch, g // 2, i, st] = vb[g].T
            bc[st, g // 2, 2 + i, ch] = vc[g].T
    return bc


def grouped(w):
    rows, n = w.shape
    return np.ascontiguousarray(w.reshape(rows // P, P, n // GROUP, GROUP).transpose(2, 1, 0, 3)).reshape(
        n // GROUP * P, rows // P * GROUP)


WEIGHTS = ["w_in", "w_branch_a", "w_branch_b", "w_out", "w_up", "w_down", "w_ple_in", "w_ple_gate",
           "w_in_2", "w_glu_2", "w_branch_attn_2", "w_branch_ssm_2", "w_out_2", "w_up_2", "w_down_2"]


def kernel(**inputs):
    import concourse.bacc as bacc
    from concourse.bass_utils import run_bass_kernel_spmd

    def turned(x, tiles):
        return np.ascontiguousarray(np.asarray(x).reshape(TOK, tiles, P).transpose(2, 1, 0))

    arrays = {"xT": turned(inputs["x"], DT), "pT": turned(inputs["p"], 2), "tables": tables(),
              "params": params(inputs), "bc_pad": padded(inputs)}
    for name in WEIGHTS:
        arrays[name] = grouped(np.asarray(inputs[name])[0])
    nc = bacc.Bacc("TRN2", target_bir_lowering=False, num_devices=1)
    a = {k: nc.dram_tensor(f"in_{k}", v.shape, mybir.dt.from_np(v.dtype), kind="ExternalInput").ap()
         for k, v in arrays.items()}
    out = nc.dram_tensor("out_T", (P, DT, TOK), F32, kind="ExternalOutput").ap()
    build(nc, a, out)
    r = run_bass_kernel_spmd(nc, [{f"in_{k}": v for k, v in arrays.items()}], core_ids=[0])
    got = r.results[0]["out_T"]
    return np.ascontiguousarray(got.transpose(2, 1, 0)).reshape(1, TOK, D)
```
